# Optimizing a Trainium2 kernel written in Bass

```python
import math
import jax
import jax.numpy as jnp
from jax import lax
import numpy as np

D_MODEL = 1024
BATCH = 1
SEQ = 1024
DEPTH = 2

N_EVEN = (DEPTH + 1) // 2
N_ODD = DEPTH // 2
N_DIR = 2
EPS = 1e-6
CONV_W = 4

SSD_WIDTH = D_MODEL
SSD_HEADDIM = 64
SSD_HEADS = SSD_WIDTH // SSD_HEADDIM
SSD_GROUPS = 4
SSD_HPG = SSD_HEADS // SSD_GROUPS
SSD_STATE = 128
SSD_XBC = SSD_WIDTH + 2 * SSD_GROUPS * SSD_STATE
SSD_CHUNK = 64

LRU_WIDTH = D_MODEL
LRU_BLOCKS = 16
LRU_BLOCK = LRU_WIDTH // LRU_BLOCKS
LRU_C = 8.0

CONV_CH = SSD_XBC + LRU_WIDTH
EVEN_IN = CONV_CH + SSD_WIDTH + LRU_WIDTH + N_DIR * SSD_HEADS
EVEN_MIX = SSD_WIDTH + LRU_WIDTH

HGRN_WIDTH = D_MODEL
HGRN_HEADDIM = 128
HGRN_HEADS = HGRN_WIDTH // HGRN_HEADDIM
HGRN_CHUNK = 32
HGRN_SCALE = HGRN_HEADDIM ** -0.5
ODD_IN = 5 * HGRN_WIDTH

D_FF = 4 * D_MODEL

kernel_name = 'hybrid_ssd_rglru_hgrn2_encoder'

def rmsnorm(u, g):
    uf = u.astype(jnp.float32)
    uf = uf * lax.rsqrt(jnp.mean(uf * uf, axis=-1, keepdims=True) + EPS)
    return (uf * g.astype(jnp.float32)).astype(u.dtype)

def centred_conv(u, w, b):
    s_ = u.shape[1]
    pad_l = (CONV_W - 1) // 2
    up = jnp.pad(u, ((0, 0), (pad_l, CONV_W - 1 - pad_l), (0, 0)))
    out = b
    for k in range(CONV_W):
        out = out + up[:, k:k + s_] * w[k]
    return out

def dir_stack(u_f, u_b):
    return jnp.stack([u_f, jnp.flip(u_b, axis=1)], axis=0)

def two_dir(u):
    return dir_stack(u, u)

def merge_dir(y):
    return y[0] + jnp.flip(y[1], axis=1)

def linear_scan(a, b):
    def step(h, ab):
        h = ab[0] * h + ab[1]
        return h, h
    h0 = jnp.zeros_like(a[:, :, 0])
    _, h = lax.scan(step, h0, (jnp.moveaxis(a, 2, 0), jnp.moveaxis(b, 2, 0)))
    return jnp.moveaxis(h, 0, 2)

def ssd_chunked(x, dt, a, bm, cm):
    r_, b_, s_ = x.shape[:3]
    n_chunks = s_ // SSD_CHUNK

    def chunks(u):
        u = u.reshape(r_, b_, n_chunks, SSD_CHUNK, *u.shape[3:])
        return jnp.moveaxis(u, 2, 0)

    xdt = (x * dt[..., None]).reshape(r_, b_, s_, SSD_GROUPS, SSD_HPG, SSD_HEADDIM)
    da = (dt * a[:, None, None, :]).reshape(r_, b_, s_, SSD_GROUPS, SSD_HPG)
    mask = jnp.tril(jnp.ones((SSD_CHUNK, SSD_CHUNK), dtype=bool))[:, :, None, None]

    def step(state, inp):
        xc, dac, bc, cc = inp
        cum = jnp.cumsum(dac, axis=2)
        seg = cum[:, :, :, None] - cum[:, :, None, :]
        decay = jnp.exp(jnp.where(mask, seg, -jnp.inf))
        cb = jnp.einsum('rbtgn,rbsgn->rbtsg', cc, bc)
        y_in = jnp.einsum('rbtsg,rbtsge,rbsgep->rbtgep', cb, decay, xc)
        y_st = jnp.einsum('rbtgn,rbgepn->rbtgep', cc, state) * jnp.exp(cum)[..., None]
        last = cum[:, :, -1]
        w_s = jnp.exp(last[:, :, None] - cum)
        state = state * jnp.exp(last)[..., None, None] + jnp.einsum(
            'rbsgn,rbsge,rbsgep->rbgepn', bc, w_s, xc)
        return state, y_in + y_st

    state0 = jnp.zeros((r_, b_, SSD_GROUPS, SSD_HPG, SSD_HEADDIM, SSD_STATE), jnp.float32)
    _, y = lax.scan(step, state0, (chunks(xdt), chunks(da), chunks(bm), chunks(cm)))
    return jnp.moveaxis(y, 0, 2).reshape(r_, b_, s_, SSD_HEADS, SSD_HEADDIM)

def gla_chunked(q, k, v, log_f):
    r_, b_, s_ = q.shape[:3]
    n_chunks = s_ // HGRN_CHUNK

    def chunks(u):
        u = u.reshape(r_, b_, n_chunks, HGRN_CHUNK, *u.shape[3:])
        return jnp.moveaxis(u, 2, 0)

    mask = jnp.tril(jnp.ones((HGRN_CHUNK, HGRN_CHUNK), dtype=bool))

    def step(state, inp):
        qc, kc, vc, gc = inp
        bcum = jnp.cumsum(gc, axis=2)
        q_t = qc * jnp.exp(bcum)
        k_t = kc * jnp.exp(-bcum)
        att = jnp.where(mask, jnp.einsum('rbthk,rbshk->rbhts', q_t, k_t), 0.0)
        y = jnp.einsum('rbhts,rbshv->rbthv', att, vc) + jnp.einsum(
            'rbthk,rbhkv->rbthv', q_t, state)
        last = bcum[:, :, -1]
        state = state * jnp.exp(last)[..., None] + jnp.einsum(
            'rbshk,rbshv->rbhkv', kc * jnp.exp(last[:, :, None] - bcum), vc)
        return state, y

    state0 = jnp.zeros((r_, b_, HGRN_HEADS, HGRN_HEADDIM, HGRN_HEADDIM), jnp.float32)
    _, y = lax.scan(step, state0, (chunks(q), chunks(k), chunks(v), chunks(log_f)))
    return jnp.moveaxis(y, 0, 2).reshape(r_, b_, s_, HGRN_HEADS, HGRN_HEADDIM)

def mamba2_mixer(xbc, z, dt_raw, a_log, dt_bias, d_skip, norm_w):
    f32 = jnp.float32
    b_, s_, _ = xbc.shape
    xbc = xbc.astype(f32)
    xs = xbc[..., :SSD_WIDTH].reshape(b_, s_, SSD_HEADS, SSD_HEADDIM)
    bm = xbc[..., SSD_WIDTH:SSD_WIDTH + SSD_GROUPS * SSD_STATE].reshape(b_, s_, SSD_GROUPS, SSD_STATE)
    cm = xbc[..., SSD_WIDTH + SSD_GROUPS * SSD_STATE:].reshape(b_, s_, SSD_GROUPS, SSD_STATE)
    dt = jax.nn.softplus(dt_raw.astype(f32) + dt_bias.astype(f32))
    dtd = dir_stack(dt[:, :, 0], dt[:, :, 1])
    a = -jnp.exp(a_log.astype(f32))
    y = merge_dir(ssd_chunked(two_dir(xs), dtd, a, two_dir(bm), two_dir(cm)))
    y = (y + d_skip.astype(f32)[:, None] * xs).reshape(b_, s_, SSD_WIDTH)
    u = (y * jax.nn.silu(z.astype(f32))).reshape(b_, s_, SSD_GROUPS, SSD_WIDTH // SSD_GROUPS)
    u = u * lax.rsqrt(jnp.mean(u * u, axis=-1, keepdims=True) + EPS)
    return u.reshape(b_, s_, SSD_WIDTH) * norm_w.astype(f32)

def rglru_mixer(u, gate, w_a, b_a, w_x, b_x, lam):
    f32 = jnp.float32
    b_, s_, _ = u.shape
    ud = two_dir(u.astype(f32))
    ub = ud.reshape(N_DIR, b_, s_, LRU_BLOCKS, LRU_BLOCK)
    r_gate = jax.nn.sigmoid(jnp.einsum('rbsnc,rncd->rbsnd', ub, w_a.astype(f32)).reshape(
        N_DIR, b_, s_, LRU_WIDTH) + b_a.astype(f32)[:, None, None])
    i_gate = jax.nn.sigmoid(jnp.einsum('rbsnc,rncd->rbsnd', ub, w_x.astype(f32)).reshape(
        N_DIR, b_, s_, LRU_WIDTH) + b_x.astype(f32)[:, None, None])
    log_a = -LRU_C * r_gate * jax.nn.softplus(-lam.astype(f32))[:, None, None]
    inp = jnp.sqrt(-jnp.expm1(2.0 * log_a)) * (i_gate * ud)
    h = merge_dir(linear_scan(jnp.exp(log_a), inp))
    return h * jax.nn.gelu(gate.astype(f32))

def hgrn2_mixer(q, f_raw, inp, gate, lb, norm_w):
    f32 = jnp.float32
    b_, s_, _ = q.shape
    f_raw = f_raw.astype(f32)
    lb = lb.astype(f32)
    log_f = jnp.logaddexp(jnp.log(lb), jnp.log1p(-lb) + jax.nn.log_sigmoid(f_raw))
    k = (1.0 - lb) * jax.nn.sigmoid(-f_raw)

    def heads(u):
        return u.reshape(N_DIR, b_, s_, HGRN_HEADS, HGRN_HEADDIM)

    qd = heads(two_dir(q.astype(f32) * HGRN_SCALE))
    kd = heads(dir_stack(k[:, :, 0], k[:, :, 1]))
    gd = heads(dir_stack(log_f[:, :, 0], log_f[:, :, 1]))
    vd = heads(two_dir(inp.astype(f32)))
    o = merge_dir(gla_chunked(qd, kd, vd, gd))
    o = o * lax.rsqrt(jnp.mean(o * o, axis=-1, keepdims=True) + EPS)
    o = o * norm_w.astype(f32).reshape(HGRN_HEADS, HGRN_HEADDIM)
    return o.reshape(b_, s_, HGRN_WIDTH) * jax.nn.silu(gate.astype(f32))

def setup_inputs(seed: int = 0) -> dict:
    key = jax.random.key(seed)
    ks = jax.random.split(key, 24)
    f32 = jnp.float32

    def nrm(k, shape, scale):
        return jax.random.normal(k, shape, f32) * scale

    x = nrm(ks[0], (BATCH, SEQ, D_MODEL), 1.0)
    even_w_in = nrm(ks[1], (N_EVEN, D_MODEL, EVEN_IN), D_MODEL ** -0.5)
    even_conv_w = nrm(ks[2], (N_EVEN, CONV_W, CONV_CH), CONV_W ** -0.5)
    even_conv_b = nrm(ks[3], (N_EVEN, CONV_CH), 0.01)
    ssd_a_log = jnp.log(jax.random.uniform(ks[4], (N_EVEN, N_DIR, SSD_HEADS), f32, 1.0, 16.0))
    dt0 = jnp.exp(jax.random.uniform(ks[5], (N_EVEN, N_DIR, SSD_HEADS), f32,
                                     math.log(1e-3), math.log(1e-1)))
    ssd_dt_bias = dt0 + jnp.log(-jnp.expm1(-dt0))
    ssd_d = 1.0 + nrm(ks[6], (N_EVEN, SSD_HEADS), 0.1)
    ssd_norm_w = 1.0 + nrm(ks[7], (N_EVEN, SSD_WIDTH), 0.1)
    lru_w_a = nrm(ks[8], (N_EVEN, N_DIR, LRU_BLOCKS, LRU_BLOCK, LRU_BLOCK), LRU_BLOCK ** -0.5)
    lru_b_a = nrm(ks[9], (N_EVEN, N_DIR, LRU_WIDTH), 0.01)
    lru_w_x = nrm(ks[10], (N_EVEN, N_DIR, LRU_BLOCKS, LRU_BLOCK, LRU_BLOCK), LRU_BLOCK ** -0.5)
    lru_b_x = nrm(ks[11], (N_EVEN, N_DIR, LRU_WIDTH), 0.01)
    a0 = jax.random.uniform(ks[12], (N_EVEN, N_DIR, LRU_WIDTH), f32, 0.9, 0.999)
    p0 = a0 ** (1.0 / LRU_C)
    lru_lambda = jnp.log(p0) - jnp.log1p(-p0)
    even_w_out = nrm(ks[13], (N_EVEN, EVEN_MIX, D_MODEL), EVEN_MIX ** -0.5)
    odd_w_in = nrm(ks[14], (N_ODD, D_MODEL, ODD_IN), D_MODEL ** -0.5)
    hgrn_lb_logits = nrm(ks[15], (DEPTH, HGRN_WIDTH), 0.1)
    hgrn_norm_w = 1.0 + nrm(ks[16], (N_ODD, HGRN_WIDTH), 0.1)
    odd_w_out = nrm(ks[17], (N_ODD, HGRN_WIDTH, D_MODEL), HGRN_WIDTH ** -0.5)
    norm_mix = 1.0 + nrm(ks[18], (DEPTH, D_MODEL), 0.1)
    norm_mlp = 1.0 + nrm(ks[19], (DEPTH, D_MODEL), 0.1)
    mlp_w1 = nrm(ks[20], (DEPTH, D_MODEL, D_FF), D_MODEL ** -0.5)
    mlp_w2 = nrm(ks[21], (DEPTH, D_FF, D_MODEL), D_FF ** -0.5)
    norm_final = 1.0 + nrm(ks[22], (D_MODEL,), 0.1)
    return {'x': x, 'even_w_in': even_w_in, 'even_conv_w': even_conv_w,
            'even_conv_b': even_conv_b, 'ssd_a_log': ssd_a_log, 'ssd_dt_bias': ssd_dt_bias,
            'ssd_d': ssd_d, 'ssd_norm_w': ssd_norm_w, 'lru_w_a': lru_w_a, 'lru_b_a': lru_b_a,
            'lru_w_x': lru_w_x, 'lru_b_x': lru_b_x, 'lru_lambda': lru_lambda,
            'even_w_out': even_w_out, 'odd_w_in': odd_w_in, 'hgrn_lb_logits': hgrn_lb_logits,
            'hgrn_norm_w': hgrn_norm_w, 'odd_w_out': odd_w_out, 'norm_mix': norm_mix,
            'norm_mlp': norm_mlp, 'mlp_w1': mlp_w1, 'mlp_w2': mlp_w2, 'norm_final': norm_final}

def reference(x, even_w_in, even_conv_w, even_conv_b, ssd_a_log, ssd_dt_bias, ssd_d,
              ssd_norm_w, lru_w_a, lru_b_a, lru_w_x, lru_b_x, lru_lambda, even_w_out,
              odd_w_in, hgrn_lb_logits, hgrn_norm_w, odd_w_out, norm_mix, norm_mlp,
              mlp_w1, mlp_w2, norm_final):
    b_, s_, _ = x.shape
    p_lb = jax.nn.softmax(hgrn_lb_logits.astype(jnp.float32), axis=0)
    lb_all = jnp.cumsum(p_lb, axis=0) - p_lb[0]
    for l in range(DEPTH):
        h = rmsnorm(x, norm_mix[l])
        if l % 2 == 0:
            j = l // 2
            proj = h @ even_w_in[j]
            conv = centred_conv(proj[..., :CONV_CH], even_conv_w[j], even_conv_b[j])
            xbc = jax.nn.silu(conv[..., :SSD_XBC])
            u_lru = conv[..., SSD_XBC:]
            o0 = CONV_CH
            z = proj[..., o0:o0 + SSD_WIDTH]
            g_lru = proj[..., o0 + SSD_WIDTH:o0 + SSD_WIDTH + LRU_WIDTH]
            dt_raw = proj[..., o0 + SSD_WIDTH + LRU_WIDTH:].reshape(b_, s_, N_DIR, SSD_HEADS)
            y_a = mamba2_mixer(xbc, z, dt_raw, ssd_a_log[j], ssd_dt_bias[j], ssd_d[j],
                               ssd_norm_w[j])
            y_b = rglru_mixer(u_lru, g_lru, lru_w_a[j], lru_b_a[j], lru_w_x[j], lru_b_x[j],
                              lru_lambda[j])
            mix = jnp.concatenate([y_a, y_b], axis=-1) @ even_w_out[j]
        else:
            j = l // 2
            proj = h @ odd_w_in[j]
            w_ = HGRN_WIDTH
            q = proj[..., :w_]
            f_raw = proj[..., w_:3 * w_].reshape(b_, s_, N_DIR, w_)
            inp = proj[..., 3 * w_:4 * w_]
            gate = proj[..., 4 * w_:]
            mix = hgrn2_mixer(q, f_raw, inp, gate, lb_all[l], hgrn_norm_w[j]) @ odd_w_out[j]
        x = x + mix.astype(x.dtype)
        h = rmsnorm(x, norm_mlp[l])
        x = x + (jnp.square(jax.nn.relu(h @ mlp_w1[l])) @ mlp_w2[l]).astype(x.dtype)
    return rmsnorm(x, norm_final)


_drawn_inputs = setup_inputs


def setup_inputs(seed=0):
    import zlib

    import numpy as np

    out = dict(_drawn_inputs(seed))
    spreads = {}
    factors = {'lru_b_a': 48.346, 'lru_b_x': 37.118}
    for name, (base, spread) in spreads.items():
        noise = np.random.default_rng([zlib.crc32(name.encode()), seed]).standard_normal(out[name].shape)
        drawn = base * np.exp(spread * noise) if base else spread * noise
        out[name] = jnp.asarray(drawn.astype(out[name].dtype))
    for name, factor in factors.items():
        out[name] = (out[name] * factor).astype(out[name].dtype)
    return out
```

```python
import numpy as np
from contextlib import ExitStack, contextmanager
import concourse.bass as bass
from concourse import mybir

F32 = mybir.dt.float32
U32 = mybir.dt.uint32
F32R = mybir.dt.float32r
ACT = mybir.ActivationFunctionType
ALU = mybir.AluOpType

P = 128
S = 1024
D = 1024
KT = D // P
HALF = 512
NH = S // HALF
EPS = 1e-6
FF = 4 * D


@contextmanager
def phase(nc, tag):
    sems = []
    with ExitStack() as ctx:
        def sb(name, shape, dt=F32):
            return ctx.enter_context(nc.sbuf_tensor(f"{tag}_{name}", shape, dt))

        def sem(name):
            sems.append(nc.alloc_semaphore(f"{tag}_{name}"))
            return sems[-1]

        yield ctx, sb, sem
    nc.clear_and_free_semaphores(sems)
    nc.all_engine_barrier(sem_only=True)


class Gemm:

    def __init__(self, c, sb, sem, psum):
        self.raw = [sb(f"w_raw{s}", [P, KT * P], F32) for s in range(2)]
        self.hi = [sb(f"w_hi{s}", [P, KT, P], F32R) for s in range(2)]
        self.lo = [sb(f"w_lo{s}", [P, KT, P], F32R) for s in range(2)]
        self.psum = psum
        self.zero = c["zero"]
        self.raw_full = [sem(f"w_raw_full{s}") for s in range(2)]
        self.hi_done = sem("w_hi_done")
        self.w_ready = [sem(f"w_ready{s}") for s in range(2)]
        self.tile_done = [sem(f"tile_done{s}") for s in range(2)]
        self.psum_free = [sem(f"psum_free{s}") for s in range(2)]

    def load(self, sp, w, first, pairs, single=False):
        for s in range(2):
            sp.dma_start(self.raw[s][:], w[first + s]).then_inc(self.raw_full[s], 16)
        if pairs > 1:
            with sp.Fori(1, pairs) as i:
                for s in range(2):
                    sp.wait_ge(self.w_ready[s], i)
                    sp.dma_start(self.raw[s][:], w[2 * i + (first + s)]).then_inc(self.raw_full[s], 16)
        if single:
            sp.wait_ge(self.w_ready[0], pairs)
            sp.dma_start(self.raw[0][:], w[first + 2 * pairs]).then_inc(self.raw_full[0], 16)

    def split_slot(self, pool, i, s):
        hi = self.hi[s][:].rearrange("p k n -> p (k n)")
        lo = self.lo[s][:].rearrange("p k n -> p (k n)")
        pool.wait_ge(self.raw_full[s], (i + 1) * 16)
        pool.tensor_tensor(hi, self.raw[s][:], self.zero[:, 0:1].to_broadcast([P, KT * P]), ALU.add).then_inc(self.hi_done, 1)
        pool.wait_ge(self.hi_done, 2 * i + (s + 1))
        pool.tensor_tensor(lo, self.raw[s][:], hi.bitcast(F32), ALU.subtract).then_inc(self.w_ready[s], 1)

    def split(self, pool, pairs, single=False):
        for s in range(2):
            self.split_slot(pool, 0, s)
        if pairs > 1:
            with pool.Fori(1, pairs) as i:
                for s in range(2):
                    pool.wait_ge(self.tile_done[s], i)
                    self.split_slot(pool, i, s)
        if single:
            pool.wait_ge(self.tile_done[0], pairs)
            self.split_slot(pool, pairs, 0)

    def tile(self, pe, i, s, act_hi, act_lo, before_k=None):
        pe.wait_ge(self.w_ready[s], i + 1)
        pe.wait_ge(self.psum_free[s], i + 1)
        for k in range(KT):
            if before_k is not None:
                before_k(k)
            for part, (w, a) in enumerate(((self.hi, act_hi), (self.hi, act_lo), (self.lo, act_hi))):
                for h in range(NH):
                    mm = pe.matmul(self.psum[s][:, h, :], w[s][:, k, :], a[:, k, h * HALF:(h + 1) * HALF],
                                   start=(k == 0 and part == 0), stop=(k == KT - 1 and part == 2))
        mm.then_inc(self.tile_done[s], 1)


def mlp_phase(nc, c, x, w, first, hi, lo, psum, tag):
    with phase(nc, tag) as (ctx, sb, sem):
        g = Gemm(c, sb, sem, psum)
        hid_hi, hid_lo = sb("hid_hi", [P, KT, S], F32R), sb("hid_lo", [P, KT, S], F32R)
        relu, sq = [sb(f"relu{s}", [P, S]) for s in range(2)], sb("sq", [P, S])
        relu_done, sq_done, hi_done, hid_ready, x_done = (sem(n) for n in ("relu", "sq", "hhi", "hid", "x"))
        BL = FF // (KT * P)
        PR = KT // 2
        block = ctx.enter_context(nc.Block())

        @block.sync
        def _(sp):
            g.load(sp, w, first, BL * 2 * PR)

        @block.gpsimd
        def _(pool):
            g.split(pool, BL * 2 * PR)

        @block.tensor
        def _(pe):
            with pe.Fori(0, BL) as b:
                with pe.Fori(0, PR) as i:
                    for s in range(2):
                        g.tile(pe, b * (2 * PR) + i, s, hi, lo)
                with pe.Fori(0, PR) as i:
                    for s in range(2):
                        g.tile(pe, b * (2 * PR) + i + PR, s, hid_hi, hid_lo,
                               (lambda k: pe.wait_ge(hid_ready, b * KT + (k + 2))) if s == 0 else None)

        @block.scalar
        def _(act):
            for s in range(2):
                act.sem_inc(g.psum_free[s], 1)
            act.sem_inc(sq_done, 2)
            with act.Fori(0, BL) as b:
                with act.Fori(0, PR) as i:
                    for s in range(2):
                        act.wait_ge(g.tile_done[s], b * (2 * PR) + i + 1)
                        act.wait_ge(sq_done, b * KT + (2 * i + (s + 1)))
                        act.activation(relu[s][:].rearrange("p (h n) -> p h n", h=NH), psum[s][:], ACT.Relu).then_inc(g.psum_free[s], 1)
                        act.wait_ge(g.psum_free[s], b * (2 * PR) + i + 2)
                        act.wait_ge(hid_ready, b * KT + (2 * i + (s + 1)))
                        act.activation(sq[:], relu[s][:], ACT.Square).then_inc(sq_done, 1)

        @block.vector
        def _(dve):
            dve.sem_inc(hid_ready, 1)
            with dve.Fori(0, BL) as b:
                with dve.Fori(0, PR) as i:
                    for s in range(2):
                        dve.wait_ge(sq_done, b * KT + (2 * i + (s + 3)))
                        dve.tensor_copy(hid_hi[:, 2 * i + s, :], sq[:]).then_inc(hi_done, 1)
                        dve.wait_ge(hi_done, b * KT + (2 * i + (s + 1)))
                        dve.tensor_tensor(hid_lo[:, 2 * i + s, :], sq[:], hid_hi[:, 2 * i + s, :].bitcast(F32),
                                          ALU.subtract).then_inc(hid_ready, 1)
                with dve.Fori(0, PR) as i:
                    for s in range(2):
                        dve.wait_ge(g.tile_done[s], b * (2 * PR) + i + (PR + 1))
                        dve.tensor_tensor(x[:, 2 * i + s, :].rearrange("p (h n) -> p h n", h=NH), psum[s][:],
                                          x[:, 2 * i + s, :].rearrange("p (h n) -> p h n", h=NH), ALU.add).then_inc(g.psum_free[s], 1)


G, N_ST, HEADS, HD = 4, 128, 16, 64
CH = S // P


def half(ap):
    return ap.rearrange("p (h n) -> p h n", h=NH)


def setup_phase(nc, io, c):
    with phase(nc, "su") as (ctx, sb, sem):
        lam = sb("lam", [P, 2, KT])
        loaded, a_done, v_done = sem("loaded"), sem("act"), sem("dve")
        logit = sb("logit", [P, 2, KT])
        alog = sb("alog", [P, 32])
        tmp = [sb(f"tmp{j}", [P, 2 * KT]) for j in range(3)]
        block = ctx.enter_context(nc.Block())
        loads = [(c[n][:], io[n]) for n in ("gains", "conv_w", "conv_b", "dt_bias", "ssd_norm", "hgrn_norm", "ones",
                                            "ident", "m_ui", "m_us", "m_li", "m_ls", "m_f", "m_b", "scan0", "gate_b")]
        loads += [(c["d_skip"][:], io["d_skip"].to_broadcast([P, HEADS])), (alog[:], io["a_log"].to_broadcast([P, 32])),
                  (lam[:], io["lam"]), (logit[:], io["lb_logits"])]
        one = 16 * len(loads)

        @block.sync
        def _(sp):
            for dst, src in loads:
                sp.dma_start(dst, src).then_inc(loaded, 16)
            sp.wait_ge(loaded, one)

        lam2 = lam[:].rearrange("p d k -> p (d k)")
        hs = c["lru_rate"][:].rearrange("p d k -> p (d k)")
        chain = Softplus(lam2, tmp, hs, -1.0)

        @block.scalar
        def _(act):
            act.wait_ge(loaded, one)
            chain.act(act, a_done)
            act.activation(c["a_exp"][:], alog[:], ACT.Exp).then_inc(a_done, 1)
            act.wait_ge(v_done, 1)
            act.activation(c["lb_e"][:], c["lb_d"][:], ACT.Tanh, scale=0.5).then_inc(a_done, 1)

        @block.vector
        def _(dve):
            dve.memset(c["zero"][:], 0.0)
            dve.wait_ge(loaded, one)
            dve.tensor_tensor(c["lb_d"][:], logit[:, 0, :], logit[:, 1, :], ALU.subtract).then_inc(v_done, 1)
            n = chain.dve(dve, a_done, v_done, 2, 1)
            dve.wait_ge(v_done, n)
            dve.tensor_scalar(hs, hs, -4.0, None, ALU.mult).then_inc(v_done, 1)
            dve.wait_ge(v_done, n + 1)
            dve.tensor_scalar(c["lru_rate2"][:].rearrange("p d k -> p (d k)"), hs, 2.0, None, ALU.mult)
            dve.tensor_scalar(c["lru_rate_n"][:].rearrange("p d k -> p (d k)"), hs, -1.0, None, ALU.mult)
            dve.tensor_scalar(c["gate_bh"][:], c["gate_b"][:], 0.5, None, ALU.mult)
            dve.wait_ge(a_done, 4)
            dve.tensor_scalar(c["oml"][:], c["lb_e"][:], 0.25, 0.25, ALU.mult, ALU.add)
            dve.tensor_scalar(c["noml"][:], c["lb_e"][:], -0.25, -0.25, ALU.mult, ALU.add)
            dve.tensor_scalar(c["lnb"][:], c["lb_e"][:], -0.25, 0.75, ALU.mult, ALU.add)
            dve.tensor_scalar(c["hg_gain"][:], c["hgrn_norm"][:], 0.5, None, ALU.mult)


class Softplus:

    def __init__(self, z, tmp, out, sign):
        self.z, self.tmp, self.out, self.sign = z, tmp, out, sign

    def act(self, act, a_done, base=0):
        act.activation(self.tmp[0][:], self.z, ACT.Abs).then_inc(a_done, 1)
        act.wait_ge(a_done, base + 1)
        act.activation(self.tmp[0][:], self.tmp[0][:], ACT.Exp, scale=-1.0).then_inc(a_done, 1)

    def dve(self, dve, a_done, v_done, a_count, n):
        e, s, q = (t[:] for t in self.tmp)
        dve.wait_ge(a_done, a_count)

        def step(ins):
            nonlocal n
            n += 1
            ins.then_inc(v_done, 1)
            dve.wait_ge(v_done, n)

        step(dve.tensor_scalar(s, e, 2.0, None, ALU.add))
        step(dve.reciprocal(s, s))
        step(dve.tensor_tensor(s, e, s, ALU.mult))
        step(dve.tensor_tensor(q, s, s, ALU.mult))
        step(dve.tensor_scalar(e, q, 1.0 / 17, None, ALU.mult))
        for d in (15, 13, 11, 9, 7, 5, 3):
            step(dve.scalar_tensor_tensor(out=e, in0=e, scalar=1.0 / d, in1=q, op0=ALU.add, op1=ALU.mult))
        step(dve.scalar_tensor_tensor(out=e, in0=e, scalar=1.0, in1=s, op0=ALU.add, op1=ALU.mult))
        step(dve.tensor_scalar(s, self.z, self.sign, 0.0, ALU.mult, ALU.max))
        step(dve.scalar_tensor_tensor(out=self.out, in0=e, scalar=2.0, in1=s, op0=ALU.mult, op1=ALU.add))
        return n


PAIRS_LRU, PAIRS_XZ, PAIRS_BC = 8, 8, 4


def lru_phase(nc, io, c, hi, lo, psum):
    with phase(nc, "lr") as (ctx, sb, sem):
        g = Gemm(c, sb, sem, psum[0:2])
        up, u = sb("up", [P, S + 4]), sb("u", [P, S])
        ta, tx, a, a2, th, h = ([sb(f"{n}{d}", [P, S]) for d in range(2)] for n in ("ta", "tx", "a", "a2", "th", "h"))
        gg, yb = sb("gg", [P, S]), sb("yb", [P, S])
        gw = sb("gw", [P, 4, P])
        pads, tap0, taps, gw_full, gate, gate_read = (
            sem(n) for n in ("pads", "tap0", "taps", "gw_full", "gate", "gate_read"))
        decay, q_done, root, step, y_done, y_stored = (
            sem(n) for n in ("decay", "q_done", "root", "step", "y_done", "y_stored"))
        block = ctx.enter_context(nc.Block())
        NP_ = PAIRS_LRU

        @block.sync
        def _(sp):
            w = io["w"]
            for s in range(2):
                sp.dma_start(g.raw[s][:], w[s]).then_inc(g.raw_full[s], 16)
            sp.dma_start(gw[:], io["gate_w"][0]).then_inc(gw_full, 16)
            with sp.Fori(0, NP_ - 1) as i:
                for s in range(2):
                    sp.wait_ge(g.w_ready[s], i + 1)
                    sp.dma_start(g.raw[s][:], w[2 * i + (s + 2)]).then_inc(g.raw_full[s], 16)
                sp.wait_ge(gate, i * 4 + 4)
                sp.dma_start(gw[:], io["gate_w"][i + 1]).then_inc(gw_full, 16)
                sp.wait_ge(y_done, i + 2)
                sp.dma_start(io["yb_d"][i], yb[:]).then_inc(y_stored, 16)
            sp.wait_ge(y_done, NP_ + 1)
            sp.dma_start(io["yb_d"][NP_ - 1], yb[:]).then_inc(y_stored, 16)
            sp.wait_ge(y_stored, 16 * (NP_ + 1))

        @block.gpsimd
        def _(pool):
            g.split(pool, NP_)

        @block.tensor
        def _(pe):
            with pe.Fori(0, NP_) as i:
                g.tile(pe, i, 0, hi, lo)
                g.tile(pe, i, 1, hi, lo)
                pe.wait_ge(gw_full, i * 16 + 16)
                pe.wait_ge(taps, i * 3 + 3)
                for d in range(2):
                    for r in range(2):
                        pe.wait_ge(gate_read, i * 4 + (2 * d + r + 1))
                        for hh in range(NH):
                            mm = pe.matmul(psum[2 + r][:, hh, :], gw[:, 2 * d + r, :],
                                           u[:, hh * HALF:(hh + 1) * HALF], start=True, stop=True)
                        mm.then_inc(gate, 1)

        @block.scalar
        def _(act):
            for s in range(2):
                act.sem_inc(g.psum_free[s], 1)
            act.sem_inc(gate_read, 2)
            act.wait_ge(pads, 2)
            with act.Fori(0, NP_) as i:
                act.wait_ge(g.tile_done[0], i + 1)
                act.wait_ge(y_done, i + 1)
                act.activation(half(up[:, 1:1 + S]), psum[0][:], ACT.Copy).then_inc(g.psum_free[0], 1)
                act.wait_ge(g.psum_free[0], i + 2)
                act.activation(u[:], up[:, 0:S], ACT.Identity, scale=c["conv_w"][:, bass.ds(i, 1), 0],
                               bias=c["conv_b"][:, bass.ds(i, 1)]).then_inc(tap0, 1)
                for d in range(2):
                    for r, out in enumerate((ta, tx)):
                        act.wait_ge(gate, i * 4 + (2 * d + r + 1))
                        act.activation(half(out[d][:]), psum[2 + r][:], ACT.Tanh, scale=0.5,
                                       bias=c["gate_bh"][:, bass.ds(i, 1), 2 * d + r]).then_inc(gate_read, 1)
                    act.wait_ge(gate_read, i * 4 + (2 * d + 4))
                    for out, rate, func in ((a, "lru_rate", ACT.Exp), (a2, "lru_rate2", ACT.Exp),
                                            (th, "lru_rate_n", ACT.Tanh)):
                        r_ = c[rate][:, d, bass.ds(i, 1)]
                        act.activation(out[d][:], ta[d][:], func, scale=r_, bias=r_).then_inc(decay, 1)
                for d in range(2):
                    act.wait_ge(q_done, i * 2 + (d + 1))
                    act.activation(th[d][:], th[d][:], ACT.Sqrt).then_inc(root, 1)
                act.wait_ge(g.tile_done[1], i + 1)
                act.activation(half(gg[:]), psum[1][:], ACT.Gelu_apprx_tanh).then_inc(g.psum_free[1], 1)

        @block.vector
        def _(dve):
            dve.sem_inc(y_done, 1)
            dve.sem_inc(y_stored, 16)
            dve.memset(up[:, 0:1], 0.0).then_inc(pads, 1)
            dve.memset(up[:, S + 1:S + 4], 0.0).then_inc(pads, 1)
            dve.wait_ge(pads, 2)
            with dve.Fori(0, NP_) as i:
                dve.wait_ge(tap0, i + 1)
                for k in range(1, 4):
                    if k > 1:
                        dve.wait_ge(taps, i * 3 + (k - 1))
                    dve.scalar_tensor_tensor(out=u[:], in0=up[:, k:k + S], scalar=c["conv_w"][:, bass.ds(i, 1), k],
                                             in1=u[:], op0=ALU.mult, op1=ALU.add).then_inc(taps, 1)
                dve.wait_ge(taps, i * 3 + 3)
                for d in range(2):
                    dve.wait_ge(decay, i * 6 + (3 * d + 3))
                    dve.scalar_tensor_tensor(out=th[d][:], in0=a2[d][:], scalar=1.0, in1=th[d][:],
                                             op0=ALU.add, op1=ALU.mult).then_inc(q_done, 1)
                    dve.scalar_tensor_tensor(out=tx[d][:], in0=tx[d][:], scalar=1.0, in1=u[:],
                                             op0=ALU.add, op1=ALU.mult).then_inc(step, 1)
                for d in range(2):
                    dve.wait_ge(root, i * 2 + (d + 1))
                    dve.wait_ge(step, i * 7 + (d + 2 if d == 0 else 4))
                    dve.scalar_tensor_tensor(out=tx[d][:], in0=th[d][:], scalar=0.5, in1=tx[d][:],
                                             op0=ALU.mult, op1=ALU.mult).then_inc(step, 1)
                    dve.wait_ge(step, i * 7 + (2 * d + 3))
                    t = slice(None) if d == 0 else slice(None, None, -1)
                    dve.tensor_tensor_scan(h[d][:, t], a[d][:, t], tx[d][:, t], 0.0, ALU.mult, ALU.add)\
                       .then_inc(step, 1)
                dve.wait_ge(step, i * 7 + 6)
                dve.tensor_tensor(h[0][:], h[0][:], h[1][:], ALU.add).then_inc(step, 1)
                dve.wait_ge(step, i * 7 + 7)
                dve.wait_ge(g.psum_free[1], i + 2)
                dve.wait_ge(y_stored, i * 16 + 16)
                dve.tensor_tensor(yb[:], h[0][:], gg[:], ALU.mult).then_inc(y_done, 1)


def conv_phase(nc, io, c, hi, lo, psum, dt_t):
    with phase(nc, "cv") as (ctx, sb, sem):
        g = Gemm(c, sb, sem, psum[0:2])
        up, acc, sc = ([sb(f"{n}{s}", [P, S + 4 if n == "up" else S]) for s in range(2)] for n in ("up", "acc", "sc"))
        tok = sb("tok", [P, S])
        pads, tr, tok_done, tok_stored = (sem(n) for n in ("pads", "tr", "tok_done", "tok_stored"))
        tap0, taps, silu, cm_stored = ([sem(f"{n}{s}") for s in range(2)] for n in ("tap0", "taps", "silu", "cm_stored"))
        block = ctx.enter_context(nc.Block())
        XZ, BC, W0 = PAIRS_XZ, PAIRS_BC, 2 * PAIRS_LRU
        tok3 = tok[:].rearrange("p (c n) -> p c n", c=CH)
        xs_v = io["xs_d"].rearrange("c p (i n) -> i p c n", n=P)
        bt_v = io["bt_d"].rearrange("c p (i n) -> i p c n", n=P)

        @block.sync
        def _(sp):
            w = io["w"]

            def weights(n):
                for s in range(2):
                    sp.wait_ge(g.w_ready[s], n)
                    sp.dma_start(g.raw[s][:], w[2 * n + (s + W0)]).then_inc(g.raw_full[s], 16)

            for s in range(2):
                sp.dma_start(g.raw[s][:], w[s + W0]).then_inc(g.raw_full[s], 16)
            with sp.Fori(0, XZ) as n:
                weights(n + 1)
                sp.wait_ge(g.psum_free[1], n + 2)
                sp.dma_start(io["z_d"][n], sc[1][:]).then_inc(cm_stored[1], 16)
                sp.wait_ge(tok_done, n + 2)
                sp.dma_start(xs_v[n], tok3).then_inc(tok_stored, 16)

            def store_bc(i):
                sp.wait_ge(silu[0], i + (XZ + 2))
                sp.dma_start(io["b_d"][i], sc[0][:]).then_inc(cm_stored[0], 16)
                sp.wait_ge(tok_done, i + (XZ + 2))
                sp.dma_start(bt_v[i], tok3).then_inc(tok_stored, 16)
                sp.wait_ge(silu[1], i + 2)
                sp.dma_start(io["c_d"][i], sc[1][:]).then_inc(cm_stored[1], 16)

            with sp.Fori(0, BC - 1) as i:
                weights(i + (XZ + 1))
                store_bc(i)
            sp.wait_ge(g.w_ready[0], XZ + BC)
            sp.dma_start(g.raw[0][:], w[2 * (XZ + BC) + W0]).then_inc(g.raw_full[0], 16)
            store_bc(BC - 1)
            sp.wait_ge(cm_stored[0], 16 * (BC + 1))
            sp.wait_ge(cm_stored[1], 16 * (XZ + BC + 1))
            sp.wait_ge(tok_stored, 16 * (XZ + BC + 1))

        @block.gpsimd
        def _(pool):
            g.split(pool, XZ + BC, single=True)

        @block.tensor
        def _(pe):
            pe.sem_inc(tr, 1)
            with pe.Fori(0, XZ + BC) as n:
                g.tile(pe, n, 0, hi, lo)
                g.tile(pe, n, 1, hi, lo)
                pe.wait_ge(silu[0], n + 2)
                pe.wait_ge(tok_done, n + 1)
                for cc in range(CH):
                    mm = pe.transpose(psum[2][:, cc // 4, (cc % 4) * P:(cc % 4 + 1) * P],
                                      sc[0][:, cc * P:(cc + 1) * P], c["ident"][:])
                mm.then_inc(tr, 1)
            g.tile(pe, XZ + BC, 0, hi, lo)

        def conv_head(act, s, n, m, idx):
            act.wait_ge(g.tile_done[s], n + 1)
            act.wait_ge(taps[s], m * 3 + 1)
            act.activation(half(up[s][:, 1:1 + S]), psum[s][:], ACT.Copy).then_inc(g.psum_free[s], 1)
            act.wait_ge(g.psum_free[s], n + 2)
            act.wait_ge(silu[s], m + 1)
            act.activation(acc[s][:], up[s][:, 0:S], ACT.Identity, scale=c["conv_w"][:, bass.ds(idx, 1), 0],
                           bias=c["conv_b"][:, bass.ds(idx, 1)]).then_inc(tap0[s], 1)

        def conv_taps(dve, s, m, idx):
            dve.wait_ge(tap0[s], m + 1)
            for k in range(1, 4):
                if k > 1:
                    dve.wait_ge(taps[s], m * 3 + k)
                dve.scalar_tensor_tensor(out=acc[s][:], in0=up[s][:, k:k + S],
                                         scalar=c["conv_w"][:, bass.ds(idx, 1), k], in1=acc[s][:],
                                         op0=ALU.mult, op1=ALU.add).then_inc(taps[s], 1)

        @block.scalar
        def _(act):
            for s in range(2):
                act.sem_inc(g.psum_free[s], 1)
                act.sem_inc(silu[s], 1)
            act.wait_ge(pads, 4)
            with act.Fori(0, XZ) as n:
                conv_head(act, 0, n, n, n + PAIRS_LRU)
                act.wait_ge(taps[0], n * 3 + 4)
                act.wait_ge(tr, n + 1)
                act.activation(sc[0][:], acc[0][:], ACT.Silu).then_inc(silu[0], 1)
                act.wait_ge(g.tile_done[1], n + 1)
                act.wait_ge(cm_stored[1], n * 16 + 16)
                act.activation(half(sc[1][:]), psum[1][:], ACT.Silu).then_inc(g.psum_free[1], 1)
            with act.Fori(0, BC) as i:
                n = i + XZ
                conv_head(act, 0, n, n, 2 * i + (PAIRS_LRU + XZ))
                act.wait_ge(taps[0], n * 3 + 4)
                act.wait_ge(tr, n + 1)
                act.wait_ge(cm_stored[0], i * 16 + 16)
                act.activation(sc[0][:], acc[0][:], ACT.Silu).then_inc(silu[0], 1)
                conv_head(act, 1, n, i, 2 * i + (PAIRS_LRU + XZ + 1))
                act.wait_ge(taps[1], i * 3 + 4)
                act.wait_ge(cm_stored[1], n * 16 + 16)
                act.activation(sc[1][:], acc[1][:], ACT.Silu).then_inc(silu[1], 1)
            act.wait_ge(g.tile_done[0], XZ + BC + 1)
            act.activation(half(dt_t[:]), psum[0][0:2 * HEADS], ACT.Identity, bias=c["dt_bias"][:, 0:1])

        @block.vector
        def _(dve):
            for s in range(2):
                dve.sem_inc(taps[s], 1)
                dve.sem_inc(cm_stored[s], 16)
                dve.memset(up[s][:, 0:1], 0.0).then_inc(pads, 1)
                dve.memset(up[s][:, S + 1:S + 4], 0.0).then_inc(pads, 1)
            dve.sem_inc(tok_done, 1)
            dve.sem_inc(tok_stored, 16)
            dve.wait_ge(pads, 4)

            def by_tokens(n):
                dve.wait_ge(tr, n + 2)
                dve.wait_ge(tok_stored, n * 16 + 16)
                dve.tensor_copy(half(tok[:]), psum[2][:]).then_inc(tok_done, 1)

            with dve.Fori(0, XZ) as n:
                conv_taps(dve, 0, n, n + PAIRS_LRU)
                by_tokens(n)
            with dve.Fori(0, BC) as i:
                conv_taps(dve, 0, i + XZ, 2 * i + (PAIRS_LRU + XZ))
                by_tokens(i + XZ)
                conv_taps(dve, 1, i, 2 * i + (PAIRS_LRU + XZ + 1))


HH = HEADS // 2
CW = HH * HD


def ssd_coef_phase(nc, c, dt_t, co, psum):
    with phase(nc, "cf") as (ctx, sb, sem):
        W = CH * 2 * HEADS
        z, tmp, da = sb("z", [P, W]), [sb(f"tmp{j}", [P, W]) for j in range(3)], co["da"]
        tr, a_done, v_done, sums, exps = sem("tr"), sem("act"), sem("dve"), sem("sums"), sem("exps")
        flat = lambda t: t[:].rearrange("p c h -> p (c h)")
        sp_ = Softplus(z[:], tmp, flat(co["dt"]), 1.0)
        block = ctx.enter_context(nc.Block())

        @block.tensor
        def _(pe):
            for n in range(CH):
                mm = pe.transpose(psum[0][:, 0, n * 32:n * 32 + 32], dt_t[:, n * P:(n + 1) * P], c["ident"][0:32, 0:32])
            mm.then_inc(tr, 1)
            pe.wait_ge(v_done, 1000)
            f, b = da[:, :, 0:HEADS], da[:, :, HEADS:2 * HEADS]
            w = psum[1][:, 0, 0:W].rearrange("p (c h) -> p c h", c=CH)
            e = psum[1][:, 1, 0:W].rearrange("p (c h) -> p c h", c=CH)
            for out, mask, rhs in ((w[:, :, 0:HEADS], "m_ls", f), (w[:, :, HEADS:], "m_us", b),
                                   (e[:, :, 0:HEADS], "m_ui", f), (e[:, :, HEADS:], "m_li", b),
                                   (psum[2][:, 0, 0:W].rearrange("p (c h) -> p c h", c=CH), "ones", da[:])):
                mm = pe.matmul(out, c[mask][:], rhs, start=True, stop=True)
            mm.then_inc(sums, 1)

        @block.scalar
        def _(act):
            act.wait_ge(tr, 1)
            act.activation(z[:], psum[0][:, 0, 0:W], ACT.Copy).then_inc(a_done, 1)
            act.wait_ge(a_done, 1)
            sp_.act(act, a_done, 1)
            act.wait_ge(sums, 1)
            for out, src in (("w", psum[1][:, 0, 0:W]), ("e", psum[1][:, 1, 0:W]), ("tot", psum[2][:, 0, 0:W])):
                act.activation(flat(co[out]), src, ACT.Exp).then_inc(exps, 1)

        @block.vector
        def _(dve):
            n = sp_.dve(dve, a_done, v_done, 3, 0)
            dve.scalar_tensor_tensor(out=da[:], in0=co["dt"][:], scalar=-1.0,
                                     in1=c["a_exp"][:].unsqueeze(1).to_broadcast([P, CH, 2 * HEADS]),
                                     op0=ALU.mult, op1=ALU.mult).then_inc(v_done, 1000 - n)
            dve.wait_ge(exps, 3)
            dve.tensor_tensor(co["cw"][:], co["dt"][:], co["w"][:], ALU.mult)


def ssd_back_states_phase(nc, io, co, hb, psum):
    with phase(nc, "bs") as (ctx, sb, sem):
        bt, xs, xw = ([sb(f"{n}{q}", [P, w]) for q in range(2)] for n, w in (("bt", G * N_ST), ("xs", D), ("xw", D)))
        full = [sem(f"full{q}") for q in range(2)]
        xw_done, s_done, decayed, h_done = sem("xw_done"), sem("s_done"), sem("decayed"), sem("h_done")
        LAST = CH - 1
        block = ctx.enter_context(nc.Block())

        def steps(eng, step):
            for j in range(LAST):
                step(j, j % 2, j // 2)

        @block.sync
        def _(sp):
            def load(cc, q):
                sp.dma_start(bt[q][:], io["bt_d"][cc]).then_inc(full[q], 16)
                sp.dma_start(xs[q][:], io["xs_d"][cc]).then_inc(full[q], 16)

            load(LAST, 0)
            load(LAST - 1, 1)
            for j in range(2, LAST):
                sp.wait_ge(s_done, j - 1)
                load(LAST - j, j % 2)

        @block.gpsimd
        def _(pool):
            def step(j, q, i):
                pool.wait_ge(full[q], i * 32 + 32)
                pool.tensor_tensor(xw[q][:].rearrange("p (h d) -> p h d", h=HEADS),
                                   xs[q][:].rearrange("p (h d) -> p h d", h=HEADS),
                                   co["cw"][:, LAST - j, HEADS:].unsqueeze(2)
                                   .to_broadcast([P, HEADS, HD]), ALU.mult).then_inc(xw_done, 1)

            steps(pool, step)

        @block.tensor
        def _(pe):
            def step(j, q, i):
                pe.wait_ge(xw_done, j + 1)
                pe.wait_ge(h_done, j + 1)
                for gg in range(G):
                    mm = pe.matmul(psum[q][:, gg // 2, (gg % 2) * 256:(gg % 2) * 256 + 256],
                                   bt[q][:, gg * N_ST:(gg + 1) * N_ST], xw[q][:, gg * 256:(gg + 1) * 256],
                                   start=True, stop=True)
                mm.then_inc(s_done, 1)

            steps(pe, step)

        @block.vector
        def _(dve):
            dve.memset(hb[:, LAST, :], 0.0).then_inc(h_done, 2)

            def step(j, q, i):
                cc = LAST - j
                tot = co["tot"][:, cc, HEADS:].unsqueeze(2).to_broadcast([P, HEADS, HD])
                new = hb[:, cc - 1, :]
                dve.wait_ge(h_done, j + 2)
                dve.tensor_tensor(new.rearrange("p (h d) -> p h d", h=HEADS),
                                  hb[:, cc, :].rearrange("p (h d) -> p h d", h=HEADS), tot, ALU.mult)\
                   .then_inc(decayed, 1)
                dve.wait_ge(decayed, j + 1)
                dve.wait_ge(s_done, j + 1)
                dve.tensor_tensor(half(new), psum[q][:], half(new), ALU.add).then_inc(h_done, 1)

            steps(dve, step)


def ssd_phase(nc, io, c, co, hb, u, psum):
    with phase(nc, "sd") as (ctx, sb, sem):
        two = lambda n, shape: [sb(f"{n}{s}", shape) for s in range(2)]
        bc, cc_, z = ([sb(f"{n}{q}", shape) for q in range(4)] for n, shape in
                      (("b", [P, 2, P]), ("c", [P, 2, P]), ("z", [P, 4, P])))
        bt, xs = [sb(f"bt{q}", [P, 2 * N_ST]) for q in range(4)], [sb(f"xs{q}", [P, CW]) for q in range(4)]
        xf, xb, xw, dx, y, y2 = (two(n, [P, CW]) for n in ("xf", "xb", "xw", "dx", "y", "y2"))
        rf, rb, ex, gu, gl = (two(n, [P, HH, P]) for n in ("rf", "rb", "ex", "gu", "gl"))
        cu, cl = two("cu", [P, 2, P]), two("cl", [P, 2, P])
        hf = sb("hf", [P, 2, CW])
        full = [sem(f"full{q}") for q in range(4)]
        (rf_ok, rb_ok, xsc, dx_ok, seg, cbt, exp_ok, cul, gu_ok, gl_ok, back, hf_ok, y_ok, tr, u_ok) = (
            [sem(f"{n}{s}") for s in range(2)] for n in
            ("rf_ok", "rb_ok", "xsc", "dx_ok", "seg", "cbt", "exp_ok", "cul", "gu_ok", "gl_ok", "back", "hf_ok",
             "y_ok", "tr", "u_ok"))
        dstep = sem("dstep")
        block = ctx.enter_context(nc.Block())
        TURNS = CH // 2

        def pipeline(eng, front, third, back_):
            def step(i, m, first=False, last=False):
                if not last:
                    front(i, m + 1) if m < 3 else front(i + 1, 0)
                if not first:
                    third(i, m - 1) if m else third(i - 1, 3)
                back_(i, m)

            front(0, 0)
            for m in range(4):
                step(0, m, first=(m == 0))
            with eng.Fori(1, TURNS - 1) as i:
                for m in range(4):
                    step(i, m)
            for m in range(4):
                step(TURNS - 1, m, last=(m == 3))
            third(TURNS - 1, 3)

        none = lambda i, m: None
        heads = lambda ap: ap.rearrange("p (h d) -> p h d", h=HH)

        def coef(name, d, i, m):
            at = d * HEADS + (m % 2) * HH
            return co[name][:, bass.ds(2 * i + m // 2, 1), at:at + HH].rearrange("p c h -> p (c h)").unsqueeze(2)

        @block.sync
        def _(sp):
            def load(i, m):
                h, c_ = m % 2, 2 * i + m // 2
                t = bass.ds(c_ * P, P)
                for dst, src in ((bc[m][:], io["b_d"][2 * h:2 * h + 2, :, t].rearrange("g p t -> p g t")),
                                 (cc_[m][:], io["c_d"][2 * h:2 * h + 2, :, t].rearrange("g p t -> p g t")),
                                 (xs[m][:], io["xs_d"][c_][:, h * CW:(h + 1) * CW]),
                                 (bt[m][:], io["bt_d"][c_][:, h * 256:(h + 1) * 256]),
                                 (z[m][:], io["z_d"][4 * h:4 * h + 4, :, t].rearrange("k p t -> p k t"))):
                    sp.dma_start(dst, src).then_inc(full[m], 16)

            for m in range(4):
                load(0, m)
            with sp.Fori(1, TURNS) as i:
                for m in range(4):
                    sp.wait_ge(u_ok[m % 2], 2 * i + m // 2)
                    load(i, m)

        @block.gpsimd
        def _(pool):
            def front(i, m):
                h, c_ = m % 2, 2 * i + m // 2
                pool.wait_ge(full[m], i * 80 + 80)
                pool.wait_ge(back[h], c_ + 1)
                pool.tensor_tensor(rb[h][:], c["m_li"][:].unsqueeze(1).to_broadcast([P, HH, P]),
                                   coef("da", 1, i, m).to_broadcast([P, HH, P]), ALU.mult).then_inc(rb_ok[h], 1)
                for dst, name, d in ((xf, "dt", 0), (xb, "dt", 1), (xw, "cw", 0)):
                    pool.tensor_tensor(heads(dst[h][:]), heads(xs[m][:]), coef(name, d, i, m).to_broadcast([P, HH, HD]),
                                       ALU.mult).then_inc(xsc[h], 1)
                pool.wait_ge(y_ok[h], c_ + 1)
                pool.tensor_tensor(heads(dx[h][:]), heads(xs[m][:]), c["d_skip"][:, h * HH:(h + 1) * HH].unsqueeze(2)
                                   .to_broadcast([P, HH, HD]), ALU.mult).then_inc(dx_ok[h], 1)
                pool.wait_ge(exp_ok[h], c_ + 2)
                pool.wait_ge(cul[h], c_ * 2 + 4)
                pool.tensor_tensor(gl[h][:].rearrange("p (g h) t -> p g h t", g=2),
                                   ex[h][:].rearrange("p (g h) t -> p g h t", g=2),
                                   cl[h][:].unsqueeze(2).to_broadcast([P, 2, 4, P]), ALU.mult).then_inc(gl_ok[h], 1)

            pipeline(pool, front, none, none)

        @block.tensor
        def _(pe):
            for s in range(2):
                pe.sem_inc(back[s], 1)
                pe.sem_inc(tr[s], 1)

            def front(i, m):
                h, c_ = m % 2, 2 * i + m // 2
                pe.wait_ge(rf_ok[h], c_ + 1)
                pe.wait_ge(rb_ok[h], c_ + 1)
                pe.wait_ge(exp_ok[1 - h], c_ + (1 + h))
                for gg in range(2):
                    for mask, r, start in (("m_ls", rf, True), ("m_us", rb, False)):
                        mm = pe.matmul(psum[0][:, gg, :], c[mask][:], r[h][:, 4 * gg:4 * gg + 4, :],
                                       start=start, stop=not start)
                mm.then_inc(seg[h], 1)
                pe.wait_ge(full[m], i * 80 + 80)
                pe.wait_ge(cul[1 - h], c_ * 2 + (2 + 2 * h))
                for gg in range(2):
                    mm = pe.matmul(psum[1][:, 0, gg * P:(gg + 1) * P], bc[m][:, gg, :], cc_[m][:, gg, :],
                                   start=True, stop=True)
                mm.then_inc(cbt[h], 1)

            def third(i, m):
                h, c_ = m % 2, 2 * i + m // 2
                pe.wait_ge(y_ok[h], c_ + 2)
                pe.wait_ge(u_ok[1 - h], c_ + (1 + h))
                for j in range(4):
                    mm = pe.transpose(psum[3][:, 1, j * P:(j + 1) * P], y[h][:, j * P:(j + 1) * P], c["ident"][:])
                mm.then_inc(tr[h], 1)

            def back_(i, m):
                h, c_ = m % 2, 2 * i + m // 2
                pe.wait_ge(gu_ok[h], c_ + 1)
                pe.wait_ge(gl_ok[h], c_ + 1)
                pe.wait_ge(xsc[h], c_ * 3 + 3)
                pe.wait_ge(y_ok[1 - h], c_ + (1 + h))
                pe.wait_ge(hf_ok[1 - h], c_ + (1 + h))
                pe.wait_ge(hf_ok[h], c_ + 1)
                for hd in range(HH):
                    o = psum[1][:, 1, hd * HD:(hd + 1) * HD]
                    pe.matmul(o, gu[h][:, hd, :], xf[h][:, hd * HD:(hd + 1) * HD], start=True, stop=False)
                    pe.matmul(o, gl[h][:, hd, :], xb[h][:, hd * HD:(hd + 1) * HD], start=False, stop=True)
                for gg in range(2):
                    q = slice(gg * 256, (gg + 1) * 256)
                    pe.matmul(psum[2][:, 0, q], cc_[m][:, gg, :], hf[:, h, q], start=True, stop=True)
                    pe.matmul(psum[2][:, 1, q], cc_[m][:, gg, :],
                              hb[:, bass.ds(c_, 1), h * CW + gg * 256:h * CW + gg * 256 + 256]
                              .rearrange("p c n -> p (c n)"), start=True, stop=True)
                    mm = pe.matmul(psum[3][:, 0, q], bt[m][:, gg * N_ST:(gg + 1) * N_ST], xw[h][:, q],
                                   start=True, stop=True)
                mm.then_inc(back[h], 1)

            pipeline(pe, front, third, back_)

        @block.scalar
        def _(act):
            for s in range(2):
                act.sem_inc(exp_ok[s], 1)

            def front(i, m):
                h, c_ = m % 2, 2 * i + m // 2
                act.wait_ge(seg[h], c_ + 1)
                act.wait_ge(back[h], c_ + 1)
                act.activation(ex[h][:].rearrange("p (g h) t -> p g (h t)", g=2), psum[0][:], ACT.Exp)\
                   .then_inc(exp_ok[h], 1)

            pipeline(act, front, none, none)

        @block.vector
        def _(dve):
            for s in range(2):
                dve.sem_inc(cul[s], 2)
                dve.sem_inc(y_ok[s], 1)
                dve.sem_inc(u_ok[s], 1)
                dve.memset(hf[:, s, :], 0.0).then_inc(hf_ok[s], 1)

            def front(i, m):
                h, c_ = m % 2, 2 * i + m // 2
                dve.wait_ge(back[h], c_ + 1)
                dve.tensor_tensor(rf[h][:], c["m_ui"][:].unsqueeze(1).to_broadcast([P, HH, P]),
                                  coef("da", 0, i, m).to_broadcast([P, HH, P]), ALU.mult).then_inc(rf_ok[h], 1)

            def products(i, m):
                h, c_ = m % 2, 2 * i + m // 2
                dve.wait_ge(cbt[h], c_ + 1)
                for dst, mask in ((cu, "m_ui"), (cl, "m_li")):
                    dve.tensor_tensor(dst[h][:], psum[1][:, 0, 0:2 * P].rearrange("p (g t) -> p g t", g=2),
                                      c[mask][:].unsqueeze(1).to_broadcast([P, 2, P]), ALU.mult).then_inc(cul[h], 1)
                dve.wait_ge(exp_ok[h], c_ + 2)
                dve.wait_ge(cul[h], c_ * 2 + 4)
                dve.tensor_tensor(gu[h][:].rearrange("p (g h) t -> p g h t", g=2),
                                  ex[h][:].rearrange("p (g h) t -> p g h t", g=2),
                                  cu[h][:].unsqueeze(2).to_broadcast([P, 2, 4, P]), ALU.mult).then_inc(gu_ok[h], 1)

            def third(i, m):
                h, c_ = m % 2, 2 * i + m // 2
                dve.wait_ge(tr[h], c_ + 2)
                dve.tensor_tensor(u[:, 4 * h:4 * h + 4, bass.ds(c_ * P, P)],
                                  psum[3][:, 1, :].rearrange("p (k t) -> p k t", k=4), z[m][:], ALU.mult)\
                   .then_inc(u_ok[h], 1)

            def back_(i, m):
                h, c_, n = m % 2, 2 * i + m // 2, i * 20 + 5 * m
                dve.wait_ge(back[h], c_ + 2)
                dve.wait_ge(tr[h], c_ + 1)
                dve.tensor_tensor(heads(y[h][:]), heads(psum[2][:, 0, :]), coef("e", 0, i, m).to_broadcast([P, HH, HD]),
                                  ALU.mult).then_inc(dstep, 1)
                dve.tensor_tensor(heads(y2[h][:]), heads(psum[2][:, 1, :]), coef("e", 1, i, m)
                                  .to_broadcast([P, HH, HD]), ALU.mult).then_inc(dstep, 1)
                dve.tensor_tensor(heads(hf[:, h, :]), heads(hf[:, h, :]), coef("tot", 0, i, m)
                                  .to_broadcast([P, HH, HD]), ALU.mult).then_inc(dstep, 1)
                dve.wait_ge(dstep, n + 2)
                dve.tensor_tensor(y[h][:], y[h][:], y2[h][:], ALU.add).then_inc(dstep, 1)
                dve.wait_ge(dstep, n + 3)
                dve.tensor_tensor(hf[:, h, :], psum[3][:, 0, :], hf[:, h, :], ALU.add).then_inc(hf_ok[h], 1)
                dve.wait_ge(dstep, n + 4)
                dve.tensor_tensor(y[h][:], psum[1][:, 1, :], y[h][:], ALU.add).then_inc(dstep, 1)
                dve.wait_ge(dx_ok[h], c_ + 1)
                dve.wait_ge(dstep, n + 5)
                dve.tensor_tensor(y[h][:], y[h][:], dx[h][:], ALU.add).then_inc(y_ok[h], 1)

            def front_only(i, m):
                front(i, m)

            def step(i, m, first=False, last=False):
                nxt = (i, m + 1) if m < 3 else (i + 1, 0)
                if not last:
                    front(*nxt)
                if not first:
                    third(i, m - 1) if m else third(i - 1, 3)
                if not last:
                    products(*nxt)
                back_(i, m)

            front(0, 0)
            products(0, 0)
            for m in range(4):
                step(0, m, first=(m == 0))
            with dve.Fori(1, TURNS - 1) as i:
                for m in range(4):
                    step(i, m)
            for m in range(4):
                step(TURNS - 1, m, last=(m == 3))
            third(TURNS - 1, 3)


GH = 8
GC = 64
NCH = S // GC
SCALE = float(P) ** -0.5
MAGIC = float(0x5F3759DF)
I32 = mybir.dt.int32


def rsqrt_steps(dve, done, n, v, r, t, src, inv_n):
    def step(ins):
        nonlocal n
        n = n + 1
        ins.then_inc(done, 1)
        dve.wait_ge(done, n)

    step(dve.tensor_scalar(v, src, inv_n, EPS, ALU.mult, ALU.add))
    step(dve.tensor_scalar(t.bitcast(I32), v.bitcast(I32), 1, None, ALU.arith_shift_right))
    step(dve.tensor_scalar(r.bitcast(I32), t.bitcast(I32), -1.0, MAGIC, ALU.mult, ALU.add))
    for _ in range(4):
        step(dve.tensor_tensor(t, r, r, ALU.mult))
        step(dve.scalar_tensor_tensor(out=t, in0=t, scalar=-0.5, in1=v, op0=ALU.mult, op1=ALU.mult))
        step(dve.scalar_tensor_tensor(out=r, in0=t, scalar=1.5, in1=r, op0=ALU.add, op1=ALU.mult))
    return n


RSQRT_STEPS = 15


def norm_phase(nc, c, src, groups, gain, hi, lo, psum, tag, out=None, store=None):
    per = KT // groups
    with phase(nc, tag) as (ctx, sb, sem):
        sq, h = [sb(f"sq{b}", [P, S]) for b in range(2)], [sb(f"h{b}", [P, S]) for b in range(2)]
        diag = sb("diag", [P, CH, P])
        v, r, t = (sb(n, [P, CH]) for n in ("v", "r", "t"))
        sq_done, sq_used, newton, diag_done, spread, h_done, hi_done, lo_done = (
            sem(n) for n in ("sq_done", "sq_used", "newton", "diag_done", "spread", "h_done", "hi_done", "lo_done"))
        block = ctx.enter_context(nc.Block())

        @block.scalar
        def _(act):
            def split_hi(k):
                act.wait_ge(h_done, k + 1)
                act.activation(hi[:, k, :], h[k % 2][:], ACT.Copy).then_inc(hi_done, 1)

            for k in range(KT):
                if k >= 2:
                    act.wait_ge(sq_used, k - 1)
                act.activation(sq[k % 2][:], src[:, k, :], ACT.Square).then_inc(sq_done, 1)
            if out is None:
                for k in range(KT):
                    split_hi(k)

        @block.tensor
        def _(pe):
            def spread_group(g):
                pe.wait_ge(diag_done, g + 1)
                if g >= 2:
                    pe.wait_ge(h_done, (g - 1) * per)
                for hh in range(NH):
                    mm = pe.matmul(psum[2 + g % 2][:, hh, :], c["ones"][:],
                                   diag[:, 4 * hh:4 * hh + 4, :], start=True, stop=True)
                mm.then_inc(spread, 1)

            for g in range(groups):
                if g >= 2:
                    pe.wait_ge(newton, (g - 2) * RSQRT_STEPS + 1)
                for k in range(g * per, (g + 1) * per):
                    pe.wait_ge(sq_done, k + 1)
                    for n in range(CH):
                        mm = pe.matmul(psum[g % 2][:, 0, n:n + 1], sq[k % 2][:, n * P:(n + 1) * P], c["ones"][:, 0:1],
                                       start=(k == g * per and n == 0), stop=(k == (g + 1) * per - 1),
                                       skip_group_check=True)
                    mm.then_inc(sq_used, 1)
                if g >= 1:
                    spread_group(g - 1)
            spread_group(groups - 1)

        @block.vector
        def _(dve):
            def split_lo(k):
                dve.wait_ge(hi_done, k + 1)
                dve.tensor_tensor(lo[:, k, :], h[k % 2][:], hi[:, k, :].bitcast(F32), ALU.subtract).then_inc(lo_done, 1)

            for g in range(groups):
                dve.wait_ge(sq_used, (g + 1) * per)
                rsqrt_steps(dve, newton, g * RSQRT_STEPS, v[:], r[:], t[:], psum[g % 2][:, 0, 0:CH], 1.0 / (per * P))
                if g >= 1:
                    dve.wait_ge(spread, g)
                dve.tensor_tensor(diag[:], c["ident"][:].unsqueeze(1).to_broadcast([P, CH, P]),
                                  r[:].unsqueeze(2).to_broadcast([P, CH, P]), ALU.mult).then_inc(diag_done, 1)
                dve.wait_ge(spread, g + 1)
                for k in range(g * per, (g + 1) * per):
                    if out is None and k >= 2:
                        dve.wait_ge(lo_done, k - 1)
                    dst = h[k % 2][:] if out is None else out[:, k, :]
                    dve.scalar_tensor_tensor(out=half(dst), in0=half(src[:, k, :]), scalar=gain[:, k:k + 1],
                                             in1=psum[2 + g % 2][:], op0=ALU.mult, op1=ALU.mult).then_inc(h_done, 1)
                    if out is None and k >= 1:
                        split_lo(k - 1)
            if out is None:
                split_lo(KT - 1)

        if store is not None:
            @block.sync
            def _(sp):
                stored = sem("stored")
                for k in range(KT):
                    sp.wait_ge(h_done, k + 1)
                    sp.dma_start(store[:, k, :], out[:, k, :]).then_inc(stored, 16)
                sp.wait_ge(stored, 16 * KT)


def split_phase(nc, src, hi, lo, tag):
    with phase(nc, tag) as (ctx, sb, sem):
        y = [sb(f"y{k}", [P, S]) for k in range(2)]
        full, hi_done, lo_done = [sem(f"full{b}") for b in range(2)], sem("hi_done"), sem("lo_done")
        block = ctx.enter_context(nc.Block())

        @block.sync
        def _(sp):
            for k in range(KT):
                if k >= 2:
                    sp.wait_ge(lo_done, k - 1)
                sp.dma_start(y[k % 2][:], src[k]).then_inc(full[k % 2], 16)

        @block.scalar
        def _(act):
            for k in range(KT):
                act.wait_ge(full[k % 2], 16 * (k // 2 + 1))
                act.activation(hi[:, k, :], y[k % 2][:], ACT.Copy).then_inc(hi_done, 1)

        @block.vector
        def _(dve):
            for k in range(KT):
                dve.wait_ge(hi_done, k + 1)
                dve.tensor_tensor(lo[:, k, :], y[k % 2][:], hi[:, k, :].bitcast(F32), ALU.subtract).then_inc(lo_done, 1)


def out_phase(nc, io, c, x, first, halves, psum, tag):
    with phase(nc, tag) as (ctx, sb, sem):
        g = Gemm(c, sb, sem, psum[0:2])
        PR = KT // 2
        block = ctx.enter_context(nc.Block())

        @block.sync
        def _(sp):
            g.load(sp, io["w"], first, PR * len(halves))

        @block.gpsimd
        def _(pool):
            g.split(pool, PR * len(halves))

        @block.tensor
        def _(pe):
            for b, (hi, lo) in enumerate(halves):
                with pe.Fori(0, PR) as i:
                    for s in range(2):
                        g.tile(pe, i + b * PR, s, hi, lo)

        @block.vector
        def _(dve):
            for s in range(2):
                dve.sem_inc(g.psum_free[s], 1)
            for b in range(len(halves)):
                with dve.Fori(0, PR) as i:
                    for s in range(2):
                        dve.wait_ge(g.tile_done[s], i + (b * PR + 1))
                        dve.tensor_tensor(half2(x, 2 * i + s), psum[s][:], half2(x, 2 * i + s), ALU.add)\
                           .then_inc(g.psum_free[s], 1)


def half2(x, k):
    return x[:, bass.ds(k, 1), :].rearrange("p k (h n) -> p (k h) n", h=NH)


def gla_phase(nc, io, c, first, hi, lo, psum):
    with phase(nc, "gl") as (ctx, sb, sem):
        g = Gemm(c, sb, sem, psum[0:2])
        X, Y = psum[2], psum[3]
        two = lambda n, shape: [sb(f"{n}{d}", shape) for d in ("f", "b")]
        kk, gs, qh, kh = (two(n, [P, S]) for n in ("k", "gs", "qh", "kh"))
        q, v = sb("q", [P, S]), sb("v", [P, S])
        kt, vt = two("kt", [P, CH, P]), sb("vt", [P, CH, P])
        at = two("at", [P, CH, P])
        m = two("m", [P, P, NCH])
        wb = sb("wrep", [P, P, NCH])
        tot, ws, w = two("tot", [P, 2 * NCH]), two("ws", [P, NCH - 1]), two("w", [P, NCH])
        tick = sb("tick", [P, 2])
        y, sqd, gate, o = sb("y", [P, S]), sb("sqd", [P, CH, P]), [sb(f"gate{b}", [P, S]) for b in range(2)], sb("o", [P, S])
        rv, rr, rt = (sb(n, [P, CH]) for n in ("rv", "rr", "rt"))
        (zeroed, th, lg, kdone, fsum, totd, xdone, wsum, wexp, en, kh_ok, ep, qh_ok, qcopy, vcopy, att, at_ok, kv, kv_ok,
         wbc, m_ok, ymm, ycopy, sqok, tr, trcopy, stat, newton, dg, bc, norm, o_ok, o_stored, gth) = (
            sem(n) for n in ("zeroed", "th", "lg", "kdone", "fsum", "totd", "xdone", "wsum", "wexp", "en", "kh_ok", "ep",
                             "qh_ok", "qcopy", "vcopy", "att", "at_ok", "kv", "kv_ok", "wbc", "m_ok", "ymm", "ycopy",
                             "sqok", "tr", "trcopy", "stat", "newton", "dg", "bc", "norm", "o_ok", "o_stored", "gth"))
        block = ctx.enter_context(nc.Block())
        TURNS = GH // 2

        def turns(eng, turn):
            turn(0, 0, 0, True, False, False)
            turn(1, 0, 1, True, True, False)
            with eng.Fori(1, TURNS) as i:
                for b in range(2):
                    turn(2 * i + b, i, b, True, True, True)
            turn(GH, TURNS, 0, False, True, True)
            turn(GH + 1, TURNS, 1, False, False, True)

        def slot(i, b, j):
            return (5 * b + j) % 2, 5 * i + (5 * b + j) // 2

        blocks = lambda ap: ap.rearrange("p (c a t) -> p c a t", a=2, t=32)
        def kv_sets(d, hf_):
            for par in range(2):
                cs = [cc for cc in range(8 * hf_ + par, 8 * hf_ + 8, 2) if cc != (NCH - 1 if d == 0 else 0)]
                yield par, cs

        KV_OPS = 4

        @block.sync
        def _(sp):
            wt = io["w"]
            for s in range(2):
                sp.dma_start(g.raw[s][:], wt[first + s]).then_inc(g.raw_full[s], 16)

            def weights(pair, s):
                sp.wait_ge(g.w_ready[s], pair)
                sp.dma_start(g.raw[s][:], wt[2 * pair + (first + s)]).then_inc(g.raw_full[s], 16)

            def turn(n, i, b, cur, prev, prev2):
                if cur:
                    for p_ in ((1, 2, 3) if b == 0 else (4, 5)):
                        if not (isinstance(i, int) and 5 * i + p_ == 5 * TURNS):
                            for s in range(2):
                                weights(5 * i + p_, s)
                if prev2:
                    sp.wait_ge(o_ok, n - 1)
                    sp.dma_start(io["hg_d"][n - 2], o[:]).then_inc(o_stored, 16)

            turn(0, 0, 0, True, False, False)
            turn(1, 0, 1, True, True, False)
            with sp.Fori(1, TURNS - 1) as i:
                for b in range(2):
                    turn(2 * i + b, i, b, True, True, True)
            for b in range(2):
                turn(GH - 2 + b, TURNS - 1, b, True, True, True)
            turn(GH, TURNS, 0, False, True, True)
            turn(GH + 1, TURNS, 1, False, False, True)
            sp.wait_ge(o_stored, 16 * (GH + 1))

        @block.gpsimd
        def _(pool):
            g.split(pool, 5 * TURNS)

        @block.tensor
        def _(pe):
            def turn(n, i, b, cur, prev, prev2):
                def gemm(j):
                    if cur:
                        s, pair = slot(i, b, j)
                        g.tile(pe, pair, s, hi, lo)

                def kv_half(d, hf_, ps, wait_n):
                    for par, cs in kv_sets(d, hf_):
                        rows = slice(64 * par, 64 * par + 64)
                        for cc in cs:
                            jj = (cc // 2) % 4
                            mm = pe.matmul(ps[:, par, jj * P:(jj + 1) * P], kt[d][rows, cc // 2, :], vt[rows, cc // 2, :],
                                           start=True, stop=True)
                    mm.then_inc(kv, 1)

                def transposes(src, ps):
                    for n_ in range(CH):
                        mm = pe.transpose(ps[:, n_ // 4, (n_ % 4) * P:(n_ % 4 + 1) * P], src[:, n_ * P:(n_ + 1) * P],
                                          c["ident"][:])
                    mm.then_inc(tr, 1)

                gemm(0)
                if prev2:
                    pe.wait_ge(sqok, n - 1)
                    pe.wait_ge(trcopy, (n if prev else GH) * 3)
                    for n_ in range(CH):
                        mm = pe.matmul(X[:, 0, n_:n_ + 1], sqd[:, n_, :], c["ones"][:, 0:1], start=(n_ == 0), stop=True,
                                       skip_group_check=True)
                    mm.then_inc(stat, 1)
                if prev:
                    pe.wait_ge(qh_ok, n * 2)
                    pe.wait_ge(kh_ok, n * 2)
                    pe.wait_ge(trcopy, n * 3)
                    if prev2:
                        pe.wait_ge(newton, (n - 2) * RSQRT_STEPS + 1)
                    for d, ps in enumerate((X, Y)):
                        for n_ in range(CH):
                            t_ = slice(n_ * P, (n_ + 1) * P)
                            mm = pe.matmul(ps[:, n_ // 4, (n_ % 4) * P:(n_ % 4 + 1) * P], kh[d][:, t_], qh[d][:, t_],
                                           start=True, stop=True)
                        mm.then_inc(att, 1)
                gemm(1)
                if prev2:
                    pe.wait_ge(dg, n - 1)
                    if prev:
                        pe.wait_ge(at_ok, n * 2)
                    for hh in range(NH):
                        mm = pe.matmul(X[:, hh, :], c["ones"][:], sqd[:, 4 * hh:4 * hh + 4, :], start=True, stop=True)
                    mm.then_inc(bc, 1)
                if prev:
                    pe.wait_ge(at_ok, n * 2)
                    kv_half(0, 1, Y, 0)
                    if prev2:
                        pe.wait_ge(norm, n - 1)
                    kv_half(0, 0, X, 0)
                gemm(2)
                if prev:
                    pe.wait_ge(kv_ok, (n - 1) * (4 * KV_OPS // 2) + 2)
                    kv_half(1, 1, Y, 0)
                    pe.wait_ge(kv_ok, (n - 1) * (4 * KV_OPS // 2) + 4)
                    kv_half(1, 0, X, 0)
                gemm(3)
                if prev:
                    pe.wait_ge(m_ok, n * 2)
                    pe.wait_ge(at_ok, n * 2)
                    pe.wait_ge(kv_ok, n * (4 * KV_OPS // 2))
                    for n_ in range(CH):
                        o_ = lambda a_, w_: X[:, n_ // 4, (n_ % 4) * P + a_:(n_ % 4) * P + a_ + w_]
                        for d in range(2):
                            pe.matmul(o_(0, P), vt[:, n_, :], at[d][:, n_, :], start=(d == 0), stop=(d == 1), skip_group_check=True)
                        parts = [(d, 2 * n_ + a_) for a_ in range(2) for d in range(2)
                                 if (d, 2 * n_ + a_) not in ((0, 0), (1, NCH - 1))]
                        for d, cc in parts:
                            mm = pe.matmul(o_((cc % 2) * GC, GC), m[d][:, :, cc], qh[d][:, cc * GC:(cc + 1) * GC],
                                           start=False, stop=True, skip_group_check=True)
                    mm.then_inc(ymm, 1)
                if cur:
                    pe.wait_ge(kh_ok, 2 * n + 1)
                    if prev:
                        pe.wait_ge(kv_ok, n * (4 * KV_OPS // 2))
                    transposes(kh[0], Y)
                gemm(4)
                if cur:
                    pe.wait_ge(kh_ok, 2 * n + 2)
                    if prev:
                        pe.wait_ge(ycopy, n)
                    transposes(kh[1], X)
                    pe.wait_ge(vcopy, n + 1)
                    pe.wait_ge(trcopy, 3 * n + 1)
                    transposes(v, Y)

            turns(pe, turn)

        @block.scalar
        def _(act):
            for s in range(2):
                act.sem_inc(g.psum_free[s], 1)
            act.wait_ge(zeroed, 6)

            def turn(n, i, b, cur, prev, prev2):
                if cur:
                    hd = bass.ds(n, 1)
                    for j in range(2):
                        s, pair = slot(i, b, j)
                        act.wait_ge(g.tile_done[s], pair + 1)
                        if prev:
                            act.wait_ge(kh_ok, n * 2)
                        act.activation(half(kk[j][:]), psum[s][:], ACT.Tanh, scale=0.5).then_inc(g.psum_free[s], 1)
                        act.wait_ge(g.psum_free[s], pair + 2)
                    if prev:
                        act.wait_ge(ep, n * 2)
                    act.wait_ge(zeroed, 6)
                    for d in range(2):
                        act.activation(gs[d][:], kk[d][:], ACT.Ln, scale=c["oml"][:, hd], bias=c["lnb"][:, hd])\
                           .then_inc(lg, 1)
                    s, pair = slot(i, b, 2)
                    act.wait_ge(g.tile_done[s], pair + 1)
                    if prev:
                        act.wait_ge(qh_ok, n * 2)
                    act.activation(half(q[:]), psum[s][:], ACT.Copy, scale=SCALE).then_inc(g.psum_free[s], 1)
                if prev:
                    if prev2:
                        act.wait_ge(m_ok, (n - 1) * 2)
                    act.activation(wb[:], w[0][:].unsqueeze(1).to_broadcast([P, P, NCH]), ACT.Copy).then_inc(wbc, 1)
                if cur:
                    for d in range(2):
                        act.wait_ge(xdone, 2 * n + d + 1)
                        if prev:
                            act.wait_ge(att, n * 2)
                        act.activation(kh[d][:], gs[d][:], ACT.Exp, scale=-1.0).then_inc(en, 1)
                if prev:
                    act.wait_ge(m_ok, n * 2 - 1)
                    act.activation(wb[:], w[1][:].unsqueeze(1).to_broadcast([P, P, NCH]), ACT.Copy).then_inc(wbc, 1)
                if cur:
                    s, pair = slot(i, b, 3)
                    act.wait_ge(g.tile_done[s], pair + 1)
                    if prev:
                        act.wait_ge(tr, n * 3)
                    act.activation(half(v[:]), psum[s][:], ACT.Copy).then_inc(g.psum_free[s], 1)
                    act.wait_ge(g.psum_free[s], pair + 2)
                    act.activation(v[0:1, 0:1], v[0:1, 0:1], ACT.Copy).then_inc(vcopy, 1)
                    if prev:
                        act.wait_ge(wbc, n * 2)
                        act.wait_ge(kv_ok, n * (4 * KV_OPS // 2))
                    for d in range(2):
                        act.wait_ge(wsum, 2 * n + d + 1)
                        act.activation(w[d][:, 1 - d:NCH - d], ws[d][:], ACT.Exp).then_inc(wexp, 1)
                if prev:
                    act.wait_ge(ymm, n)
                    if prev2:
                        act.wait_ge(norm, (n - 1) * 1)
                        act.wait_ge(o_ok, n - 1)
                    act.activation(half(y[:]), X[:], ACT.Copy).then_inc(ycopy, 1)
                    act.wait_ge(ycopy, n)
                    if prev2:
                        act.wait_ge(bc, n - 1)
                    act.activation(sqd[:].rearrange("p c t -> p (c t)"), y[:], ACT.Square).then_inc(sqok, 1)
                if cur:
                    act.wait_ge(tr, 3 * n + 1)
                    act.activation(kt[0][:].rearrange("p (h c) t -> p h (c t)", h=NH), Y[:], ACT.Copy).then_inc(trcopy, 1)
                    for d in range(2):
                        act.activation(qh[d][:], gs[d][:], ACT.Exp).then_inc(ep, 1)
                    s, pair = slot(i, b, 4)
                    act.wait_ge(g.tile_done[s], pair + 1)
                    if prev2:
                        act.wait_ge(o_ok, n - 1)
                    act.activation(half(gate[b][:]), psum[s][:], ACT.Tanh, scale=0.5).then_inc(gth, 1)
                    for dst, k_, ps in ((kt[1], 2, X), (vt, 3, Y)):
                        act.wait_ge(tr, 3 * n + k_)
                        act.activation(dst[:].rearrange("p (h c) t -> p h (c t)", h=NH), ps[:], ACT.Copy)\
                           .then_inc(trcopy, 1)

            turns(act, turn)

        @block.vector
        def _(dve):
            dve.sem_inc(o_stored, 16)
            for d in range(2):
                dve.memset(at[d][:], 0.0).then_inc(zeroed, 1)
                dve.memset(w[d][:, d * (NCH - 1):d * (NCH - 1) + 1], 0.0).then_inc(zeroed, 1)
                dve.memset(m[d][:, :, d * (NCH - 1):d * (NCH - 1) + 1], 0.0).then_inc(zeroed, 1)
            dve.wait_ge(zeroed, 6)

            def turn(n, i, b, cur, prev, prev2):
                if prev2:
                    dve.wait_ge(stat, n - 1)
                    rsqrt_steps(dve, newton, (n - 2) * RSQRT_STEPS, rv[:], rr[:], rt[:], X[:, 0, 0:CH], 1.0 / P)
                    dve.tensor_tensor(sqd[:], c["ident"][:].unsqueeze(1).to_broadcast([P, CH, P]),
                                      rr[:].unsqueeze(2).to_broadcast([P, CH, P]), ALU.mult).then_inc(dg, 1)
                if prev:
                    for d, (ps, mask) in enumerate(((X, "m_f"), (Y, "m_b"))):
                        dve.wait_ge(att, n * 2 - 1 + d)
                        if prev2:
                            dve.wait_ge(ymm, n - 1)
                        dve.memset(tick[:, d:d + 1], 0.0)
                        dve.copy_predicated(at[d][:], c[mask][:].unsqueeze(1).to_broadcast([P, CH, P]),
                                            ps[:].rearrange("p h (c t) -> p (h c) t", t=P)).then_inc(at_ok, 1)
                if prev2:
                    dve.wait_ge(bc, n - 1)
                    dve.scalar_tensor_tensor(out=half(y[:]), in0=half(y[:]), scalar=c["hg_gain"][:, bass.ds(n - 2, 1)],
                                             in1=X[:], op0=ALU.mult, op1=ALU.mult).then_inc(norm, 1)
                    dve.wait_ge(norm, n - 1)
                    dve.wait_ge(o_stored, (n - 1) * 16)
                    dve.tensor_tensor(o[:], y[:], gate[b][:], ALU.mult).then_inc(o_ok, 1)

                def kv_read(d, hf_, ps, k_):
                    dve.wait_ge(kv, (n - 1) * 4 + k_)
                    for par, cs in kv_sets(d, hf_):
                        a_, st = cs[0] + (1 if d == 0 else -1), len(cs)
                        sl = slice(a_, a_ + 2 * st - 1, 2)
                        j0 = (cs[0] // 2) % 4
                        dve.tensor_tensor(m[d][:, :, sl].rearrange("p v c -> p c v"),
                                          ps[:, par, j0 * P:(j0 + st) * P].rearrange("p (c v) -> p c v", v=P),
                                          w[d][:, sl].unsqueeze(2).to_broadcast([P, st, P]), ALU.mult).then_inc(kv_ok, 1)

                if prev:
                    dve.wait_ge(wexp, n * 2)
                    if prev2:
                        dve.wait_ge(ymm, n - 1)
                    kv_read(0, 1, Y, 1)
                    kv_read(0, 0, X, 2)

                if cur:
                    hd = bass.ds(n, 1)
                    for d in range(2):
                        dve.wait_ge(lg, 2 * n + d + 1)
                        dve.tensor_scalar(kk[d][:], kk[d][:], c["noml"][:, hd], c["oml"][:, hd], ALU.mult, ALU.add)\
                           .then_inc(kdone, 1)
                        t_ = slice(None) if d == 0 else slice(None, None, -1)
                        dve.tensor_tensor_scan(gs[d][:, t_], c["scan0"][:], gs[d][:, t_], 0.0, ALU.mult, ALU.add)\
                           .then_inc(fsum, 1)
                    for d in range(2):
                        dve.wait_ge(fsum, 2 * n + d + 1)
                        if prev:
                            dve.wait_ge(wsum, n * 2)
                        dve.tensor_copy(tot[d][:], gs[d][:, 31 if d == 0 else 0::32]).then_inc(totd, 1)
                    for d in range(2):
                        dve.wait_ge(totd, 2 * n + d + 1)
                        a_ = d
                        xv = blocks(gs[d][:])[:, :, a_, :]
                        dve.tensor_tensor(xv, xv, tot[d][:, a_::2].unsqueeze(2).to_broadcast([P, NCH, 32]), ALU.subtract)\
                           .then_inc(xdone, 1)
                        if prev:
                            dve.wait_ge(wexp, n * 2)
                        dve.tensor_tensor(ws[d][:], tot[d][:, 1:2 * NCH - 2:2], tot[d][:, 2::2], ALU.add).then_inc(wsum, 1)
                if prev:
                    dve.wait_ge(wbc, n * 2 - 1)
                    dve.wait_ge(kv_ok, (n - 1) * 8 + 4)
                    fl = lambda ap: ap.rearrange("p v c -> p (v c)")
                    dve.tensor_tensor_scan(fl(m[0][:]), fl(wb[:]), fl(m[0][:]), 0.0, ALU.mult, ALU.add).then_inc(m_ok, 1)
                    kv_read(1, 1, Y, 3)
                    kv_read(1, 0, X, 4)
                    dve.wait_ge(wbc, n * 2)
                    dve.wait_ge(kv_ok, n * 8)
                    dve.tensor_tensor_scan(fl(m[1][:])[:, ::-1], fl(wb[:])[:, ::-1], fl(m[1][:])[:, ::-1], 0.0,
                                           ALU.mult, ALU.add).then_inc(m_ok, 1)
                if cur:
                    for d in range(2):
                        dve.wait_ge(en, 2 * n + d + 1)
                        dve.wait_ge(kdone, 2 * n + d + 1)
                        dve.tensor_tensor(kh[d][:], kh[d][:], kk[d][:], ALU.mult).then_inc(kh_ok, 1)
                    s, pair = slot(i, b, 2)
                    dve.wait_ge(g.psum_free[s], pair + 2)
                    for d in range(2):
                        dve.wait_ge(ep, 2 * n + d + 1)
                        dve.tensor_tensor(qh[d][:], qh[d][:], q[:], ALU.mult).then_inc(qh_ok, 1)
                    s, pair = slot(i, b, 4)
                    dve.wait_ge(gth, n + 1)
                    dve.scalar_tensor_tensor(out=half(gate[b][:]), in0=half(gate[b][:]), scalar=1.0, in1=psum[s][:],
                                             op0=ALU.add, op1=ALU.mult).then_inc(g.psum_free[s], 1)

            turns(dve, turn)

W_EVEN_OUT = 2 * (PAIRS_LRU + PAIRS_XZ + PAIRS_BC) + 1
W_MLP0 = W_EVEN_OUT + 2 * KT
W_ODD_IN = W_MLP0 + 2 * FF // P
W_ODD_OUT = W_ODD_IN + 5 * GH
W_MLP1 = W_ODD_OUT + KT

CONST = dict(
    gains=[P, 5, KT], conv_w=[P, 24, 4], conv_b=[P, 24], gate_b=[P, KT, 4], dt_bias=[2 * HEADS, 1], ssd_norm=[P, KT],
    hgrn_norm=[P, KT], d_skip=[P, HEADS], ones=[P, P], ident=[P, P], m_ui=[P, P], m_us=[P, P], m_li=[P, P], m_ls=[P, P],
    m_f=[P, P], m_b=[P, P], scan0=[P, S],
    a_exp=[P, 2 * HEADS], lb_e=[P, KT], lb_d=[P, KT], lru_rate=[P, 2, KT], lru_rate2=[P, 2, KT], lru_rate_n=[P, 2, KT],
    gate_bh=[P, KT, 4], oml=[P, KT], noml=[P, KT], lnb=[P, KT], hg_gain=[P, KT], zero=[P, 1])

SCRATCH = dict(yb_d=[KT, P, S], hg_d=[KT, P, S], z_d=[KT, P, S], xs_d=[CH, P, D], b_d=[G, P, S], c_d=[G, P, S],
               bt_d=[CH, P, G * N_ST], x_d=[P, KT, S])


def encoder(nc, io):
    with ExitStack() as ctx:
        sb = lambda n, shape, dt=F32: ctx.enter_context(nc.sbuf_tensor(n, shape, dt))
        c = {n: sb(f"c_{n}", shape, U32 if n in ("m_f", "m_b") else F32) for n, shape in CONST.items()}
        psum = [ctx.enter_context(nc.psum_tensor(f"ps{b}", [P, NH, HALF], F32)) for b in range(4)]
        parts = lambda n: (ctx.enter_context(nc.sbuf_tensor(f"{n}_{part}", [P, KT, S], F32R)) for part in ("hi", "lo"))
        io = dict(io, **{n: nc.dram_tensor(n, shape, F32).ap() for n, shape in SCRATCH.items()})
        gain = lambda n: c["gains"][:, n, :]
        setup_phase(nc, io, c)

        u_guard = nc.sbuf_tensor("u", [P, KT, S], F32, side="right")
        with ExitStack() as ssd:
            sb0 = lambda n, shape, dt=F32: ssd.enter_context(nc.sbuf_tensor(n, shape, dt))
            dt_t = sb0("dt_t", [2 * HEADS, S])
            co = {n: sb0(f"co_{n}", [P, CH, 2 * HEADS]) for n in ("dt", "da", "w", "e", "tot", "cw")}
            with nc.sbuf_tensor("h0_hi", [P, KT, S], F32R) as hi, nc.sbuf_tensor("h0_lo", [P, KT, S], F32R) as lo:
                with nc.sbuf_tensor("x_first", [P, KT, S], F32) as x:
                    copy_phase(nc, x, io["xT"], "xa")
                    norm_phase(nc, c, x, 1, gain(0), hi, lo, psum, "na")
                lru_phase(nc, io, c, hi, lo, psum)
                conv_phase(nc, io, c, hi, lo, psum, dt_t)
            ssd_coef_phase(nc, c, dt_t, co, psum)
            with nc.sbuf_tensor("hb", [P, CH, D], F32) as hb:
                u = u_guard.__enter__()
                ssd_back_states_phase(nc, io, co, hb, psum)
                ssd_phase(nc, io, c, co, hb, u, psum)
        hi, lo = parts("h")
        norm_phase(nc, c, u, G, c["ssd_norm"], hi, lo, psum, "nu")
        u_guard.__exit__(None, None, None)
        with nc.sbuf_tensor("x_even", [P, KT, S], F32) as x:
            copy_phase(nc, x, io["xT"], "xb")
            with nc.sbuf_tensor("yb_hi", [P, KT, S], F32R) as yb_hi, nc.sbuf_tensor("yb_lo", [P, KT, S], F32R) as yb_lo:
                split_phase(nc, io["yb_d"], yb_hi, yb_lo, "sb")
                out_phase(nc, io, c, x, W_EVEN_OUT, [(yb_hi, yb_lo), (hi, lo)], psum, "oe")
            norm_phase(nc, c, x, 1, gain(1), hi, lo, psum, "nb")
            mlp_phase(nc, c, x, io["w"], W_MLP0, hi, lo, psum, "me")
            norm_phase(nc, c, x, 1, gain(2), hi, lo, psum, "nc")
            copy_phase(nc, io["x_d"], x, "xc")

        gla_phase(nc, io, c, W_ODD_IN, hi, lo, psum)
        with nc.sbuf_tensor("x_odd", [P, KT, S], F32) as x:
            copy_phase(nc, x, io["x_d"], "xd")
            split_phase(nc, io["hg_d"], hi, lo, "sh")
            out_phase(nc, io, c, x, W_ODD_OUT, [(hi, lo)], psum, "oo")
            norm_phase(nc, c, x, 1, gain(3), hi, lo, psum, "nd")
            mlp_phase(nc, c, x, io["w"], W_MLP1, hi, lo, psum, "mo")
            norm_phase(nc, c, x, 1, gain(4), hi, lo, psum, "ne", out=x, store=io["out"])


def copy_phase(nc, dst, src, tag):
    with phase(nc, tag) as (ctx, sb, sem):
        copied = sem("copied")
        block = ctx.enter_context(nc.Block())

        @block.sync
        def _(sp):
            for k in range(KT):
                sp.dma_start(dst[:, k, :], src[:, k, :]).then_inc(copied, 16)
            sp.wait_ge(copied, 16 * KT)


def tiles(w):
    K, N = w.shape
    return w.reshape(K // 1024, 8, P, N // P, P).transpose(0, 3, 2, 1, 4).reshape(K // 1024, N // P, P, 1024)
def cols(v):
    v = v.reshape(*v.shape[:-1], v.shape[-1] // P, P)
    return np.moveaxis(v, -1, 0)
def mlp(w1, w2):
    a = tiles(w1)[0].reshape(4, 8, P, 1024)
    return np.concatenate([a, tiles(w2)], axis=1).reshape(64, P, 1024)
def layout(x, even_w_in, even_conv_w, even_conv_b, ssd_a_log, ssd_dt_bias, ssd_d,
              ssd_norm_w, lru_w_a, lru_b_a, lru_w_x, lru_b_x, lru_lambda, even_w_out,
              odd_w_in, hgrn_lb_logits, hgrn_norm_w, odd_w_out, norm_mix, norm_mlp,
              mlp_w1, mlp_w2, norm_final):
    f = np.float32
    e = tiles(even_w_in[0][:, :5120])[0]
    x_, b_, c_, u_, z_, g_ = e[0:8], e[8:12], e[12:16], e[16:24], e[24:32], e[32:40]
    pair = lambda a, b: np.stack([a, b], 1).reshape(-1, P, 1024)
    dtw = tiles(np.concatenate([even_w_in[0][:, 5120:], np.zeros((1024, 96), f)], 1))[0]
    eo = tiles(even_w_out[0])
    o = tiles(odd_w_in[0])[0].reshape(5, 8, P, 1024)
    o = o[[1, 2, 0, 3, 4]].transpose(1, 0, 2, 3).reshape(40, P, 1024)
    w = np.concatenate([pair(u_, g_), pair(x_, z_), pair(b_, c_), dtw, eo[1], eo[0], mlp(mlp_w1[0], mlp_w2[0]),
                        o, tiles(odd_w_out[0])[0], mlp(mlp_w1[1], mlp_w2[1])])
    cw = even_conv_w[0].reshape(4, 24, P); cb = even_conv_b[0].reshape(24, P)
    order = list(range(16, 24)) + list(range(8)) + [n for i in range(4) for n in (8 + i, 12 + i)]
    gw = np.zeros((8, P, 2, 2, P), f)
    for r, m in enumerate((lru_w_a[0], lru_w_x[0])):
        for hb in range(2):
            q = slice(64 * hb, 64 * hb + 64)
            gw[:, q, :, r, q] = m[:, hb::2].transpose(1, 2, 0, 3)
    gb = np.stack([lru_b_a[0], lru_b_x[0]], 1).reshape(4, 8, P).transpose(2, 1, 0)
    i = np.arange(P)
    s, t = i[:, None], i[None, :]
    same = s // 64 == t // 64
    A = lambda a: np.ascontiguousarray(a)
    return dict(
        xT=A(x[0].T.reshape(8, P, 1024).transpose(1, 0, 2)), w=A(w), gate_w=A(gw.reshape(8, P, 4 * P)),
        conv_w=A(cw[:, order].transpose(2, 1, 0)), conv_b=A(cb[order].T), gate_b=A(gb),
        gains=A(cols(np.stack([norm_mix[0], norm_mlp[0], norm_mix[1], norm_mlp[1], norm_final]))),
        dt_bias=A(ssd_dt_bias[0].reshape(32, 1)), a_log=A(ssd_a_log[0].reshape(1, 32)), d_skip=A(ssd_d[0].reshape(1, 16)),
        ssd_norm=A(cols(ssd_norm_w[0])), hgrn_norm=A(cols(hgrn_norm_w[0])), lam=A(cols(lru_lambda[0])),
        lb_logits=A(cols(hgrn_lb_logits)),
        ones=np.ones((P, P), f), ident=np.eye(P, dtype=f),
        m_ui=(s <= t).astype(f), m_us=(s < t).astype(f), m_li=(s >= t).astype(f), m_ls=(s > t).astype(f),
        m_f=A((same & (s <= t)).astype(np.uint32)), m_b=A((same & (s >= t)).astype(np.uint32)),
        scan0=A(np.tile((np.arange(1024) % 32 != 0).astype(f), (P, 1))),
    )


def kernel(**inputs):
    import concourse.bacc as bacc
    from concourse.bass_utils import run_bass_kernel_spmd

    arrays = layout(**{name: np.asarray(value) for name, value in inputs.items()})
    nc = bacc.Bacc("TRN2", target_bir_lowering=False, num_devices=1)
    io = {name: nc.dram_tensor(f"in_{name}", a.shape, mybir.dt.from_np(a.dtype), kind="ExternalInput").ap()
          for name, a in arrays.items()}
    io["out"] = nc.dram_tensor("out_y", [P, KT, S], F32, kind="ExternalOutput").ap()
    encoder(nc, io)
    r = run_bass_kernel_spmd(nc, [{f"in_{name}": a for name, a in arrays.items()}], core_ids=[0])
    return np.ascontiguousarray(r.results[0]["out_y"].transpose(2, 1, 0).reshape(1, S, D))
```

```python
import numpy as np
from contextlib import ExitStack, contextmanager
import concourse.bass as bass
from concourse import mybir

F32 = mybir.dt.float32
U32 = mybir.dt.uint32
F32R = mybir.dt.float32r
ACT = mybir.ActivationFunctionType
ALU = mybir.AluOpType

P = 128
S = 1024
D = 1024
KT = D // P
HALF = 512
NH = S // HALF
EPS = 1e-6
FF = 4 * D


@contextmanager
def phase(nc, tag):
    sems = []
    with ExitStack() as ctx:
        def sb(name, shape, dt=F32):
            return ctx.enter_context(nc.sbuf_tensor(f"{tag}_{name}", shape, dt))

        def sem(name):
            sems.append(nc.alloc_semaphore(f"{tag}_{name}"))
            return sems[-1]

        yield ctx, sb, sem
    nc.clear_and_free_semaphores(sems)
    nc.all_engine_barrier(sem_only=True)


class Gemm:

    def __init__(self, c, sb, sem, psum):
        self.raw = [sb(f"w_raw{s}", [P, KT * P], F32) for s in range(2)]
        self.hi = [sb(f"w_hi{s}", [P, KT, P], F32R) for s in range(2)]
        self.lo = [sb(f"w_lo{s}", [P, KT, P], F32R) for s in range(2)]
        self.psum = psum
        self.zero = c["zero"]
        self.raw_full = [sem(f"w_raw_full{s}") for s in range(2)]
        self.hi_done = sem("w_hi_done")
        self.w_ready = [sem(f"w_ready{s}") for s in range(2)]
        self.tile_done = [sem(f"tile_done{s}") for s in range(2)]
        self.psum_free = [sem(f"psum_free{s}") for s in range(2)]

    def load(self, sp, w, first, pairs, single=False):
        for s in range(2):
            sp.dma_start(self.raw[s][:], w[first + s]).then_inc(self.raw_full[s], 16)
        if pairs > 1:
            with sp.Fori(1, pairs) as i:
                for s in range(2):
                    sp.wait_ge(self.w_ready[s], i)
                    sp.dma_start(self.raw[s][:], w[2 * i + (first + s)]).then_inc(self.raw_full[s], 16)
        if single:
            sp.wait_ge(self.w_ready[0], pairs)
            sp.dma_start(self.raw[0][:], w[first + 2 * pairs]).then_inc(self.raw_full[0], 16)

    def split_slot(self, pool, i, s):
        hi = self.hi[s][:].rearrange("p k n -> p (k n)")
        lo = self.lo[s][:].rearrange("p k n -> p (k n)")
        pool.wait_ge(self.raw_full[s], (i + 1) * 16)
        pool.tensor_tensor(hi, self.raw[s][:], self.zero[:, 0:1].to_broadcast([P, KT * P]), ALU.add).then_inc(self.hi_done, 1)
        pool.wait_ge(self.hi_done, 2 * i + (s + 1))
        pool.tensor_tensor(lo, self.raw[s][:], hi.bitcast(F32), ALU.subtract).then_inc(self.w_ready[s], 1)

    def split(self, pool, pairs, single=False):
        for s in range(2):
            self.split_slot(pool, 0, s)
        if pairs > 1:
            with pool.Fori(1, pairs) as i:
                for s in range(2):
                    pool.wait_ge(self.tile_done[s], i)
                    self.split_slot(pool, i, s)
        if single:
            pool.wait_ge(self.tile_done[0], pairs)
            self.split_slot(pool, pairs, 0)

    def tile(self, pe, i, s, act_hi, act_lo, before_k=None):
        pe.wait_ge(self.w_ready[s], i + 1)
        pe.wait_ge(self.psum_free[s], i + 1)
        for k in range(KT):
            if before_k is not None:
                before_k(k)
            for part, (w, a) in enumerate(((self.hi, act_hi), (self.hi, act_lo), (self.lo, act_hi))):
                for h in range(NH):
                    mm = pe.matmul(self.psum[s][:, h, :], w[s][:, k, :], a[:, k, h * HALF:(h + 1) * HALF],
                                   start=(k == 0 and part == 0), stop=(k == KT - 1 and part == 2))
        mm.then_inc(self.tile_done[s], 1)


G, N_ST, HEADS, HD = 4, 128, 16, 64
CH = S // P


def half(ap):
    return ap.rearrange("p (h n) -> p h n", h=NH)


def setup_phase(nc, io, c):
    with phase(nc, "su") as (ctx, sb, sem):
        lam = sb("lam", [P, 2, KT])
        loaded, a_done, v_done = sem("loaded"), sem("act"), sem("dve")
        logit = sb("logit", [P, 2, KT])
        alog = sb("alog", [P, 32])
        tmp = [sb(f"tmp{j}", [P, 2 * KT]) for j in range(3)]
        block = ctx.enter_context(nc.Block())
        loads = [(c[n][:], io[n]) for n in ("gains", "conv_w", "conv_b", "dt_bias", "ssd_norm", "hgrn_norm", "ones",
                                            "ident", "m_ui", "m_us", "m_li", "m_ls", "gate_b")]
        loads += [(c["d_skip"][:], io["d_skip"].to_broadcast([P, HEADS])), (alog[:], io["a_log"].to_broadcast([P, 32])),
                  (lam[:], io["lam"]), (logit[:], io["lb_logits"])]
        one = 16 * len(loads)

        @block.sync
        def _(sp):
            for dst, src in loads:
                sp.dma_start(dst, src).then_inc(loaded, 16)
            sp.wait_ge(loaded, one)

        lam2 = lam[:].rearrange("p d k -> p (d k)")
        hs = c["lru_rate"][:].rearrange("p d k -> p (d k)")
        chain = Softplus(lam2, tmp, hs, -1.0)

        @block.scalar
        def _(act):
            act.wait_ge(loaded, one)
            chain.act(act, a_done)
            act.activation(c["a_exp"][:], alog[:], ACT.Exp).then_inc(a_done, 1)
            act.wait_ge(v_done, 1)
            act.activation(c["lb_e"][:], c["lb_d"][:], ACT.Tanh, scale=0.5).then_inc(a_done, 1)

        @block.vector
        def _(dve):
            dve.memset(c["zero"][:], 0.0)
            dve.wait_ge(loaded, one)
            dve.tensor_tensor(c["lb_d"][:], logit[:, 0, :], logit[:, 1, :], ALU.subtract).then_inc(v_done, 1)
            n = chain.dve(dve, a_done, v_done, 2, 1)
            dve.wait_ge(v_done, n)
            dve.tensor_scalar(hs, hs, -4.0, None, ALU.mult).then_inc(v_done, 1)
            dve.wait_ge(v_done, n + 1)
            dve.tensor_scalar(c["lru_rate2"][:].rearrange("p d k -> p (d k)"), hs, 2.0, None, ALU.mult)
            dve.tensor_scalar(c["lru_rate_n"][:].rearrange("p d k -> p (d k)"), hs, -1.0, None, ALU.mult)
            dve.tensor_scalar(c["gate_bh"][:], c["gate_b"][:], 0.5, None, ALU.mult)
            dve.wait_ge(a_done, 4)
            dve.tensor_scalar(c["oml"][:], c["lb_e"][:], 0.25, 0.25, ALU.mult, ALU.add)
            dve.tensor_scalar(c["noml"][:], c["lb_e"][:], -0.25, -0.25, ALU.mult, ALU.add)
            dve.tensor_scalar(c["lnb"][:], c["lb_e"][:], -0.25, 0.75, ALU.mult, ALU.add)
            dve.tensor_scalar(c["hg_gain"][:], c["hgrn_norm"][:], 0.5, None, ALU.mult)


class Softplus:

    def __init__(self, z, tmp, out, sign):
        self.z, self.tmp, self.out, self.sign = z, tmp, out, sign

    def act(self, act, a_done, base=0):
        act.activation(self.tmp[0][:], self.z, ACT.Abs).then_inc(a_done, 1)
        act.wait_ge(a_done, base + 1)
        act.activation(self.tmp[0][:], self.tmp[0][:], ACT.Exp, scale=-1.0).then_inc(a_done, 1)

    def dve(self, dve, a_done, v_done, a_count, n):
        e, s, q = (t[:] for t in self.tmp)
        dve.wait_ge(a_done, a_count)

        def step(ins):
            nonlocal n
            n += 1
            ins.then_inc(v_done, 1)
            dve.wait_ge(v_done, n)

        step(dve.tensor_scalar(s, e, 2.0, None, ALU.add))
        step(dve.reciprocal(s, s))
        step(dve.tensor_tensor(s, e, s, ALU.mult))
        step(dve.tensor_tensor(q, s, s, ALU.mult))
        step(dve.tensor_scalar(e, q, 1.0 / 17, None, ALU.mult))
        for d in (15, 13, 11, 9, 7, 5, 3):
            step(dve.scalar_tensor_tensor(out=e, in0=e, scalar=1.0 / d, in1=q, op0=ALU.add, op1=ALU.mult))
        step(dve.scalar_tensor_tensor(out=e, in0=e, scalar=1.0, in1=s, op0=ALU.add, op1=ALU.mult))
        step(dve.tensor_scalar(s, self.z, self.sign, 0.0, ALU.mult, ALU.max))
        step(dve.scalar_tensor_tensor(out=self.out, in0=e, scalar=2.0, in1=s, op0=ALU.mult, op1=ALU.add))
        return n


PAIRS_LRU, PAIRS_XZ, PAIRS_BC = 8, 8, 4


def lru_phase(nc, io, c, hi, lo, psum):
    with phase(nc, "lr") as (ctx, sb, sem):
        g = Gemm(c, sb, sem, psum[0:2])
        up, u = sb("up", [P, S + 4]), sb("u", [P, S])
        ta, tx, a, a2, th, h = ([sb(f"{n}{d}", [P, S]) for d in range(2)] for n in ("ta", "tx", "a", "a2", "th", "h"))
        gg, yb = sb("gg", [P, S]), sb("yb", [P, S])
        gw = sb("gw", [P, 4, P])
        pads, tap0, taps, gw_full, gate, gate_read = (
            sem(n) for n in ("pads", "tap0", "taps", "gw_full", "gate", "gate_read"))
        decay, q_done, root, step, y_done, y_stored = (
            sem(n) for n in ("decay", "q_done", "root", "step", "y_done", "y_stored"))
        block = ctx.enter_context(nc.Block())
        NP_ = PAIRS_LRU

        @block.sync
        def _(sp):
            w = io["w"]
            for s in range(2):
                sp.dma_start(g.raw[s][:], w[s]).then_inc(g.raw_full[s], 16)
            sp.dma_start(gw[:], io["gate_w"][0]).then_inc(gw_full, 16)
            with sp.Fori(0, NP_ - 1) as i:
                for s in range(2):
                    sp.wait_ge(g.w_ready[s], i + 1)
                    sp.dma_start(g.raw[s][:], w[2 * i + (s + 2)]).then_inc(g.raw_full[s], 16)
                sp.wait_ge(gate, i * 4 + 4)
                sp.dma_start(gw[:], io["gate_w"][i + 1]).then_inc(gw_full, 16)
                sp.wait_ge(y_done, i + 2)
                sp.dma_start(io["yb_d"][i], yb[:]).then_inc(y_stored, 16)
            sp.wait_ge(y_done, NP_ + 1)
            sp.dma_start(io["yb_d"][NP_ - 1], yb[:]).then_inc(y_stored, 16)
            sp.wait_ge(y_stored, 16 * (NP_ + 1))

        @block.gpsimd
        def _(pool):
            g.split(pool, NP_)

        @block.tensor
        def _(pe):
            with pe.Fori(0, NP_) as i:
                g.tile(pe, i, 0, hi, lo)
                g.tile(pe, i, 1, hi, lo)
                pe.wait_ge(gw_full, i * 16 + 16)
                pe.wait_ge(taps, i * 3 + 3)
                for d in range(2):
                    for r in range(2):
                        pe.wait_ge(gate_read, i * 4 + (2 * d + r + 1))
                        for hh in range(NH):
                            mm = pe.matmul(psum[2 + r][:, hh, :], gw[:, 2 * d + r, :],
                                           u[:, hh * HALF:(hh + 1) * HALF], start=True, stop=True)
                        mm.then_inc(gate, 1)

        @block.scalar
        def _(act):
            for s in range(2):
                act.sem_inc(g.psum_free[s], 1)
            act.sem_inc(gate_read, 2)
            act.wait_ge(pads, 2)
            with act.Fori(0, NP_) as i:
                act.wait_ge(g.tile_done[0], i + 1)
                act.wait_ge(y_done, i + 1)
                act.activation(half(up[:, 1:1 + S]), psum[0][:], ACT.Copy).then_inc(g.psum_free[0], 1)
                act.wait_ge(g.psum_free[0], i + 2)
                act.activation(u[:], up[:, 0:S], ACT.Identity, scale=c["conv_w"][:, bass.ds(i, 1), 0],
                               bias=c["conv_b"][:, bass.ds(i, 1)]).then_inc(tap0, 1)
                for d in range(2):
                    for r, out in enumerate((ta, tx)):
                        act.wait_ge(gate, i * 4 + (2 * d + r + 1))
                        act.activation(half(out[d][:]), psum[2 + r][:], ACT.Tanh, scale=0.5,
                                       bias=c["gate_bh"][:, bass.ds(i, 1), 2 * d + r]).then_inc(gate_read, 1)
                    act.wait_ge(gate_read, i * 4 + (2 * d + 4))
                    for out, rate, func in ((a, "lru_rate", ACT.Exp), (a2, "lru_rate2", ACT.Exp),
                                            (th, "lru_rate_n", ACT.Tanh)):
                        r_ = c[rate][:, d, bass.ds(i, 1)]
                        act.activation(out[d][:], ta[d][:], func, scale=r_, bias=r_).then_inc(decay, 1)
                for d in range(2):
                    act.wait_ge(q_done, i * 2 + (d + 1))
                    act.activation(th[d][:], th[d][:], ACT.Sqrt).then_inc(root, 1)
                act.wait_ge(g.tile_done[1], i + 1)
                act.activation(half(gg[:]), psum[1][:], ACT.Gelu_apprx_tanh).then_inc(g.psum_free[1], 1)

        @block.vector
        def _(dve):
            dve.sem_inc(y_done, 1)
            dve.sem_inc(y_stored, 16)
            dve.memset(up[:, 0:1], 0.0).then_inc(pads, 1)
            dve.memset(up[:, S + 1:S + 4], 0.0).then_inc(pads, 1)
            dve.wait_ge(pads, 2)
            with dve.Fori(0, NP_) as i:
                dve.wait_ge(tap0, i + 1)
                for k in range(1, 4):
                    if k > 1:
                        dve.wait_ge(taps, i * 3 + (k - 1))
                    dve.scalar_tensor_tensor(out=u[:], in0=up[:, k:k + S], scalar=c["conv_w"][:, bass.ds(i, 1), k],
                                             in1=u[:], op0=ALU.mult, op1=ALU.add).then_inc(taps, 1)
                dve.wait_ge(taps, i * 3 + 3)
                for d in range(2):
                    dve.wait_ge(decay, i * 6 + (3 * d + 3))
                    dve.scalar_tensor_tensor(out=th[d][:], in0=a2[d][:], scalar=1.0, in1=th[d][:],
                                             op0=ALU.add, op1=ALU.mult).then_inc(q_done, 1)
                    dve.scalar_tensor_tensor(out=tx[d][:], in0=tx[d][:], scalar=1.0, in1=u[:],
                                             op0=ALU.add, op1=ALU.mult).then_inc(step, 1)
                for d in range(2):
                    dve.wait_ge(root, i * 2 + (d + 1))
                    dve.wait_ge(step, i * 7 + (d + 2 if d == 0 else 4))
                    dve.scalar_tensor_tensor(out=tx[d][:], in0=th[d][:], scalar=0.5, in1=tx[d][:],
                                             op0=ALU.mult, op1=ALU.mult).then_inc(step, 1)
                    dve.wait_ge(step, i * 7 + (2 * d + 3))
                    t = slice(None) if d == 0 else slice(None, None, -1)
                    dve.tensor_tensor_scan(h[d][:, t], a[d][:, t], tx[d][:, t], 0.0, ALU.mult, ALU.add)\
                       .then_inc(step, 1)
                dve.wait_ge(step, i * 7 + 6)
                dve.tensor_tensor(h[0][:], h[0][:], h[1][:], ALU.add).then_inc(step, 1)
                dve.wait_ge(step, i * 7 + 7)
                dve.wait_ge(g.psum_free[1], i + 2)
                dve.wait_ge(y_stored, i * 16 + 16)
                dve.tensor_tensor(yb[:], h[0][:], gg[:], ALU.mult).then_inc(y_done, 1)


def conv_phase(nc, io, c, hi, lo, psum, dt_t):
    with phase(nc, "cv") as (ctx, sb, sem):
        g = Gemm(c, sb, sem, psum[0:2])
        up, acc, sc = ([sb(f"{n}{s}", [P, S + 4 if n == "up" else S]) for s in range(2)] for n in ("up", "acc", "sc"))
        tok = sb("tok", [P, S])
        pads, tr, tok_done, tok_stored = (sem(n) for n in ("pads", "tr", "tok_done", "tok_stored"))
        tap0, taps, silu, cm_stored = ([sem(f"{n}{s}") for s in range(2)] for n in ("tap0", "taps", "silu", "cm_stored"))
        block = ctx.enter_context(nc.Block())
        XZ, BC, W0 = PAIRS_XZ, PAIRS_BC, 2 * PAIRS_LRU
        tok3 = tok[:].rearrange("p (c n) -> p c n", c=CH)
        xs_v = io["xs_d"].rearrange("c p (i n) -> i p c n", n=P)
        bt_v = io["bt_d"].rearrange("c p (i n) -> i p c n", n=P)

        @block.sync
        def _(sp):
            w = io["w"]

            def weights(n):
                for s in range(2):
                    sp.wait_ge(g.w_ready[s], n)
                    sp.dma_start(g.raw[s][:], w[2 * n + (s + W0)]).then_inc(g.raw_full[s], 16)

            for s in range(2):
                sp.dma_start(g.raw[s][:], w[s + W0]).then_inc(g.raw_full[s], 16)
            with sp.Fori(0, XZ) as n:
                weights(n + 1)
                sp.wait_ge(g.psum_free[1], n + 2)
                sp.dma_start(io["z_d"][n], sc[1][:]).then_inc(cm_stored[1], 16)
                sp.wait_ge(tok_done, n + 2)
                sp.dma_start(xs_v[n], tok3).then_inc(tok_stored, 16)

            def store_bc(i):
                sp.wait_ge(silu[0], i + (XZ + 2))
                sp.dma_start(io["b_d"][i], sc[0][:]).then_inc(cm_stored[0], 16)
                sp.wait_ge(tok_done, i + (XZ + 2))
                sp.dma_start(bt_v[i], tok3).then_inc(tok_stored, 16)
                sp.wait_ge(silu[1], i + 2)
                sp.dma_start(io["c_d"][i], sc[1][:]).then_inc(cm_stored[1], 16)

            with sp.Fori(0, BC - 1) as i:
                weights(i + (XZ + 1))
                store_bc(i)
            sp.wait_ge(g.w_ready[0], XZ + BC)
            sp.dma_start(g.raw[0][:], w[2 * (XZ + BC) + W0]).then_inc(g.raw_full[0], 16)
            store_bc(BC - 1)
            sp.wait_ge(cm_stored[0], 16 * (BC + 1))
            sp.wait_ge(cm_stored[1], 16 * (XZ + BC + 1))
            sp.wait_ge(tok_stored, 16 * (XZ + BC + 1))

        @block.gpsimd
        def _(pool):
            g.split(pool, XZ + BC, single=True)

        @block.tensor
        def _(pe):
            pe.sem_inc(tr, 1)
            with pe.Fori(0, XZ + BC) as n:
                g.tile(pe, n, 0, hi, lo)
                g.tile(pe, n, 1, hi, lo)
                pe.wait_ge(silu[0], n + 2)
                pe.wait_ge(tok_done, n + 1)
                for cc in range(CH):
                    mm = pe.transpose(psum[2][:, cc // 4, (cc % 4) * P:(cc % 4 + 1) * P],
                                      sc[0][:, cc * P:(cc + 1) * P], c["ident"][:])
                mm.then_inc(tr, 1)
            g.tile(pe, XZ + BC, 0, hi, lo)

        def conv_head(act, s, n, m, idx):
            act.wait_ge(g.tile_done[s], n + 1)
            act.wait_ge(taps[s], m * 3 + 1)
            act.activation(half(up[s][:, 1:1 + S]), psum[s][:], ACT.Copy).then_inc(g.psum_free[s], 1)
            act.wait_ge(g.psum_free[s], n + 2)
            act.wait_ge(silu[s], m + 1)
            act.activation(acc[s][:], up[s][:, 0:S], ACT.Identity, scale=c["conv_w"][:, bass.ds(idx, 1), 0],
                           bias=c["conv_b"][:, bass.ds(idx, 1)]).then_inc(tap0[s], 1)

        def conv_taps(dve, s, m, idx):
            dve.wait_ge(tap0[s], m + 1)
            for k in range(1, 4):
                if k > 1:
                    dve.wait_ge(taps[s], m * 3 + k)
                dve.scalar_tensor_tensor(out=acc[s][:], in0=up[s][:, k:k + S],
                                         scalar=c["conv_w"][:, bass.ds(idx, 1), k], in1=acc[s][:],
                                         op0=ALU.mult, op1=ALU.add).then_inc(taps[s], 1)

        @block.scalar
        def _(act):
            for s in range(2):
                act.sem_inc(g.psum_free[s], 1)
                act.sem_inc(silu[s], 1)
            act.wait_ge(pads, 4)
            with act.Fori(0, XZ) as n:
                conv_head(act, 0, n, n, n + PAIRS_LRU)
                act.wait_ge(taps[0], n * 3 + 4)
                act.wait_ge(tr, n + 1)
                act.activation(sc[0][:], acc[0][:], ACT.Silu).then_inc(silu[0], 1)
                act.wait_ge(g.tile_done[1], n + 1)
                act.wait_ge(cm_stored[1], n * 16 + 16)
                act.activation(half(sc[1][:]), psum[1][:], ACT.Silu).then_inc(g.psum_free[1], 1)
            with act.Fori(0, BC) as i:
                n = i + XZ
                conv_head(act, 0, n, n, 2 * i + (PAIRS_LRU + XZ))
                act.wait_ge(taps[0], n * 3 + 4)
                act.wait_ge(tr, n + 1)
                act.wait_ge(cm_stored[0], i * 16 + 16)
                act.activation(sc[0][:], acc[0][:], ACT.Silu).then_inc(silu[0], 1)
                conv_head(act, 1, n, i, 2 * i + (PAIRS_LRU + XZ + 1))
                act.wait_ge(taps[1], i * 3 + 4)
                act.wait_ge(cm_stored[1], n * 16 + 16)
                act.activation(sc[1][:], acc[1][:], ACT.Silu).then_inc(silu[1], 1)
            act.wait_ge(g.tile_done[0], XZ + BC + 1)
            act.activation(half(dt_t[:]), psum[0][0:2 * HEADS], ACT.Identity, bias=c["dt_bias"][:, 0:1])

        @block.vector
        def _(dve):
            for s in range(2):
                dve.sem_inc(taps[s], 1)
                dve.sem_inc(cm_stored[s], 16)
                dve.memset(up[s][:, 0:1], 0.0).then_inc(pads, 1)
                dve.memset(up[s][:, S + 1:S + 4], 0.0).then_inc(pads, 1)
            dve.sem_inc(tok_done, 1)
            dve.sem_inc(tok_stored, 16)
            dve.wait_ge(pads, 4)

            def by_tokens(n):
                dve.wait_ge(tr, n + 2)
                dve.wait_ge(tok_stored, n * 16 + 16)
                dve.tensor_copy(half(tok[:]), psum[2][:]).then_inc(tok_done, 1)

            with dve.Fori(0, XZ) as n:
                conv_taps(dve, 0, n, n + PAIRS_LRU)
                by_tokens(n)
            with dve.Fori(0, BC) as i:
                conv_taps(dve, 0, i + XZ, 2 * i + (PAIRS_LRU + XZ))
                by_tokens(i + XZ)
                conv_taps(dve, 1, i, 2 * i + (PAIRS_LRU + XZ + 1))


HH = HEADS // 2
CW = HH * HD


def ssd_coef_phase(nc, c, dt_t, co, psum):
    with phase(nc, "cf") as (ctx, sb, sem):
        W = CH * 2 * HEADS
        z, tmp, da = sb("z", [P, W]), [sb(f"tmp{j}", [P, W]) for j in range(3)], co["da"]
        tr, a_done, v_done, sums, exps = sem("tr"), sem("act"), sem("dve"), sem("sums"), sem("exps")
        flat = lambda t: t[:].rearrange("p c h -> p (c h)")
        sp_ = Softplus(z[:], tmp, flat(co["dt"]), 1.0)
        block = ctx.enter_context(nc.Block())

        @block.tensor
        def _(pe):
            for n in range(CH):
                mm = pe.transpose(psum[0][:, 0, n * 32:n * 32 + 32], dt_t[:, n * P:(n + 1) * P], c["ident"][0:32, 0:32])
            mm.then_inc(tr, 1)
            pe.wait_ge(v_done, 1000)
            f, b = da[:, :, 0:HEADS], da[:, :, HEADS:2 * HEADS]
            w = psum[1][:, 0, 0:W].rearrange("p (c h) -> p c h", c=CH)
            e = psum[1][:, 1, 0:W].rearrange("p (c h) -> p c h", c=CH)
            for out, mask, rhs in ((w[:, :, 0:HEADS], "m_ls", f), (w[:, :, HEADS:], "m_us", b),
                                   (e[:, :, 0:HEADS], "m_ui", f), (e[:, :, HEADS:], "m_li", b),
                                   (psum[2][:, 0, 0:W].rearrange("p (c h) -> p c h", c=CH), "ones", da[:])):
                mm = pe.matmul(out, c[mask][:], rhs, start=True, stop=True)
            mm.then_inc(sums, 1)

        @block.scalar
        def _(act):
            act.wait_ge(tr, 1)
            act.activation(z[:], psum[0][:, 0, 0:W], ACT.Copy).then_inc(a_done, 1)
            act.wait_ge(a_done, 1)
            sp_.act(act, a_done, 1)
            act.wait_ge(sums, 1)
            for out, src in (("w", psum[1][:, 0, 0:W]), ("e", psum[1][:, 1, 0:W]), ("tot", psum[2][:, 0, 0:W])):
                act.activation(flat(co[out]), src, ACT.Exp).then_inc(exps, 1)

        @block.vector
        def _(dve):
            n = sp_.dve(dve, a_done, v_done, 3, 0)
            dve.scalar_tensor_tensor(out=da[:], in0=co["dt"][:], scalar=-1.0,
                                     in1=c["a_exp"][:].unsqueeze(1).to_broadcast([P, CH, 2 * HEADS]),
                                     op0=ALU.mult, op1=ALU.mult).then_inc(v_done, 1000 - n)
            dve.wait_ge(exps, 3)
            dve.tensor_tensor(co["cw"][:], co["dt"][:], co["w"][:], ALU.mult)


def ssd_back_states_phase(nc, io, co, hb, psum):
    with phase(nc, "bs") as (ctx, sb, sem):
        bt, xs, xw = ([sb(f"{n}{q}", [P, w]) for q in range(2)] for n, w in (("bt", G * N_ST), ("xs", D), ("xw", D)))
        full = [sem(f"full{q}") for q in range(2)]
        xw_done, s_done, decayed, h_done = sem("xw_done"), sem("s_done"), sem("decayed"), sem("h_done")
        LAST = CH - 1
        block = ctx.enter_context(nc.Block())

        def steps(eng, step):
            for j in range(LAST):
                step(j, j % 2, j // 2)

        @block.sync
        def _(sp):
            def load(cc, q):
                sp.dma_start(bt[q][:], io["bt_d"][cc]).then_inc(full[q], 16)
                sp.dma_start(xs[q][:], io["xs_d"][cc]).then_inc(full[q], 16)

            load(LAST, 0)
            load(LAST - 1, 1)
            for j in range(2, LAST):
                sp.wait_ge(s_done, j - 1)
                load(LAST - j, j % 2)

        @block.gpsimd
        def _(pool):
            def step(j, q, i):
                pool.wait_ge(full[q], i * 32 + 32)
                pool.tensor_tensor(xw[q][:].rearrange("p (h d) -> p h d", h=HEADS),
                                   xs[q][:].rearrange("p (h d) -> p h d", h=HEADS),
                                   co["cw"][:, LAST - j, HEADS:].unsqueeze(2)
                                   .to_broadcast([P, HEADS, HD]), ALU.mult).then_inc(xw_done, 1)

            steps(pool, step)

        @block.tensor
        def _(pe):
            def step(j, q, i):
                pe.wait_ge(xw_done, j + 1)
                pe.wait_ge(h_done, j + 1)
                for gg in range(G):
                    mm = pe.matmul(psum[q][:, gg // 2, (gg % 2) * 256:(gg % 2) * 256 + 256],
                                   bt[q][:, gg * N_ST:(gg + 1) * N_ST], xw[q][:, gg * 256:(gg + 1) * 256],
                                   start=True, stop=True)
                mm.then_inc(s_done, 1)

            steps(pe, step)

        @block.vector
        def _(dve):
            dve.memset(hb[:, LAST, :], 0.0).then_inc(h_done, 2)

            def step(j, q, i):
                cc = LAST - j
                tot = co["tot"][:, cc, HEADS:].unsqueeze(2).to_broadcast([P, HEADS, HD])
                new = hb[:, cc - 1, :]
                dve.wait_ge(h_done, j + 2)
                dve.tensor_tensor(new.rearrange("p (h d) -> p h d", h=HEADS),
                                  hb[:, cc, :].rearrange("p (h d) -> p h d", h=HEADS), tot, ALU.mult)\
                   .then_inc(decayed, 1)
                dve.wait_ge(decayed, j + 1)
                dve.wait_ge(s_done, j + 1)
                dve.tensor_tensor(half(new), psum[q][:], half(new), ALU.add).then_inc(h_done, 1)

            steps(dve, step)


def ssd_phase(nc, io, c, co, hb, u, psum):
    with phase(nc, "sd") as (ctx, sb, sem):
        two = lambda n, shape: [sb(f"{n}{s}", shape) for s in range(2)]
        bc, cc_, z = ([sb(f"{n}{q}", shape) for q in range(4)] for n, shape in
                      (("b", [P, 2, P]), ("c", [P, 2, P]), ("z", [P, 4, P])))
        bt, xs = [sb(f"bt{q}", [P, 2 * N_ST]) for q in range(4)], [sb(f"xs{q}", [P, CW]) for q in range(4)]
        xf, xb, xw, dx, y, y2 = (two(n, [P, CW]) for n in ("xf", "xb", "xw", "dx", "y", "y2"))
        rf, rb, ex, gu, gl = (two(n, [P, HH, P]) for n in ("rf", "rb", "ex", "gu", "gl"))
        cu, cl = two("cu", [P, 2, P]), two("cl", [P, 2, P])
        hf = sb("hf", [P, 2, CW])
        full = [sem(f"full{q}") for q in range(4)]
        (rf_ok, rb_ok, xsc, dx_ok, seg, cbt, exp_ok, cul, gu_ok, gl_ok, back, hf_ok, y_ok, tr, u_ok) = (
            [sem(f"{n}{s}") for s in range(2)] for n in
            ("rf_ok", "rb_ok", "xsc", "dx_ok", "seg", "cbt", "exp_ok", "cul", "gu_ok", "gl_ok", "back", "hf_ok",
             "y_ok", "tr", "u_ok"))
        dstep = sem("dstep")
        block = ctx.enter_context(nc.Block())
        TURNS = CH // 2

        def pipeline(eng, front, third, back_):
            def step(i, m, first=False, last=False):
                if not last:
                    front(i, m + 1) if m < 3 else front(i + 1, 0)
                if not first:
                    third(i, m - 1) if m else third(i - 1, 3)
                back_(i, m)

            front(0, 0)
            for m in range(4):
                step(0, m, first=(m == 0))
            with eng.Fori(1, TURNS - 1) as i:
                for m in range(4):
                    step(i, m)
            for m in range(4):
                step(TURNS - 1, m, last=(m == 3))
            third(TURNS - 1, 3)

        none = lambda i, m: None
        heads = lambda ap: ap.rearrange("p (h d) -> p h d", h=HH)

        def coef(name, d, i, m):
            at = d * HEADS + (m % 2) * HH
            return co[name][:, bass.ds(2 * i + m // 2, 1), at:at + HH].rearrange("p c h -> p (c h)").unsqueeze(2)

        @block.sync
        def _(sp):
            def load(i, m):
                h, c_ = m % 2, 2 * i + m // 2
                t = bass.ds(c_ * P, P)
                for dst, src in ((bc[m][:], io["b_d"][2 * h:2 * h + 2, :, t].rearrange("g p t -> p g t")),
                                 (cc_[m][:], io["c_d"][2 * h:2 * h + 2, :, t].rearrange("g p t -> p g t")),
                                 (xs[m][:], io["xs_d"][c_][:, h * CW:(h + 1) * CW]),
                                 (bt[m][:], io["bt_d"][c_][:, h * 256:(h + 1) * 256]),
                                 (z[m][:], io["z_d"][4 * h:4 * h + 4, :, t].rearrange("k p t -> p k t"))):
                    sp.dma_start(dst, src).then_inc(full[m], 16)

            for m in range(4):
                load(0, m)
            with sp.Fori(1, TURNS) as i:
                for m in range(4):
                    sp.wait_ge(u_ok[m % 2], 2 * i + m // 2)
                    load(i, m)

        @block.gpsimd
        def _(pool):
            def front(i, m):
                h, c_ = m % 2, 2 * i + m // 2
                pool.wait_ge(full[m], i * 80 + 80)
                pool.wait_ge(back[h], c_ + 1)
                pool.tensor_tensor(rb[h][:], c["m_li"][:].unsqueeze(1).to_broadcast([P, HH, P]),
                                   coef("da", 1, i, m).to_broadcast([P, HH, P]), ALU.mult).then_inc(rb_ok[h], 1)
                for dst, name, d in ((xf, "dt", 0), (xb, "dt", 1), (xw, "cw", 0)):
                    pool.tensor_tensor(heads(dst[h][:]), heads(xs[m][:]), coef(name, d, i, m).to_broadcast([P, HH, HD]),
                                       ALU.mult).then_inc(xsc[h], 1)
                pool.wait_ge(y_ok[h], c_ + 1)
                pool.tensor_tensor(heads(dx[h][:]), heads(xs[m][:]), c["d_skip"][:, h * HH:(h + 1) * HH].unsqueeze(2)
                                   .to_broadcast([P, HH, HD]), ALU.mult).then_inc(dx_ok[h], 1)
                pool.wait_ge(exp_ok[h], c_ + 2)
                pool.wait_ge(cul[h], c_ * 2 + 4)
                pool.tensor_tensor(gl[h][:].rearrange("p (g h) t -> p g h t", g=2),
                                   ex[h][:].rearrange("p (g h) t -> p g h t", g=2),
                                   cl[h][:].unsqueeze(2).to_broadcast([P, 2, 4, P]), ALU.mult).then_inc(gl_ok[h], 1)

            pipeline(pool, front, none, none)

        @block.tensor
        def _(pe):
            for s in range(2):
                pe.sem_inc(back[s], 1)
                pe.sem_inc(tr[s], 1)

            def front(i, m):
                h, c_ = m % 2, 2 * i + m // 2
                pe.wait_ge(rf_ok[h], c_ + 1)
                pe.wait_ge(rb_ok[h], c_ + 1)
                pe.wait_ge(exp_ok[1 - h], c_ + (1 + h))
                for gg in range(2):
                    for mask, r, start in (("m_ls", rf, True), ("m_us", rb, False)):
                        mm = pe.matmul(psum[0][:, gg, :], c[mask][:], r[h][:, 4 * gg:4 * gg + 4, :],
                                       start=start, stop=not start)
                mm.then_inc(seg[h], 1)
                pe.wait_ge(full[m], i * 80 + 80)
                pe.wait_ge(cul[1 - h], c_ * 2 + (2 + 2 * h))
                for gg in range(2):
                    mm = pe.matmul(psum[1][:, 0, gg * P:(gg + 1) * P], bc[m][:, gg, :], cc_[m][:, gg, :],
                                   start=True, stop=True)
                mm.then_inc(cbt[h], 1)

            def third(i, m):
                h, c_ = m % 2, 2 * i + m // 2
                pe.wait_ge(y_ok[h], c_ + 2)
                pe.wait_ge(u_ok[1 - h], c_ + (1 + h))
                for j in range(4):
                    mm = pe.transpose(psum[3][:, 1, j * P:(j + 1) * P], y[h][:, j * P:(j + 1) * P], c["ident"][:])
                mm.then_inc(tr[h], 1)

            def back_(i, m):
                h, c_ = m % 2, 2 * i + m // 2
                pe.wait_ge(gu_ok[h], c_ + 1)
                pe.wait_ge(gl_ok[h], c_ + 1)
                pe.wait_ge(xsc[h], c_ * 3 + 3)
                pe.wait_ge(y_ok[1 - h], c_ + (1 + h))
                pe.wait_ge(hf_ok[1 - h], c_ + (1 + h))
                pe.wait_ge(hf_ok[h], c_ + 1)
                for hd in range(HH):
                    o = psum[1][:, 1, hd * HD:(hd + 1) * HD]
                    pe.matmul(o, gu[h][:, hd, :], xf[h][:, hd * HD:(hd + 1) * HD], start=True, stop=False)
                    pe.matmul(o, gl[h][:, hd, :], xb[h][:, hd * HD:(hd + 1) * HD], start=False, stop=True)
                for gg in range(2):
                    q = slice(gg * 256, (gg + 1) * 256)
                    pe.matmul(psum[2][:, 0, q], cc_[m][:, gg, :], hf[:, h, q], start=True, stop=True)
                    pe.matmul(psum[2][:, 1, q], cc_[m][:, gg, :],
                              hb[:, bass.ds(c_, 1), h * CW + gg * 256:h * CW + gg * 256 + 256]
                              .rearrange("p c n -> p (c n)"), start=True, stop=True)
                    mm = pe.matmul(psum[3][:, 0, q], bt[m][:, gg * N_ST:(gg + 1) * N_ST], xw[h][:, q],
                                   start=True, stop=True)
                mm.then_inc(back[h], 1)

            pipeline(pe, front, third, back_)

        @block.scalar
        def _(act):
            for s in range(2):
                act.sem_inc(exp_ok[s], 1)

            def front(i, m):
                h, c_ = m % 2, 2 * i + m // 2
                act.wait_ge(seg[h], c_ + 1)
                act.wait_ge(back[h], c_ + 1)
                act.activation(ex[h][:].rearrange("p (g h) t -> p g (h t)", g=2), psum[0][:], ACT.Exp)\
                   .then_inc(exp_ok[h], 1)

            pipeline(act, front, none, none)

        @block.vector
        def _(dve):
            for s in range(2):
                dve.sem_inc(cul[s], 2)
                dve.sem_inc(y_ok[s], 1)
                dve.sem_inc(u_ok[s], 1)
                dve.memset(hf[:, s, :], 0.0).then_inc(hf_ok[s], 1)

            def front(i, m):
                h, c_ = m % 2, 2 * i + m // 2
                dve.wait_ge(back[h], c_ + 1)
                dve.tensor_tensor(rf[h][:], c["m_ui"][:].unsqueeze(1).to_broadcast([P, HH, P]),
                                  coef("da", 0, i, m).to_broadcast([P, HH, P]), ALU.mult).then_inc(rf_ok[h], 1)

            def products(i, m):
                h, c_ = m % 2, 2 * i + m // 2
                dve.wait_ge(cbt[h], c_ + 1)
                for dst, mask in ((cu, "m_ui"), (cl, "m_li")):
                    dve.tensor_tensor(dst[h][:], psum[1][:, 0, 0:2 * P].rearrange("p (g t) -> p g t", g=2),
                                      c[mask][:].unsqueeze(1).to_broadcast([P, 2, P]), ALU.mult).then_inc(cul[h], 1)
                dve.wait_ge(exp_ok[h], c_ + 2)
                dve.wait_ge(cul[h], c_ * 2 + 4)
                dve.tensor_tensor(gu[h][:].rearrange("p (g h) t -> p g h t", g=2),
                                  ex[h][:].rearrange("p (g h) t -> p g h t", g=2),
                                  cu[h][:].unsqueeze(2).to_broadcast([P, 2, 4, P]), ALU.mult).then_inc(gu_ok[h], 1)

            def third(i, m):
                h, c_ = m % 2, 2 * i + m // 2
                dve.wait_ge(tr[h], c_ + 2)
                dve.tensor_tensor(u[:, 4 * h:4 * h + 4, bass.ds(c_ * P, P)],
                                  psum[3][:, 1, :].rearrange("p (k t) -> p k t", k=4), z[m][:], ALU.mult)\
                   .then_inc(u_ok[h], 1)

            def back_(i, m):
                h, c_, n = m % 2, 2 * i + m // 2, i * 20 + 5 * m
                dve.wait_ge(back[h], c_ + 2)
                dve.wait_ge(tr[h], c_ + 1)
                dve.tensor_tensor(heads(y[h][:]), heads(psum[2][:, 0, :]), coef("e", 0, i, m).to_broadcast([P, HH, HD]),
                                  ALU.mult).then_inc(dstep, 1)
                dve.tensor_tensor(heads(y2[h][:]), heads(psum[2][:, 1, :]), coef("e", 1, i, m)
                                  .to_broadcast([P, HH, HD]), ALU.mult).then_inc(dstep, 1)
                dve.tensor_tensor(heads(hf[:, h, :]), heads(hf[:, h, :]), coef("tot", 0, i, m)
                                  .to_broadcast([P, HH, HD]), ALU.mult).then_inc(dstep, 1)
                dve.wait_ge(dstep, n + 2)
                dve.tensor_tensor(y[h][:], y[h][:], y2[h][:], ALU.add).then_inc(dstep, 1)
                dve.wait_ge(dstep, n + 3)
                dve.tensor_tensor(hf[:, h, :], psum[3][:, 0, :], hf[:, h, :], ALU.add).then_inc(hf_ok[h], 1)
                dve.wait_ge(dstep, n + 4)
                dve.tensor_tensor(y[h][:], psum[1][:, 1, :], y[h][:], ALU.add).then_inc(dstep, 1)
                dve.wait_ge(dx_ok[h], c_ + 1)
                dve.wait_ge(dstep, n + 5)
                dve.tensor_tensor(y[h][:], y[h][:], dx[h][:], ALU.add).then_inc(y_ok[h], 1)

            def front_only(i, m):
                front(i, m)

            def step(i, m, first=False, last=False):
                nxt = (i, m + 1) if m < 3 else (i + 1, 0)
                if not last:
                    front(*nxt)
                if not first:
                    third(i, m - 1) if m else third(i - 1, 3)
                if not last:
                    products(*nxt)
                back_(i, m)

            front(0, 0)
            products(0, 0)
            for m in range(4):
                step(0, m, first=(m == 0))
            with dve.Fori(1, TURNS - 1) as i:
                for m in range(4):
                    step(i, m)
            for m in range(4):
                step(TURNS - 1, m, last=(m == 3))
            third(TURNS - 1, 3)


GH = 8
GC = 64
NCH = S // GC
SCALE = float(P) ** -0.5
MAGIC = float(0x5F3759DF)
I32 = mybir.dt.int32


def rsqrt_steps(dve, done, n, v, r, t, src, inv_n):
    def step(ins):
        nonlocal n
        n = n + 1
        ins.then_inc(done, 1)
        dve.wait_ge(done, n)

    step(dve.tensor_scalar(v, src, inv_n, EPS, ALU.mult, ALU.add))
    step(dve.tensor_scalar(t.bitcast(I32), v.bitcast(I32), 1, None, ALU.arith_shift_right))
    step(dve.tensor_scalar(r.bitcast(I32), t.bitcast(I32), -1.0, MAGIC, ALU.mult, ALU.add))
    for _ in range(4):
        step(dve.tensor_tensor(t, r, r, ALU.mult))
        step(dve.scalar_tensor_tensor(out=t, in0=t, scalar=-0.5, in1=v, op0=ALU.mult, op1=ALU.mult))
        step(dve.scalar_tensor_tensor(out=r, in0=t, scalar=1.5, in1=r, op0=ALU.add, op1=ALU.mult))
    return n


RSQRT_STEPS = 15


def norm_phase(nc, c, src, groups, gain, hi, lo, psum, tag, load=None):
    per = KT // groups
    with phase(nc, tag) as (ctx, sb, sem):
        sq, h = [sb(f"sq{b}", [P, S]) for b in range(2)], [sb(f"h{b}", [P, S]) for b in range(2)]
        diag = sb("diag", [P, CH, P])
        v, r, t = (sb(n, [P, CH]) for n in ("v", "r", "t"))
        sq_done, sq_used, newton, diag_done, spread, h_done, hi_done, lo_done = (
            sem(n) for n in ("sq_done", "sq_used", "newton", "diag_done", "spread", "h_done", "hi_done", "lo_done"))
        full = [sem(f"full{q}") for q in range(KT)]
        block = ctx.enter_context(nc.Block())

        if load is not None:
            @block.sync
            def _(sp):
                for k in range(KT):
                    sp.dma_start(src[:, k, :], load[:, k, :]).then_inc(full[k], 16)

        @block.scalar
        def _(act):
            def split_hi(k):
                act.wait_ge(h_done, k + 1)
                act.activation(hi[:, k, :], h[k % 2][:], ACT.Copy).then_inc(hi_done, 1)

            for k in range(KT):
                if k >= 2:
                    act.wait_ge(sq_used, k - 1)
                if load is not None:
                    act.wait_ge(full[k], 16)
                act.activation(sq[k % 2][:], src[:, k, :], ACT.Square).then_inc(sq_done, 1)
            for k in range(KT):
                split_hi(k)

        @block.tensor
        def _(pe):
            def spread_group(g):
                pe.wait_ge(diag_done, g + 1)
                if g >= 2:
                    pe.wait_ge(h_done, (g - 1) * per)
                for hh in range(NH):
                    mm = pe.matmul(psum[2 + g % 2][:, hh, :], c["ones"][:],
                                   diag[:, 4 * hh:4 * hh + 4, :], start=True, stop=True)
                mm.then_inc(spread, 1)

            for g in range(groups):
                if g >= 2:
                    pe.wait_ge(newton, (g - 2) * RSQRT_STEPS + 1)
                for k in range(g * per, (g + 1) * per):
                    pe.wait_ge(sq_done, k + 1)
                    for n in range(CH):
                        mm = pe.matmul(psum[g % 2][:, 0, n:n + 1], sq[k % 2][:, n * P:(n + 1) * P], c["ones"][:, 0:1],
                                       start=(k == g * per and n == 0), stop=(k == (g + 1) * per - 1),
                                       skip_group_check=True)
                    mm.then_inc(sq_used, 1)
                if g >= 1:
                    spread_group(g - 1)
            spread_group(groups - 1)

        @block.vector
        def _(dve):
            def split_lo(k):
                dve.wait_ge(hi_done, k + 1)
                dve.tensor_tensor(lo[:, k, :], h[k % 2][:], hi[:, k, :].bitcast(F32), ALU.subtract).then_inc(lo_done, 1)

            for g in range(groups):
                dve.wait_ge(sq_used, (g + 1) * per)
                rsqrt_steps(dve, newton, g * RSQRT_STEPS, v[:], r[:], t[:], psum[g % 2][:, 0, 0:CH], 1.0 / (per * P))
                if g >= 1:
                    dve.wait_ge(spread, g)
                dve.tensor_tensor(diag[:], c["ident"][:].unsqueeze(1).to_broadcast([P, CH, P]),
                                  r[:].unsqueeze(2).to_broadcast([P, CH, P]), ALU.mult).then_inc(diag_done, 1)
                dve.wait_ge(spread, g + 1)
                for k in range(g * per, (g + 1) * per):
                    if k >= 2:
                        dve.wait_ge(lo_done, k - 1)
                    dve.scalar_tensor_tensor(out=half(h[k % 2][:]), in0=half(src[:, k, :]), scalar=gain[:, k:k + 1],
                                             in1=psum[2 + g % 2][:], op0=ALU.mult, op1=ALU.mult).then_inc(h_done, 1)
                    if k >= 1:
                        split_lo(k - 1)
            split_lo(KT - 1)


def half2(x, k):
    return x[:, bass.ds(k, 1), :].rearrange("p k (h n) -> p (k h) n", h=NH)


def gla_phase(nc, io, c, first, hi, lo, psum):
    with phase(nc, "gl") as (ctx, sb, sem):
        g = Gemm(c, sb, sem, psum[0:2])
        scan0, masks = sb("scan0", [P, S]), [sb(n, [P, P], U32) for n in ("m_f", "m_b")]
        const_full = sem("const_full")
        X, Y = psum[2], psum[3]
        two = lambda n, shape: [sb(f"{n}{d}", shape) for d in ("f", "b")]
        kk, gs, qh, kh = (two(n, [P, S]) for n in ("k", "gs", "qh", "kh"))
        q, v = sb("q", [P, S]), sb("v", [P, S])
        kt, vt = two("kt", [P, CH, P]), sb("vt", [P, CH, P])
        at = two("at", [P, CH, P])
        m = two("m", [P, P, NCH])
        wb = sb("wrep", [P, P, NCH])
        tot, ws, w = two("tot", [P, 2 * NCH]), two("ws", [P, NCH - 1]), two("w", [P, NCH])
        tick = sb("tick", [P, 2])
        y, sqd, gate, o = sb("y", [P, S]), sb("sqd", [P, CH, P]), [sb(f"gate{b}", [P, S]) for b in range(2)], sb("o", [P, S])
        rv, rr, rt = (sb(n, [P, CH]) for n in ("rv", "rr", "rt"))
        (zeroed, th, lg, kdone, fsum, totd, xdone, wsum, wexp, en, kh_ok, ep, qh_ok, qcopy, vcopy, att, at_ok, kv, kv_ok,
         wbc, m_ok, ymm, ycopy, sqok, tr, trcopy, stat, newton, dg, bc, norm, o_ok, o_stored, gth) = (
            sem(n) for n in ("zeroed", "th", "lg", "kdone", "fsum", "totd", "xdone", "wsum", "wexp", "en", "kh_ok", "ep",
                             "qh_ok", "qcopy", "vcopy", "att", "at_ok", "kv", "kv_ok", "wbc", "m_ok", "ymm", "ycopy",
                             "sqok", "tr", "trcopy", "stat", "newton", "dg", "bc", "norm", "o_ok", "o_stored", "gth"))
        block = ctx.enter_context(nc.Block())
        TURNS = GH // 2

        def turns(eng, turn):
            turn(0, 0, 0, True, False, False)
            turn(1, 0, 1, True, True, False)
            with eng.Fori(1, TURNS) as i:
                for b in range(2):
                    turn(2 * i + b, i, b, True, True, True)
            turn(GH, TURNS, 0, False, True, True)
            turn(GH + 1, TURNS, 1, False, False, True)

        def slot(i, b, j):
            return (5 * b + j) % 2, 5 * i + (5 * b + j) // 2

        blocks = lambda ap: ap.rearrange("p (c a t) -> p c a t", a=2, t=32)
        def kv_sets(d, hf_):
            for par in range(2):
                cs = [cc for cc in range(8 * hf_ + par, 8 * hf_ + 8, 2) if cc != (NCH - 1 if d == 0 else 0)]
                yield par, cs

        KV_OPS = 4

        @block.sync
        def _(sp):
            wt = io["w"]
            for s in range(2):
                sp.dma_start(g.raw[s][:], wt[first + s]).then_inc(g.raw_full[s], 16)
            for dst, n in ((scan0, "scan0"), (masks[0], "m_f"), (masks[1], "m_b")):
                sp.dma_start(dst[:], io[n]).then_inc(const_full, 16)

            def weights(pair, s):
                sp.wait_ge(g.w_ready[s], pair)
                sp.dma_start(g.raw[s][:], wt[2 * pair + (first + s)]).then_inc(g.raw_full[s], 16)

            def turn(n, i, b, cur, prev, prev2):
                if cur:
                    for p_ in ((1, 2, 3) if b == 0 else (4, 5)):
                        if not (isinstance(i, int) and 5 * i + p_ == 5 * TURNS):
                            for s in range(2):
                                weights(5 * i + p_, s)
                if prev2:
                    sp.wait_ge(o_ok, n - 1)
                    sp.dma_start(io["hg_d"][n - 2], o[:]).then_inc(o_stored, 16)

            turn(0, 0, 0, True, False, False)
            turn(1, 0, 1, True, True, False)
            with sp.Fori(1, TURNS - 1) as i:
                for b in range(2):
                    turn(2 * i + b, i, b, True, True, True)
            for b in range(2):
                turn(GH - 2 + b, TURNS - 1, b, True, True, True)
            turn(GH, TURNS, 0, False, True, True)
            turn(GH + 1, TURNS, 1, False, False, True)
            sp.wait_ge(o_stored, 16 * (GH + 1))

        @block.gpsimd
        def _(pool):
            g.split(pool, 5 * TURNS)

        @block.tensor
        def _(pe):
            def turn(n, i, b, cur, prev, prev2):
                def gemm(j):
                    if cur:
                        s, pair = slot(i, b, j)
                        g.tile(pe, pair, s, hi, lo)

                def kv_half(d, hf_, ps, wait_n):
                    for par, cs in kv_sets(d, hf_):
                        rows = slice(64 * par, 64 * par + 64)
                        for cc in cs:
                            jj = (cc // 2) % 4
                            mm = pe.matmul(ps[:, par, jj * P:(jj + 1) * P], kt[d][rows, cc // 2, :], vt[rows, cc // 2, :],
                                           start=True, stop=True)
                    mm.then_inc(kv, 1)

                def transposes(src, ps):
                    for n_ in range(CH):
                        mm = pe.transpose(ps[:, n_ // 4, (n_ % 4) * P:(n_ % 4 + 1) * P], src[:, n_ * P:(n_ + 1) * P],
                                          c["ident"][:])
                    mm.then_inc(tr, 1)

                gemm(0)
                if prev2:
                    pe.wait_ge(sqok, n - 1)
                    pe.wait_ge(trcopy, (n if prev else GH) * 3)
                    for n_ in range(CH):
                        mm = pe.matmul(X[:, 0, n_:n_ + 1], sqd[:, n_, :], c["ones"][:, 0:1], start=(n_ == 0), stop=True,
                                       skip_group_check=True)
                    mm.then_inc(stat, 1)
                if prev:
                    pe.wait_ge(qh_ok, n * 2)
                    pe.wait_ge(kh_ok, n * 2)
                    pe.wait_ge(trcopy, n * 3)
                    if prev2:
                        pe.wait_ge(newton, (n - 2) * RSQRT_STEPS + 1)
                    for d, ps in enumerate((X, Y)):
                        for n_ in range(CH):
                            t_ = slice(n_ * P, (n_ + 1) * P)
                            mm = pe.matmul(ps[:, n_ // 4, (n_ % 4) * P:(n_ % 4 + 1) * P], kh[d][:, t_], qh[d][:, t_],
                                           start=True, stop=True)
                        mm.then_inc(att, 1)
                gemm(1)
                if prev2:
                    pe.wait_ge(dg, n - 1)
                    if prev:
                        pe.wait_ge(at_ok, n * 2)
                    for hh in range(NH):
                        mm = pe.matmul(X[:, hh, :], c["ones"][:], sqd[:, 4 * hh:4 * hh + 4, :], start=True, stop=True)
                    mm.then_inc(bc, 1)
                if prev:
                    pe.wait_ge(at_ok, n * 2)
                    kv_half(0, 1, Y, 0)
                    if prev2:
                        pe.wait_ge(norm, n - 1)
                    kv_half(0, 0, X, 0)
                gemm(2)
                if prev:
                    pe.wait_ge(kv_ok, (n - 1) * (4 * KV_OPS // 2) + 2)
                    kv_half(1, 1, Y, 0)
                    pe.wait_ge(kv_ok, (n - 1) * (4 * KV_OPS // 2) + 4)
                    kv_half(1, 0, X, 0)
                gemm(3)
                if prev:
                    pe.wait_ge(m_ok, n * 2)
                    pe.wait_ge(at_ok, n * 2)
                    pe.wait_ge(kv_ok, n * (4 * KV_OPS // 2))
                    for n_ in range(CH):
                        o_ = lambda a_, w_: X[:, n_ // 4, (n_ % 4) * P + a_:(n_ % 4) * P + a_ + w_]
                        for d in range(2):
                            pe.matmul(o_(0, P), vt[:, n_, :], at[d][:, n_, :], start=(d == 0), stop=(d == 1), skip_group_check=True)
                        parts = [(d, 2 * n_ + a_) for a_ in range(2) for d in range(2)
                                 if (d, 2 * n_ + a_) not in ((0, 0), (1, NCH - 1))]
                        for d, cc in parts:
                            mm = pe.matmul(o_((cc % 2) * GC, GC), m[d][:, :, cc], qh[d][:, cc * GC:(cc + 1) * GC],
                                           start=False, stop=True, skip_group_check=True)
                    mm.then_inc(ymm, 1)
                if cur:
                    pe.wait_ge(kh_ok, 2 * n + 1)
                    if prev:
                        pe.wait_ge(kv_ok, n * (4 * KV_OPS // 2))
                    transposes(kh[0], Y)
                gemm(4)
                if cur:
                    pe.wait_ge(kh_ok, 2 * n + 2)
                    if prev:
                        pe.wait_ge(ycopy, n)
                    transposes(kh[1], X)
                    pe.wait_ge(vcopy, n + 1)
                    pe.wait_ge(trcopy, 3 * n + 1)
                    transposes(v, Y)

            turns(pe, turn)

        @block.scalar
        def _(act):
            for s in range(2):
                act.sem_inc(g.psum_free[s], 1)
            act.wait_ge(zeroed, 6)

            def turn(n, i, b, cur, prev, prev2):
                if cur:
                    hd = bass.ds(n, 1)
                    for j in range(2):
                        s, pair = slot(i, b, j)
                        act.wait_ge(g.tile_done[s], pair + 1)
                        if prev:
                            act.wait_ge(kh_ok, n * 2)
                        act.activation(half(kk[j][:]), psum[s][:], ACT.Tanh, scale=0.5).then_inc(g.psum_free[s], 1)
                        act.wait_ge(g.psum_free[s], pair + 2)
                    if prev:
                        act.wait_ge(ep, n * 2)
                    act.wait_ge(zeroed, 6)
                    for d in range(2):
                        act.activation(gs[d][:], kk[d][:], ACT.Ln, scale=c["oml"][:, hd], bias=c["lnb"][:, hd])\
                           .then_inc(lg, 1)
                    s, pair = slot(i, b, 2)
                    act.wait_ge(g.tile_done[s], pair + 1)
                    if prev:
                        act.wait_ge(qh_ok, n * 2)
                    act.activation(half(q[:]), psum[s][:], ACT.Copy, scale=SCALE).then_inc(g.psum_free[s], 1)
                if prev:
                    if prev2:
                        act.wait_ge(m_ok, (n - 1) * 2)
                    act.activation(wb[:], w[0][:].unsqueeze(1).to_broadcast([P, P, NCH]), ACT.Copy).then_inc(wbc, 1)
                if cur:
                    for d in range(2):
                        act.wait_ge(xdone, 2 * n + d + 1)
                        if prev:
                            act.wait_ge(att, n * 2)
                        act.activation(kh[d][:], gs[d][:], ACT.Exp, scale=-1.0).then_inc(en, 1)
                if prev:
                    act.wait_ge(m_ok, n * 2 - 1)
                    act.activation(wb[:], w[1][:].unsqueeze(1).to_broadcast([P, P, NCH]), ACT.Copy).then_inc(wbc, 1)
                if cur:
                    s, pair = slot(i, b, 3)
                    act.wait_ge(g.tile_done[s], pair + 1)
                    if prev:
                        act.wait_ge(tr, n * 3)
                    act.activation(half(v[:]), psum[s][:], ACT.Copy).then_inc(g.psum_free[s], 1)
                    act.wait_ge(g.psum_free[s], pair + 2)
                    act.activation(v[0:1, 0:1], v[0:1, 0:1], ACT.Copy).then_inc(vcopy, 1)
                    if prev:
                        act.wait_ge(wbc, n * 2)
                        act.wait_ge(kv_ok, n * (4 * KV_OPS // 2))
                    for d in range(2):
                        act.wait_ge(wsum, 2 * n + d + 1)
                        act.activation(w[d][:, 1 - d:NCH - d], ws[d][:], ACT.Exp).then_inc(wexp, 1)
                if prev:
                    act.wait_ge(ymm, n)
                    if prev2:
                        act.wait_ge(norm, (n - 1) * 1)
                        act.wait_ge(o_ok, n - 1)
                    act.activation(half(y[:]), X[:], ACT.Copy).then_inc(ycopy, 1)
                    act.wait_ge(ycopy, n)
                    if prev2:
                        act.wait_ge(bc, n - 1)
                    act.activation(sqd[:].rearrange("p c t -> p (c t)"), y[:], ACT.Square).then_inc(sqok, 1)
                if cur:
                    act.wait_ge(tr, 3 * n + 1)
                    act.activation(kt[0][:].rearrange("p (h c) t -> p h (c t)", h=NH), Y[:], ACT.Copy).then_inc(trcopy, 1)
                    for d in range(2):
                        act.activation(qh[d][:], gs[d][:], ACT.Exp).then_inc(ep, 1)
                    s, pair = slot(i, b, 4)
                    act.wait_ge(g.tile_done[s], pair + 1)
                    if prev2:
                        act.wait_ge(o_ok, n - 1)
                    act.activation(half(gate[b][:]), psum[s][:], ACT.Tanh, scale=0.5).then_inc(gth, 1)
                    for dst, k_, ps in ((kt[1], 2, X), (vt, 3, Y)):
                        act.wait_ge(tr, 3 * n + k_)
                        act.activation(dst[:].rearrange("p (h c) t -> p h (c t)", h=NH), ps[:], ACT.Copy)\
                           .then_inc(trcopy, 1)

            turns(act, turn)

        @block.vector
        def _(dve):
            dve.sem_inc(o_stored, 16)
            for d in range(2):
                dve.memset(at[d][:], 0.0).then_inc(zeroed, 1)
                dve.memset(w[d][:, d * (NCH - 1):d * (NCH - 1) + 1], 0.0).then_inc(zeroed, 1)
                dve.memset(m[d][:, :, d * (NCH - 1):d * (NCH - 1) + 1], 0.0).then_inc(zeroed, 1)
            dve.wait_ge(zeroed, 6)
            dve.wait_ge(const_full, 48)

            def turn(n, i, b, cur, prev, prev2):
                if prev2:
                    dve.wait_ge(stat, n - 1)
                    rsqrt_steps(dve, newton, (n - 2) * RSQRT_STEPS, rv[:], rr[:], rt[:], X[:, 0, 0:CH], 1.0 / P)
                    dve.tensor_tensor(sqd[:], c["ident"][:].unsqueeze(1).to_broadcast([P, CH, P]),
                                      rr[:].unsqueeze(2).to_broadcast([P, CH, P]), ALU.mult).then_inc(dg, 1)
                if prev:
                    for d, (ps, mask) in enumerate(((X, masks[0]), (Y, masks[1]))):
                        dve.wait_ge(att, n * 2 - 1 + d)
                        if prev2:
                            dve.wait_ge(ymm, n - 1)
                        dve.memset(tick[:, d:d + 1], 0.0)
                        dve.copy_predicated(at[d][:], mask[:].unsqueeze(1).to_broadcast([P, CH, P]),
                                            ps[:].rearrange("p h (c t) -> p (h c) t", t=P)).then_inc(at_ok, 1)
                if prev2:
                    dve.wait_ge(bc, n - 1)
                    dve.scalar_tensor_tensor(out=half(y[:]), in0=half(y[:]), scalar=c["hg_gain"][:, bass.ds(n - 2, 1)],
                                             in1=X[:], op0=ALU.mult, op1=ALU.mult).then_inc(norm, 1)
                    dve.wait_ge(norm, n - 1)
                    dve.wait_ge(o_stored, (n - 1) * 16)
                    dve.tensor_tensor(o[:], y[:], gate[b][:], ALU.mult).then_inc(o_ok, 1)

                def kv_read(d, hf_, ps, k_):
                    dve.wait_ge(kv, (n - 1) * 4 + k_)
                    for par, cs in kv_sets(d, hf_):
                        a_, st = cs[0] + (1 if d == 0 else -1), len(cs)
                        sl = slice(a_, a_ + 2 * st - 1, 2)
                        j0 = (cs[0] // 2) % 4
                        dve.tensor_tensor(m[d][:, :, sl].rearrange("p v c -> p c v"),
                                          ps[:, par, j0 * P:(j0 + st) * P].rearrange("p (c v) -> p c v", v=P),
                                          w[d][:, sl].unsqueeze(2).to_broadcast([P, st, P]), ALU.mult).then_inc(kv_ok, 1)

                if prev:
                    dve.wait_ge(wexp, n * 2)
                    if prev2:
                        dve.wait_ge(ymm, n - 1)
                    kv_read(0, 1, Y, 1)
                    kv_read(0, 0, X, 2)

                if cur:
                    hd = bass.ds(n, 1)
                    for d in range(2):
                        dve.wait_ge(lg, 2 * n + d + 1)
                        dve.tensor_scalar(kk[d][:], kk[d][:], c["noml"][:, hd], c["oml"][:, hd], ALU.mult, ALU.add)\
                           .then_inc(kdone, 1)
                        t_ = slice(None) if d == 0 else slice(None, None, -1)
                        dve.tensor_tensor_scan(gs[d][:, t_], scan0[:], gs[d][:, t_], 0.0, ALU.mult, ALU.add)\
                           .then_inc(fsum, 1)
                    for d in range(2):
                        dve.wait_ge(fsum, 2 * n + d + 1)
                        if prev:
                            dve.wait_ge(wsum, n * 2)
                        dve.tensor_copy(tot[d][:], gs[d][:, 31 if d == 0 else 0::32]).then_inc(totd, 1)
                    for d in range(2):
                        dve.wait_ge(totd, 2 * n + d + 1)
                        a_ = d
                        xv = blocks(gs[d][:])[:, :, a_, :]
                        dve.tensor_tensor(xv, xv, tot[d][:, a_::2].unsqueeze(2).to_broadcast([P, NCH, 32]), ALU.subtract)\
                           .then_inc(xdone, 1)
                        if prev:
                            dve.wait_ge(wexp, n * 2)
                        dve.tensor_tensor(ws[d][:], tot[d][:, 1:2 * NCH - 2:2], tot[d][:, 2::2], ALU.add).then_inc(wsum, 1)
                if prev:
                    dve.wait_ge(wbc, n * 2 - 1)
                    dve.wait_ge(kv_ok, (n - 1) * 8 + 4)
                    fl = lambda ap: ap.rearrange("p v c -> p (v c)")
                    dve.tensor_tensor_scan(fl(m[0][:]), fl(wb[:]), fl(m[0][:]), 0.0, ALU.mult, ALU.add).then_inc(m_ok, 1)
                    kv_read(1, 1, Y, 3)
                    kv_read(1, 0, X, 4)
                    dve.wait_ge(wbc, n * 2)
                    dve.wait_ge(kv_ok, n * 8)
                    dve.tensor_tensor_scan(fl(m[1][:])[:, ::-1], fl(wb[:])[:, ::-1], fl(m[1][:])[:, ::-1], 0.0,
                                           ALU.mult, ALU.add).then_inc(m_ok, 1)
                if cur:
                    for d in range(2):
                        dve.wait_ge(en, 2 * n + d + 1)
                        dve.wait_ge(kdone, 2 * n + d + 1)
                        dve.tensor_tensor(kh[d][:], kh[d][:], kk[d][:], ALU.mult).then_inc(kh_ok, 1)
                    s, pair = slot(i, b, 2)
                    dve.wait_ge(g.psum_free[s], pair + 2)
                    for d in range(2):
                        dve.wait_ge(ep, 2 * n + d + 1)
                        dve.tensor_tensor(qh[d][:], qh[d][:], q[:], ALU.mult).then_inc(qh_ok, 1)
                    s, pair = slot(i, b, 4)
                    dve.wait_ge(gth, n + 1)
                    dve.scalar_tensor_tensor(out=half(gate[b][:]), in0=half(gate[b][:]), scalar=1.0, in1=psum[s][:],
                                             op0=ALU.add, op1=ALU.mult).then_inc(g.psum_free[s], 1)

            turns(dve, turn)


class RmsParts:

    def __init__(self, c, sb, sem, diag, sums, spread):
        self.c, self.diag, self.sums, self.spread = c, diag, sums, spread
        self.v, self.r, self.t = (sb(n, [P, CH]) for n in ("rms_v", "rms_r", "rms_t"))
        self.summed, self.newton, self.diag_done, self.spread_done = (
            sem(n) for n in ("summed", "newton", "diag_done", "spread_done"))

    def pe_sums(self, pe, acc):
        for n in range(CH):
            mm = pe.matmul(self.sums[:, 0, n:n + 1], acc[:, n * P:(n + 1) * P], self.c["ones"][:, 0:1],
                           start=(n == 0), stop=True, skip_group_check=True)
        mm.then_inc(self.summed, 1)

    def dve_roots(self, dve):
        dve.wait_ge(self.summed, 1)
        rsqrt_steps(dve, self.newton, 0, self.v[:], self.r[:], self.t[:], self.sums[:, 0, 0:CH], 1.0 / D)
        dve.tensor_tensor(self.diag[:].rearrange("p (c t) -> p c t", c=CH),
                          self.c["ident"][:].unsqueeze(1).to_broadcast([P, CH, P]),
                          self.r[:].unsqueeze(2).to_broadcast([P, CH, P]), ALU.mult).then_inc(self.diag_done, 1)

    def pe_spread(self, pe):
        pe.wait_ge(self.diag_done, 1)
        for hh in range(NH):
            mm = pe.matmul(self.spread[:, hh, :], self.c["ones"][:], self.diag[:, hh * HALF:(hh + 1) * HALF],
                           start=True, stop=True)
        mm.then_inc(self.spread_done, 1)


def scale_phase(nc, c, x, acc, gain, psum, tag, hi=None, lo=None, store=None):
    with phase(nc, tag) as (ctx, sb, sem):
        diag, h = sb("diag", [P, S]), [sb(f"h{b}", [P, S]) for b in range(2)]
        rms = RmsParts(c, sb, sem, diag, psum[0], psum[1])
        h_done, hi_done, lo_done, stored = sem("h_done"), sem("hi_done"), sem("lo_done"), sem("stored")
        block = ctx.enter_context(nc.Block())
        parts = hi is not None

        @block.sync
        def _(sp):
            for k in range(KT):
                if not parts:
                    sp.wait_ge(h_done, k + 1)
                sp.dma_start(store[:, k, :], x[:, k, :]).then_inc(stored, 16)
            sp.wait_ge(stored, 16 * KT)

        @block.tensor
        def _(pe):
            rms.pe_sums(pe, acc)
            rms.pe_spread(pe)

        @block.scalar
        def _(act):
            if parts:
                for k in range(KT):
                    act.wait_ge(h_done, k + 1)
                    act.activation(hi[:, k, :], h[k % 2][:], ACT.Copy).then_inc(hi_done, 1)

        @block.vector
        def _(dve):
            def split_lo(k):
                dve.wait_ge(hi_done, k + 1)
                dve.tensor_tensor(lo[:, k, :], h[k % 2][:], hi[:, k, :].bitcast(F32), ALU.subtract).then_inc(lo_done, 1)

            rms.dve_roots(dve)
            dve.wait_ge(rms.spread_done, 1)
            for k in range(KT):
                if parts and k >= 2:
                    dve.wait_ge(lo_done, k - 1)
                dst = h[k % 2][:] if parts else x[:, k, :]
                dve.scalar_tensor_tensor(out=half(dst), in0=half(x[:, k, :]), scalar=gain[:, k:k + 1],
                                         in1=psum[1][:], op0=ALU.mult, op1=ALU.mult).then_inc(h_done, 1)
                if parts and k >= 1:
                    split_lo(k - 1)
            if parts:
                split_lo(KT - 1)


def tail_phase(nc, io, c, x, acc, x_src, y_src, last, other, halves, first, gain, psum, tag):
    with phase(nc, tag) as (ctx, sb, sem):
        g = Gemm(c, sb, sem, psum[0:2])
        t = [sb(f"t{s}", [P, S]) for s in range(2)]
        sq, rstd = sb("sq", [P, S]), sb("rstd", [P, S])
        rms = RmsParts(c, sb, sem, sq, psum[2], psum[3])
        y_full = [sem(f"y_full{s}") for s in range(2)]
        (x_full, y_hi, y_ready, x_hi, x_ready, sq_done, acc_done, rstd_done, squared, hid_hi, hid_ready) = (
            sem(n) for n in ("x_full", "y_hi", "y_ready", "x_hi", "x_ready", "sq_done", "acc_done", "rstd_done",
                             "squared", "hid_hi", "hid_ready"))
        BL = FF // D
        PR = KT // 2
        BASE = halves * PR
        PAIRS = BASE + BL * 2 * PR
        ya = other if halves == 2 else last
        (y_hi_t, y_lo_t), (n_hi, n_lo), (h_hi, h_lo) = ya, other, last
        block = ctx.enter_context(nc.Block())

        def stage_pairs(eng, body, start=0):
            with eng.Fori(start, PR) as i:
                for s in range(2):
                    body(i, s)

        @block.sync
        def _(sp):
            for s in range(2):
                sp.dma_start(g.raw[s][:], io["w"][first + s]).then_inc(g.raw_full[s], 16)
            for k in range(KT):
                if k >= 2:
                    sp.wait_ge(y_ready, k - 1)
                sp.dma_start(t[k % 2][:], y_src[k]).then_inc(y_full[k % 2], 16)
            with sp.Fori(1, PAIRS) as i:
                for s in range(2):
                    sp.wait_ge(g.w_ready[s], i)
                    sp.dma_start(g.raw[s][:], io["w"][2 * i + (first + s)]).then_inc(g.raw_full[s], 16)

        @block.gpsimd
        def _(pool):
            g.split(pool, PAIRS)

        @block.tensor
        def _(pe):
            g.tile(pe, 0, 0, y_hi_t, y_lo_t, lambda k: pe.wait_ge(y_ready, k + 1))
            g.tile(pe, 0, 1, y_hi_t, y_lo_t)
            stage_pairs(pe, lambda i, s: g.tile(pe, i, s, y_hi_t, y_lo_t), 1)
            if halves == 2:
                stage_pairs(pe, lambda i, s: g.tile(pe, i + PR, s, h_hi, h_lo))

            def spread(k):
                if k == PR:
                    rms.pe_spread(pe)

            def stage2(b, i, s):
                wait = (lambda k: pe.wait_ge(hid_ready, b * KT + (k + 1))) if s == 0 else None
                g.tile(pe, b * (2 * PR) + (i + (BASE + PR)), s, h_hi, h_lo, wait)

            g.tile(pe, BASE, 0, n_hi, n_lo, lambda k: pe.wait_ge(x_ready, k + 1))
            pe.wait_ge(acc_done, KT + 1)
            rms.pe_sums(pe, acc)
            g.tile(pe, BASE, 1, n_hi, n_lo, spread)
            stage_pairs(pe, lambda i, s: g.tile(pe, i + BASE, s, n_hi, n_lo), 1)
            stage_pairs(pe, lambda i, s: stage2(0, i, s))
            with pe.Fori(1, BL) as b:
                stage_pairs(pe, lambda i, s: g.tile(pe, b * (2 * PR) + (i + BASE), s, n_hi, n_lo))
                stage_pairs(pe, lambda i, s: stage2(b, i, s))

        @block.scalar
        def _(act):
            for k in range(KT):
                act.dma_start(x[:, k, :], x_src[:, k, :]).then_inc(x_full, 16)
            for k in range(KT):
                act.wait_ge(y_full[k % 2], 16 * (k // 2 + 1))
                act.activation(y_hi_t[:, k, :], t[k % 2][:], ACT.Copy).then_inc(y_hi, 1)

            def square(i, s):
                act.activation(sq[:], at(x, 2 * i + s), ACT.Square).then_inc(sq_done, 1)

            def last_half(i, s):
                act.wait_ge(g.psum_free[s], i + (BASE - PR + 2))
                act.wait_ge(acc_done, 2 * i + (s + 1))
                act.activation(at(n_hi, 2 * i + s), at(x, 2 * i + s), ACT.Copy, scale=gain[:, bass.ds(2 * i + s, 1)])\
                   .then_inc(x_hi, 1)
                square(i, s)

            def hidden(b, i, s):
                n = b * KT + (2 * i + (s + 1))
                act.wait_ge(g.psum_free[s], b * (2 * PR) + (i + (BASE + 2)))
                act.activation(t[s][:], t[s][:], ACT.Square).then_inc(squared, 1)
                act.wait_ge(squared, n)
                act.activation(at(h_hi, 2 * i + s), t[s][:], ACT.Copy).then_inc(hid_hi, 1)

            stage_pairs(act, last_half)
            act.wait_ge(rms.spread_done, 1)
            act.activation(half(rstd[:]), psum[3][:], ACT.Copy).then_inc(rstd_done, 1)
            with act.Fori(0, BL) as b:
                stage_pairs(act, lambda i, s: hidden(b, i, s))

            def last_sums(i, s):
                act.wait_ge(g.psum_free[s], i + (PAIRS - PR + 2))
                act.wait_ge(acc_done, 2 * i + (s + (KT + 2)))
                square(i, s)

            stage_pairs(act, last_sums)

        @block.vector
        def _(dve):
            for s in range(2):
                dve.sem_inc(g.psum_free[s], 1)
            dve.memset(acc[:], 0.0).then_inc(acc_done, 1)
            for k in range(KT):
                dve.wait_ge(y_hi, k + 1)
                dve.tensor_tensor(y_lo_t[:, k, :], t[k % 2][:], y_hi_t[:, k, :].bitcast(F32), ALU.subtract)\
                   .then_inc(y_ready, 1)
            dve.wait_ge(y_ready, KT)
            dve.wait_ge(x_full, 16 * KT)

            def add(pair, i, s):
                dve.wait_ge(g.tile_done[s], pair + 1)
                dve.tensor_tensor(half2(x, 2 * i + s), psum[s][:], half2(x, 2 * i + s), ALU.add)\
                   .then_inc(g.psum_free[s], 1)

            def add_square(i, s, squares, sums):
                dve.wait_ge(sq_done, 2 * i + (s + 1 + squares))
                dve.wait_ge(acc_done, 2 * i + (s + sums))
                dve.tensor_tensor(acc[:], acc[:], sq[:], ALU.add).then_inc(acc_done, 1)

            def last_half(i, s):
                add(i + (BASE - PR), i, s)
                dve.wait_ge(x_hi, 2 * i + (s + 1))
                dve.scalar_tensor_tensor(out=at(n_lo, 2 * i + s), in0=at(x, 2 * i + s),
                                         scalar=gain[:, bass.ds(2 * i + s, 1)], in1=at(n_hi, 2 * i + s).bitcast(F32),
                                         op0=ALU.mult, op1=ALU.subtract).then_inc(x_ready, 1)
                add_square(i, s, 0, 1)

            def hidden(b, i, s):
                n = b * KT + (2 * i + (s + 1))
                dve.wait_ge(g.tile_done[s], b * (2 * PR) + (i + (BASE + 1)))
                dve.scalar_tensor_tensor(out=half(t[s][:]), in0=psum[s][:], scalar=0.0, in1=half(rstd[:]),
                                         op0=ALU.max, op1=ALU.mult).then_inc(g.psum_free[s], 1)
                dve.wait_ge(hid_hi, n)
                dve.tensor_tensor(at(h_lo, 2 * i + s), t[s][:], at(h_hi, 2 * i + s).bitcast(F32), ALU.subtract)\
                   .then_inc(hid_ready, 1)
                dve.wait_ge(hid_ready, n)

            if halves == 2:
                stage_pairs(dve, lambda i, s: add(i, i, s))
            stage_pairs(dve, last_half)
            dve.wait_ge(acc_done, KT + 1)
            rms.dve_roots(dve)
            dve.memset(acc[:], 0.0).then_inc(acc_done, 1)
            dve.wait_ge(rstd_done, 1)

            def stage2(b, i, s):
                add(b * (2 * PR) + (i + (BASE + PR)), i, s)

            with dve.Fori(0, BL - 1) as b:
                stage_pairs(dve, lambda i, s: hidden(b, i, s))
                stage_pairs(dve, lambda i, s: stage2(b, i, s))
            stage_pairs(dve, lambda i, s: hidden(BL - 1, i, s))

            def last_sums(i, s):
                stage2(BL - 1, i, s)
                add_square(i, s, KT, KT + 2)

            stage_pairs(dve, last_sums)


def at(t, k):
    return t[:, bass.ds(k, 1), :].rearrange("p k n -> p (k n)")

W_EVEN_OUT = 2 * (PAIRS_LRU + PAIRS_XZ + PAIRS_BC) + 1
W_MLP0 = W_EVEN_OUT + 2 * KT
W_ODD_IN = W_MLP0 + 2 * FF // P
W_ODD_OUT = W_ODD_IN + 5 * GH
W_MLP1 = W_ODD_OUT + KT

CONST = dict(
    gains=[P, 5, KT], conv_w=[P, 24, 4], conv_b=[P, 24], gate_b=[P, KT, 4], dt_bias=[2 * HEADS, 1], ssd_norm=[P, KT],
    hgrn_norm=[P, KT], d_skip=[P, HEADS], ones=[P, P], ident=[P, P],
    a_exp=[P, 2 * HEADS], lb_e=[P, KT], lb_d=[P, KT], lru_rate=[P, 2, KT], lru_rate2=[P, 2, KT], lru_rate_n=[P, 2, KT],
    gate_bh=[P, KT, 4], oml=[P, KT], noml=[P, KT], lnb=[P, KT], hg_gain=[P, KT], zero=[P, 1])
TRIANGLES = ("m_ui", "m_us", "m_li", "m_ls")

SCRATCH = dict(yb_d=[KT, P, S], hg_d=[KT, P, S], z_d=[KT, P, S], xs_d=[CH, P, D], b_d=[G, P, S], c_d=[G, P, S],
               bt_d=[CH, P, G * N_ST], x_d=[P, KT, S])


def encoder(nc, io):
    with ExitStack() as ctx:
        psum = [ctx.enter_context(nc.psum_tensor(f"ps{b}", [P, NH, HALF], F32)) for b in range(4)]
        io = dict(io, **{n: nc.dram_tensor(n, shape, F32).ap() for n, shape in SCRATCH.items()})
        keep = lambda stack, n, shape, dt=F32, **side: stack.enter_context(nc.sbuf_tensor(n, shape, dt, **side))
        pair = lambda stack, n: tuple(keep(stack, f"{n}_{part}", [P, KT, S], F32R) for part in ("hi", "lo"))
        c = {n: keep(ctx, f"c_{n}", shape) for n, shape in CONST.items()}
        gain = lambda n: c["gains"][:, n, :]

        with ExitStack() as at_right:
            with ExitStack() as ssd:
                c.update({n: keep(ssd, f"c_{n}", [P, P]) for n in TRIANGLES})
                dt_t = keep(ssd, "dt_t", [2 * HEADS, S])
                co = {n: keep(ssd, f"co_{n}", [P, CH, 2 * HEADS]) for n in ("dt", "da", "w", "e", "tot", "cw")}
                setup_phase(nc, io, c)
                with ExitStack() as proj:
                    h = pair(proj, "h0")
                    with nc.sbuf_tensor("x0", [P, KT, S], F32) as x:
                        norm_phase(nc, c, x, 1, gain(0), *h, psum, "na", load=io["xT"])
                    lru_phase(nc, io, c, *h, psum)
                    conv_phase(nc, io, c, *h, psum, dt_t)
                ssd_coef_phase(nc, c, dt_t, co, psum)
                with nc.sbuf_tensor("hb", [P, CH, D], F32) as hb:
                    u = keep(at_right, "u", [P, KT, S], side="right")
                    ssd_back_states_phase(nc, io, co, hb, psum)
                    ssd_phase(nc, io, c, co, hb, u, psum)
            h = pair(ctx, "h")
            even = ExitStack()
            y = pair(even, "y0")
            norm_phase(nc, c, u, G, c["ssd_norm"], *y, psum, "nu")
        with even:
            x, acc = keep(even, "x1", [P, KT, S]), keep(even, "acc1", [P, S])
            tail_phase(nc, io, c, x, acc, io["xT"], io["yb_d"], y, h, 2, W_EVEN_OUT, gain(1), psum, "te")
            scale_phase(nc, c, x, acc, gain(2), psum, "nc", *h, store=io["x_d"])

        gla_phase(nc, io, c, W_ODD_IN, *h, psum)
        with ExitStack() as odd:
            y = pair(odd, "y1")
            x, acc = keep(odd, "x2", [P, KT, S]), keep(odd, "acc2", [P, S])
            tail_phase(nc, io, c, x, acc, io["x_d"], io["hg_d"], y, h, 1, W_ODD_OUT, gain(3), psum, "to")
            scale_phase(nc, c, x, acc, gain(4), psum, "ne", store=io["out"])


def tiles(w):
    K, N = w.shape
    return w.reshape(K // 1024, 8, P, N // P, P).transpose(0, 3, 2, 1, 4).reshape(K // 1024, N // P, P, 1024)
def cols(v):
    v = v.reshape(*v.shape[:-1], v.shape[-1] // P, P)
    return np.moveaxis(v, -1, 0)
def mlp(w1, w2):
    a = tiles(w1)[0].reshape(4, 8, P, 1024)
    return np.concatenate([a, tiles(w2)], axis=1).reshape(64, P, 1024)
def layout(x, even_w_in, even_conv_w, even_conv_b, ssd_a_log, ssd_dt_bias, ssd_d,
              ssd_norm_w, lru_w_a, lru_b_a, lru_w_x, lru_b_x, lru_lambda, even_w_out,
              odd_w_in, hgrn_lb_logits, hgrn_norm_w, odd_w_out, norm_mix, norm_mlp,
              mlp_w1, mlp_w2, norm_final):
    f = np.float32
    e = tiles(even_w_in[0][:, :5120])[0]
    x_, b_, c_, u_, z_, g_ = e[0:8], e[8:12], e[12:16], e[16:24], e[24:32], e[32:40]
    pair = lambda a, b: np.stack([a, b], 1).reshape(-1, P, 1024)
    dtw = tiles(np.concatenate([even_w_in[0][:, 5120:], np.zeros((1024, 96), f)], 1))[0]
    eo = tiles(even_w_out[0])
    o = tiles(odd_w_in[0])[0].reshape(5, 8, P, 1024)
    o = o[[1, 2, 0, 3, 4]].transpose(1, 0, 2, 3).reshape(40, P, 1024)
    w = np.concatenate([pair(u_, g_), pair(x_, z_), pair(b_, c_), dtw, eo[1], eo[0], mlp(mlp_w1[0], mlp_w2[0]),
                        o, tiles(odd_w_out[0])[0], mlp(mlp_w1[1], mlp_w2[1])])
    cw = even_conv_w[0].reshape(4, 24, P); cb = even_conv_b[0].reshape(24, P)
    order = list(range(16, 24)) + list(range(8)) + [n for i in range(4) for n in (8 + i, 12 + i)]
    gw = np.zeros((8, P, 2, 2, P), f)
    for r, m in enumerate((lru_w_a[0], lru_w_x[0])):
        for hb in range(2):
            q = slice(64 * hb, 64 * hb + 64)
            gw[:, q, :, r, q] = m[:, hb::2].transpose(1, 2, 0, 3)
    gb = np.stack([lru_b_a[0], lru_b_x[0]], 1).reshape(4, 8, P).transpose(2, 1, 0)
    i = np.arange(P)
    s, t = i[:, None], i[None, :]
    same = s // 64 == t // 64
    A = lambda a: np.ascontiguousarray(a)
    return dict(
        xT=A(x[0].T.reshape(8, P, 1024).transpose(1, 0, 2)), w=A(w), gate_w=A(gw.reshape(8, P, 4 * P)),
        conv_w=A(cw[:, order].transpose(2, 1, 0)), conv_b=A(cb[order].T), gate_b=A(gb),
        gains=A(cols(np.stack([norm_mix[0], norm_mlp[0], norm_mix[1], norm_mlp[1], norm_final]))),
        dt_bias=A(ssd_dt_bias[0].reshape(32, 1)), a_log=A(ssd_a_log[0].reshape(1, 32)), d_skip=A(ssd_d[0].reshape(1, 16)),
        ssd_norm=A(cols(ssd_norm_w[0])), hgrn_norm=A(cols(hgrn_norm_w[0])), lam=A(cols(lru_lambda[0])),
        lb_logits=A(cols(hgrn_lb_logits)),
        ones=np.ones((P, P), f), ident=np.eye(P, dtype=f),
        m_ui=(s <= t).astype(f), m_us=(s < t).astype(f), m_li=(s >= t).astype(f), m_ls=(s > t).astype(f),
        m_f=A((same & (s <= t)).astype(np.uint32)), m_b=A((same & (s >= t)).astype(np.uint32)),
        scan0=A(np.tile((np.arange(1024) % 32 != 0).astype(f), (P, 1))),
    )


def kernel(**inputs):
    import concourse.bacc as bacc
    from concourse.bass_utils import run_bass_kernel_spmd

    arrays = layout(**{name: np.asarray(value) for name, value in inputs.items()})
    nc = bacc.Bacc("TRN2", target_bir_lowering=False, num_devices=1)
    io = {name: nc.dram_tensor(f"in_{name}", a.shape, mybir.dt.from_np(a.dtype), kind="ExternalInput").ap()
          for name, a in arrays.items()}
    io["out"] = nc.dram_tensor("out_y", [P, KT, S], F32, kind="ExternalOutput").ap()
    encoder(nc, io)
    r = run_bass_kernel_spmd(nc, [{f"in_{name}": a for name, a in arrays.items()}], core_ids=[0])
    return np.ascontiguousarray(r.results[0]["out_y"].transpose(2, 1, 0).reshape(1, S, D))
```

```python
import numpy as np
from contextlib import ExitStack, contextmanager
import concourse.bass as bass
from concourse import mybir

F32 = mybir.dt.float32
U32 = mybir.dt.uint32
F32R = mybir.dt.float32r
I32 = mybir.dt.int32
ACT = mybir.ActivationFunctionType
ALU = mybir.AluOpType

P = 128
S = 1024
D = 1024
KT = D // P
HALF = 512
NH = S // HALF
CH = S // P
EPS = 1e-6
MAGIC = float(0x5F3759DF)
FF = 4 * D


def half(ap):
    return ap.rearrange("p (h n) -> p h n", h=NH)


@contextmanager
def phase(nc, tag):
    sems = []
    with ExitStack() as ctx:
        def sb(name, shape, dt=F32):
            return ctx.enter_context(nc.sbuf_tensor(f"{tag}_{name}", shape, dt))

        def sem(name):
            sems.append(nc.alloc_semaphore(f"{tag}_{name}"))
            return sems[-1]

        yield ctx, sb, sem
    nc.clear_and_free_semaphores(sems)
    nc.all_engine_barrier(sem_only=True)


class Gemm:

    def __init__(self, c, sb, sem, psum, w, pairs):
        self.raw = [sb(f"w_raw{s}", [P, KT * P], F32) for s in range(2)]
        self.hi = [sb(f"w_hi{s}", [P, KT, P], F32R) for s in range(2)]
        self.lo = [sb(f"w_lo{s}", [P, KT, P], F32R) for s in range(2)]
        self.w, self.pairs = w, pairs
        self.psum = psum
        self.zero = c["zero"]
        self.raw_full = [sem(f"w_raw_full{s}") for s in range(2)]
        self.hi_done = sem("w_hi_done")
        self.w_ready = [sem(f"w_ready{s}") for s in range(2)]
        self.tile_done = [sem(f"tile_done{s}") for s in range(2)]
        self.psum_free = [sem(f"psum_free{s}") for s in range(2)]

    def load_pair(self, sp, i, wait=True):
        for s in range(2):
            if wait:
                sp.wait_ge(self.w_ready[s], i)
            sp.dma_start(self.raw[s][:], self.w[2 * i + s]).then_inc(self.raw_full[s], 16)

    def load(self, sp, first, end):
        with sp.Fori(first + 1, min(end + 1, self.pairs)) as i:
            self.load_pair(sp, i)

    def split_pair(self, pool, i, wait=True):
        for s in range(2):
            if wait:
                pool.wait_ge(self.tile_done[s], i)
            hi = self.hi[s][:].rearrange("p k n -> p (k n)")
            lo = self.lo[s][:].rearrange("p k n -> p (k n)")
            pool.wait_ge(self.raw_full[s], (i + 1) * 16)
            pool.tensor_tensor(hi, self.raw[s][:], self.zero[:, 0:1].to_broadcast([P, KT * P]), ALU.add)\
                .then_inc(self.hi_done, 1)
            pool.wait_ge(self.hi_done, 2 * i + (s + 1))
            pool.tensor_tensor(lo, self.raw[s][:], hi.bitcast(F32), ALU.subtract).then_inc(self.w_ready[s], 1)

    def split(self, pool, first, end):
        with pool.Fori(first + 1, min(end + 1, self.pairs)) as i:
            self.split_pair(pool, i)

    def tile(self, pe, i, s, act_hi, act_lo, before_k=None):
        pe.wait_ge(self.w_ready[s], i + 1)
        pe.wait_ge(self.psum_free[s], i + 1)
        for k in range(KT):
            if before_k is not None:
                before_k(k)
            for part, (w, a) in enumerate(((self.hi, act_hi), (self.hi, act_lo), (self.lo, act_hi))):
                for h in range(NH):
                    mm = pe.matmul(self.psum[s][:, h, :], w[s][:, k, :], a[:, k, h * HALF:(h + 1) * HALF],
                                   start=(k == 0 and part == 0), stop=(k == KT - 1 and part == 2))
        mm.then_inc(self.tile_done[s], 1)


def rsqrt_steps(dve, done, n, v, r, t, src, inv_n):
    def step(ins):
        nonlocal n
        n = n + 1
        ins.then_inc(done, 1)
        dve.wait_ge(done, n)

    step(dve.tensor_scalar(v, src, inv_n, EPS, ALU.mult, ALU.add))
    step(dve.tensor_scalar(t.bitcast(I32), v.bitcast(I32), 1, None, ALU.arith_shift_right))
    step(dve.tensor_scalar(r.bitcast(I32), t.bitcast(I32), -1.0, MAGIC, ALU.mult, ALU.add))
    for _ in range(4):
        step(dve.tensor_tensor(t, r, r, ALU.mult))
        step(dve.scalar_tensor_tensor(out=t, in0=t, scalar=-0.5, in1=v, op0=ALU.mult, op1=ALU.mult))
        step(dve.scalar_tensor_tensor(out=r, in0=t, scalar=1.5, in1=r, op0=ALU.add, op1=ALU.mult))
    return n


RSQRT_STEPS = 15


class RmsParts:

    def __init__(self, c, sb, sem, diag, sums, spread):
        self.c, self.diag, self.sums, self.spread = c, diag, sums, spread
        self.v, self.r, self.t = (sb(n, [P, CH]) for n in ("rms_v", "rms_r", "rms_t"))
        self.summed, self.newton, self.diag_done, self.spread_done = (
            sem(n) for n in ("summed", "rms_newton", "rms_diag", "spread_done"))

    def pe_sums(self, pe, acc):
        for n in range(CH):
            mm = pe.matmul(self.sums[:, 0, n:n + 1], acc[:, n * P:(n + 1) * P], self.c["ones"][:, 0:1],
                           start=(n == 0), stop=True, skip_group_check=True)
        mm.then_inc(self.summed, 1)

    def dve_roots(self, dve):
        dve.wait_ge(self.summed, 1)
        rsqrt_steps(dve, self.newton, 0, self.v[:], self.r[:], self.t[:], self.sums[:, 0, 0:CH], 1.0 / D)
        dve.tensor_tensor(self.diag.rearrange("p (c t) -> p c t", c=CH),
                          self.c["ident"][:].unsqueeze(1).to_broadcast([P, CH, P]),
                          self.r[:].unsqueeze(2).to_broadcast([P, CH, P]), ALU.mult).then_inc(self.diag_done, 1)

    def pe_spread(self, pe):
        pe.wait_ge(self.diag_done, 1)
        for hh in range(NH):
            mm = pe.matmul(self.spread[:, hh, :], self.c["ones"][:], self.diag[:, hh * HALF:(hh + 1) * HALF],
                           start=True, stop=True)
        mm.then_inc(self.spread_done, 1)


G, N_ST, HEADS, HD = 4, 128, 16, 64


def setup_phase(nc, io, c, g, x, hi, lo, acc):
    with phase(nc, "su") as (ctx, sb, sem):
        lam = sb("lam", [P, 2, KT])
        loaded, zeroed, a_done, v_done = sem("loaded"), sem("zeroed"), sem("act"), sem("dve")
        logit = sb("logit", [P, 2, KT])
        alog = sb("alog", [P, 32])
        tmp = [sb(f"tmp{j}", [P, 2 * KT]) for j in range(3)]
        gain, sq = c["gains"][:, 0, :], [sb(f"sq{b}", [P, S]) for b in range(2)]
        x_full = [sem(f"x{k}") for k in range(KT)]
        gains_full, hi_done, lo_done, sq_done, acc_done = (
            sem(n) for n in ("gains_full", "hi_done", "lo_done", "sq_done", "acc_done"))
        block = ctx.enter_context(nc.Block())
        loads = [(c[n][:], io[n]) for n in ("conv_w", "conv_b", "dt_bias", "ssd_norm", "hgrn_norm", "ones",
                                            "ident", "m_ui", "m_us", "m_li", "m_ls", "gate_b")]
        loads += [(c["d_skip"][:], io["d_skip"].to_broadcast([P, HEADS])), (alog[:], io["a_log"].to_broadcast([P, 32])),
                  (lam[:], io["lam"]), (logit[:], io["lb_logits"])]
        one = 16 * len(loads)

        @block.sync
        def _(sp):
            sp.dma_start(c["gains"][:], io["gains"]).then_inc(gains_full, 16)
            for k in range(KT):
                sp.dma_start(x[:, k, :], io["xT"][:, k, :]).then_inc(x_full[k], 16)
            g.load_pair(sp, 0, wait=False)
            for dst, src in loads:
                sp.dma_start(dst, src).then_inc(loaded, 16)
            sp.wait_ge(loaded, one)

        lam2 = lam[:].rearrange("p d k -> p (d k)")
        hs = c["lru_rate"][:].rearrange("p d k -> p (d k)")
        chain = Softplus(lam2, tmp, hs, -1.0)

        @block.scalar
        def _(act):
            act.wait_ge(gains_full, 16)
            for k in range(KT):
                act.wait_ge(x_full[k], 16)
                act.activation(hi[:, k, :], x[:, k, :], ACT.Copy, scale=gain[:, k:k + 1]).then_inc(hi_done, 1)
                if k >= 2:
                    act.wait_ge(acc_done, k)
                act.activation(sq[k % 2][:], x[:, k, :], ACT.Square).then_inc(sq_done, 1)
            act.wait_ge(loaded, one)
            chain.act(act, a_done)
            act.activation(c["a_exp"][:], alog[:], ACT.Exp).then_inc(a_done, 1)
            act.wait_ge(v_done, 1)
            act.activation(c["lb_e"][:], c["lb_d"][:], ACT.Tanh, scale=0.5).then_inc(a_done, 1)

        @block.gpsimd
        def _(pool):
            pool.wait_ge(zeroed, 1)
            g.split_pair(pool, 0, wait=False)

        @block.vector
        def _(dve):
            for s in range(2):
                dve.sem_inc(g.psum_free[s], 1)
            dve.memset(c["zero"][:], 0.0).then_inc(zeroed, 1)
            dve.memset(acc[:], 0.0).then_inc(acc_done, 1)
            for k in range(KT):
                dve.wait_ge(hi_done, k + 1)
                dve.scalar_tensor_tensor(out=lo[:, k, :], in0=x[:, k, :], scalar=gain[:, k:k + 1],
                                         in1=hi[:, k, :].bitcast(F32), op0=ALU.mult, op1=ALU.subtract)\
                   .then_inc(lo_done, 1)
                dve.wait_ge(sq_done, k + 1)
                dve.wait_ge(acc_done, k + 1)
                dve.tensor_tensor(acc[:], acc[:], sq[k % 2][:], ALU.add).then_inc(acc_done, 1)
            dve.wait_ge(loaded, one)
            dve.tensor_tensor(c["lb_d"][:], logit[:, 0, :], logit[:, 1, :], ALU.subtract).then_inc(v_done, 1)
            n = chain.dve(dve, a_done, v_done, 2, 1)
            dve.wait_ge(v_done, n)
            dve.tensor_scalar(hs, hs, -4.0, None, ALU.mult).then_inc(v_done, 1)
            dve.wait_ge(v_done, n + 1)
            dve.tensor_scalar(c["lru_rate2"][:].rearrange("p d k -> p (d k)"), hs, 2.0, None, ALU.mult)
            dve.tensor_scalar(c["lru_rate_n"][:].rearrange("p d k -> p (d k)"), hs, -1.0, None, ALU.mult)
            dve.tensor_scalar(c["gate_bh"][:], c["gate_b"][:], 0.5, None, ALU.mult)
            dve.wait_ge(a_done, 4)
            dve.tensor_scalar(c["oml"][:], c["lb_e"][:], 0.25, 0.25, ALU.mult, ALU.add)
            dve.tensor_scalar(c["noml"][:], c["lb_e"][:], -0.25, -0.25, ALU.mult, ALU.add)
            dve.tensor_scalar(c["lnb"][:], c["lb_e"][:], -0.25, 0.75, ALU.mult, ALU.add)
            dve.tensor_scalar(c["hg_gain"][:], c["hgrn_norm"][:], 0.5, None, ALU.mult)


class Softplus:

    def __init__(self, z, tmp, out, sign):
        self.z, self.tmp, self.out, self.sign = z, tmp, out, sign

    def act(self, act, a_done, base=0):
        act.activation(self.tmp[0][:], self.z, ACT.Abs).then_inc(a_done, 1)
        act.wait_ge(a_done, base + 1)
        act.activation(self.tmp[0][:], self.tmp[0][:], ACT.Exp, scale=-1.0).then_inc(a_done, 1)

    def dve(self, dve, a_done, v_done, a_count, n):
        e, s, q = (t[:] for t in self.tmp)
        dve.wait_ge(a_done, a_count)

        def step(ins):
            nonlocal n
            n += 1
            ins.then_inc(v_done, 1)
            dve.wait_ge(v_done, n)

        step(dve.tensor_scalar(s, e, 2.0, None, ALU.add))
        step(dve.reciprocal(s, s))
        step(dve.tensor_tensor(s, e, s, ALU.mult))
        step(dve.tensor_tensor(q, s, s, ALU.mult))
        step(dve.tensor_scalar(e, q, 1.0 / 17, None, ALU.mult))
        for d in (15, 13, 11, 9, 7, 5, 3):
            step(dve.scalar_tensor_tensor(out=e, in0=e, scalar=1.0 / d, in1=q, op0=ALU.add, op1=ALU.mult))
        step(dve.scalar_tensor_tensor(out=e, in0=e, scalar=1.0, in1=s, op0=ALU.add, op1=ALU.mult))
        step(dve.tensor_scalar(s, self.z, self.sign, 0.0, ALU.mult, ALU.max))
        step(dve.scalar_tensor_tensor(out=self.out, in0=e, scalar=2.0, in1=s, op0=ALU.mult, op1=ALU.add))
        return n


PAIRS_LRU, PAIRS_XZ, PAIRS_BC = 8, 8, 4
PAIRS_IN = PAIRS_LRU + PAIRS_XZ + PAIRS_BC + 1


def lru_phase(nc, io, c, g, hi, lo, acc, rstd, psum):
    with phase(nc, "lr") as (ctx, sb, sem):
        up, u = sb("up", [P, S + 4]), [sb(f"u{b}", [P, S]) for b in range(2)]
        ta, tx, a, a2, th, h = ([sb(f"{n}{d}", [P, S]) for d in range(2)] for n in ("ta", "tx", "a", "a2", "th", "h"))
        gg, yb = sb("gg", [P, S]), sb("yb", [P, S])
        gw = sb("gw", [P, 4, P])
        rms, rstd_done, gelu = RmsParts(c, sb, sem, yb[:], psum[2], psum[3]), sem("rstd_done"), sem("gelu")
        pads, tap0, taps, gw_full, gate, gate_read = (
            sem(n) for n in ("pads", "tap0", "taps", "gw_full", "gate", "gate_read"))
        decay, q_done, root, step, y_done, y_stored = (
            sem(n) for n in ("decay", "q_done", "root", "step", "y_done", "y_stored"))
        block = ctx.enter_context(nc.Block())

        def tiles(eng, conv, rest):
            conv(0, 0, 0, 0)
            conv(1, 1, 1, 0)
            with eng.Fori(0, KT // 2 - 1) as j:
                for b in range(2):
                    i = 2 * j + b
                    rest(i, b, 0, i + 1)
                    conv(i + 2, b, 1, i + 1)
            rest(KT - 2, 0, 0, KT - 1)
            rest(KT - 1, 1, 1, KT - 1)

        @block.sync
        def _(sp):
            def rest(i, b, s, pair):
                if not (isinstance(i, int) and i == KT - 1):
                    g.load_pair(sp, pair)
                else:
                    g.load_pair(sp, KT)
                sp.wait_ge(gate, i * 4 + 4)
                if not (isinstance(i, int) and i == KT - 1):
                    sp.dma_start(gw[:], io["gate_w"][i + 1]).then_inc(gw_full, 16)
                sp.wait_ge(y_done, i + 2)
                sp.dma_start(io["yb_d"][i], yb[:]).then_inc(y_stored, 16)

            sp.dma_start(gw[:], io["gate_w"][0]).then_inc(gw_full, 16)
            tiles(sp, lambda *_: None, rest)
            sp.wait_ge(y_stored, 16 * (KT + 1))

        @block.gpsimd
        def _(pool):
            g.split(pool, 0, PAIRS_LRU)

        @block.tensor
        def _(pe):
            def conv(i, b, s, pair):
                if isinstance(i, int) and i == 0:
                    rms.pe_sums(pe, acc)
                g.tile(pe, pair, s, hi, lo)
                if isinstance(i, int) and i == 0:
                    rms.pe_spread(pe)
                if isinstance(i, int) and i == 1:
                    pe.wait_ge(rstd_done, 1)

            def rest(i, b, s, pair):
                pe.wait_ge(gw_full, i * 16 + 16)
                pe.wait_ge(taps, i * 3 + 3)
                for d in range(2):
                    for r in range(2):
                        pe.wait_ge(gate_read, i * 4 + (2 * d + r + 1))
                        for hh in range(NH):
                            mm = pe.matmul(psum[2 + r][:, hh, :], gw[:, 2 * d + r, :],
                                           u[b][:, hh * HALF:(hh + 1) * HALF], start=True, stop=True)
                        mm.then_inc(gate, 1)
                g.tile(pe, pair, s, hi, lo)

            tiles(pe, conv, rest)

        @block.scalar
        def _(act):
            act.sem_inc(gate_read, 2)
            act.wait_ge(pads, 2)

            act.wait_ge(rms.spread_done, 1)
            act.activation(half(rstd[:]), psum[3][:], ACT.Copy).then_inc(rstd_done, 1)

            def conv(i, b, s, pair):
                act.wait_ge(g.psum_free[s], pair + 2)
                if not (isinstance(i, int) and i < 2):
                    act.wait_ge(step, i * 7 - 10)
                act.activation(u[b][:], up[:, 0:S], ACT.Identity, scale=c["conv_w"][:, bass.ds(i, 1), 0],
                               bias=c["conv_b"][:, bass.ds(i, 1)]).then_inc(tap0, 1)

            def rest(i, b, s, pair):
                act.wait_ge(y_done, i + 1)
                for d in range(2):
                    for r, out in enumerate((ta, tx)):
                        act.wait_ge(gate, i * 4 + (2 * d + r + 1))
                        act.activation(half(out[d][:]), psum[2 + r][:], ACT.Tanh, scale=0.5,
                                       bias=c["gate_bh"][:, bass.ds(i, 1), 2 * d + r]).then_inc(gate_read, 1)
                for d in range(2):
                    act.wait_ge(gate_read, i * 4 + (2 * d + 4))
                    for out, rate, func in ((a, "lru_rate", ACT.Exp), (a2, "lru_rate2", ACT.Exp),
                                            (th, "lru_rate_n", ACT.Tanh)):
                        r_ = c[rate][:, d, bass.ds(i, 1)]
                        act.activation(out[d][:], ta[d][:], func, scale=r_, bias=r_).then_inc(decay, 1)
                for d in range(2):
                    act.wait_ge(q_done, i * 2 + (d + 1))
                    act.activation(th[d][:], th[d][:], ACT.Sqrt).then_inc(root, 1)
                act.wait_ge(g.psum_free[s], pair + 2)
                act.activation(gg[:], gg[:], ACT.Gelu_apprx_tanh).then_inc(gelu, 1)

            tiles(act, conv, rest)

        @block.vector
        def _(dve):
            dve.sem_inc(y_done, 1)
            dve.sem_inc(y_stored, 16)
            dve.memset(up[:, 0:1], 0.0).then_inc(pads, 1)
            dve.memset(up[:, S + 1:S + 4], 0.0).then_inc(pads, 1)
            dve.wait_ge(pads, 2)
            rms.dve_roots(dve)
            dve.wait_ge(rstd_done, 1)

            def take(out, s, pair):
                dve.wait_ge(g.tile_done[s], pair + 1)
                dve.tensor_tensor(half(out), psum[s][:], half(rstd[:]), ALU.mult).then_inc(g.psum_free[s], 1)

            def conv(i, b, s, pair):
                if not (isinstance(i, int) and i == 0):
                    dve.wait_ge(taps, i * 3)
                take(up[:, 1:1 + S], s, pair)
                dve.wait_ge(tap0, i + 1)
                for k in range(1, 4):
                    if k > 1:
                        dve.wait_ge(taps, i * 3 + (k - 1))
                    dve.scalar_tensor_tensor(out=u[b][:], in0=up[:, k:k + S], scalar=c["conv_w"][:, bass.ds(i, 1), k],
                                             in1=u[b][:], op0=ALU.mult, op1=ALU.add).then_inc(taps, 1)

            def rest(i, b, s, pair):
                for d in range(2):
                    dve.wait_ge(decay, i * 6 + (3 * d + 3))
                    dve.scalar_tensor_tensor(out=th[d][:], in0=a2[d][:], scalar=1.0, in1=th[d][:],
                                             op0=ALU.add, op1=ALU.mult).then_inc(q_done, 1)
                    dve.scalar_tensor_tensor(out=tx[d][:], in0=tx[d][:], scalar=1.0, in1=u[b][:],
                                             op0=ALU.add, op1=ALU.mult).then_inc(step, 1)
                dve.wait_ge(y_done, i + 1)
                take(gg[:], s, pair)
                for d in range(2):
                    dve.wait_ge(root, i * 2 + (d + 1))
                    dve.wait_ge(step, i * 7 + (d + 2 if d == 0 else 4))
                    dve.scalar_tensor_tensor(out=tx[d][:], in0=th[d][:], scalar=0.5, in1=tx[d][:],
                                             op0=ALU.mult, op1=ALU.mult).then_inc(step, 1)
                    dve.wait_ge(step, i * 7 + (2 * d + 3))
                    t = slice(None) if d == 0 else slice(None, None, -1)
                    dve.tensor_tensor_scan(h[d][:, t], a[d][:, t], tx[d][:, t], 0.0, ALU.mult, ALU.add)\
                       .then_inc(step, 1)
                dve.wait_ge(step, i * 7 + 6)
                dve.tensor_tensor(h[0][:], h[0][:], h[1][:], ALU.add).then_inc(step, 1)
                dve.wait_ge(step, i * 7 + 7)
                dve.wait_ge(gelu, i + 1)
                dve.wait_ge(y_stored, i * 16 + 16)
                dve.tensor_tensor(yb[:], h[0][:], gg[:], ALU.mult).then_inc(y_done, 1)

            tiles(dve, conv, rest)


def conv_phase(nc, io, c, g, hi, lo, rstd, psum, dt_t):
    with phase(nc, "cv") as (ctx, sb, sem):
        up, acc, sc = ([sb(f"{n}{s}", [P, S + 4 if n == "up" else S]) for s in range(2)] for n in ("up", "acc", "sc"))
        tok = sb("tok", [P, S])
        pads, tr, tok_done, tok_stored, z_done = (sem(n) for n in ("pads", "tr", "tok_done", "tok_stored", "z_done"))
        tap0, taps, silu, cm_stored = ([sem(f"{n}{s}") for s in range(2)]
                                       for n in ("tap0", "taps", "silu", "cm_stored"))
        block = ctx.enter_context(nc.Block())
        XZ, BC, BASE = PAIRS_XZ, PAIRS_BC, PAIRS_LRU
        tok3 = tok[:].rearrange("p (c n) -> p c n", c=CH)
        xs_v = io["xs_d"].rearrange("c p (i n) -> i p c n", n=P)
        bt_v = io["bt_d"].rearrange("c p (i n) -> i p c n", n=P)

        @block.sync
        def _(sp):
            with sp.Fori(0, XZ) as n:
                g.load_pair(sp, n + (BASE + 1))
                sp.wait_ge(z_done, n + 1)
                sp.dma_start(io["z_d"][n], sc[1][:]).then_inc(cm_stored[1], 16)
                sp.wait_ge(tok_done, n + 2)
                sp.dma_start(xs_v[n], tok3).then_inc(tok_stored, 16)

            def store_bc(i):
                sp.wait_ge(silu[0], i + (XZ + 2))
                sp.dma_start(io["b_d"][i], sc[0][:]).then_inc(cm_stored[0], 16)
                sp.wait_ge(tok_done, i + (XZ + 2))
                sp.dma_start(bt_v[i], tok3).then_inc(tok_stored, 16)
                sp.wait_ge(silu[1], i + 2)
                sp.dma_start(io["c_d"][i], sc[1][:]).then_inc(cm_stored[1], 16)

            with sp.Fori(0, BC - 1) as i:
                g.load_pair(sp, i + (BASE + XZ + 1))
                store_bc(i)
            g.load_pair(sp, BASE + XZ + BC)
            store_bc(BC - 1)
            g.load_pair(sp, BASE + XZ + BC + 1)
            sp.wait_ge(cm_stored[0], 16 * (BC + 1))
            sp.wait_ge(cm_stored[1], 16 * (XZ + BC + 1))
            sp.wait_ge(tok_stored, 16 * (XZ + BC + 1))

        @block.gpsimd
        def _(pool):
            g.split(pool, BASE, PAIRS_IN)

        @block.tensor
        def _(pe):
            pe.sem_inc(tr, 1)
            with pe.Fori(0, XZ + BC) as n:
                g.tile(pe, n + BASE, 0, hi, lo)
                g.tile(pe, n + BASE, 1, hi, lo)
                pe.wait_ge(silu[0], n + 2)
                pe.wait_ge(tok_done, n + 1)
                for cc in range(CH):
                    mm = pe.transpose(psum[2][:, cc // 4, (cc % 4) * P:(cc % 4 + 1) * P],
                                      sc[0][:, cc * P:(cc + 1) * P], c["ident"][:])
                mm.then_inc(tr, 1)
            g.tile(pe, BASE + XZ + BC, 0, hi, lo)
            pe.wait_ge(g.w_ready[1], PAIRS_IN)
            pe.wait_ge(g.psum_free[1], PAIRS_IN)
            pe.sem_inc(g.tile_done[1], 1)
            pe.sem_inc(g.psum_free[1], 1)

        def conv_head(act, s, n, m, idx):
            act.wait_ge(g.psum_free[s], n + (BASE + 2))
            act.wait_ge(silu[s], m + 1)
            act.activation(acc[s][:], up[s][:, 0:S], ACT.Identity, scale=c["conv_w"][:, bass.ds(idx, 1), 0],
                           bias=c["conv_b"][:, bass.ds(idx, 1)]).then_inc(tap0[s], 1)

        def take(dve, out, s, n):
            dve.wait_ge(g.tile_done[s], n + (BASE + 1))
            dve.tensor_tensor(half(out), psum[s][:], half(rstd[:]), ALU.mult).then_inc(g.psum_free[s], 1)

        def conv_taps(dve, s, n, m, idx):
            dve.wait_ge(taps[s], m * 3 + 1)
            take(dve, up[s][:, 1:1 + S], s, n)
            dve.wait_ge(tap0[s], m + 1)
            for k in range(1, 4):
                if k > 1:
                    dve.wait_ge(taps[s], m * 3 + k)
                dve.scalar_tensor_tensor(out=acc[s][:], in0=up[s][:, k:k + S],
                                         scalar=c["conv_w"][:, bass.ds(idx, 1), k], in1=acc[s][:],
                                         op0=ALU.mult, op1=ALU.add).then_inc(taps[s], 1)

        @block.scalar
        def _(act):
            for s in range(2):
                act.sem_inc(silu[s], 1)
            act.wait_ge(pads, 4)
            with act.Fori(0, XZ) as n:
                conv_head(act, 0, n, n, n + PAIRS_LRU)
                act.wait_ge(taps[0], n * 3 + 4)
                act.wait_ge(tr, n + 1)
                act.activation(sc[0][:], acc[0][:], ACT.Silu).then_inc(silu[0], 1)
                act.wait_ge(g.psum_free[1], n + (BASE + 2))
                act.activation(sc[1][:], sc[1][:], ACT.Silu).then_inc(z_done, 1)
            with act.Fori(0, BC) as i:
                n = i + XZ
                conv_head(act, 0, n, n, 2 * i + (PAIRS_LRU + XZ))
                act.wait_ge(taps[0], n * 3 + 4)
                act.wait_ge(tr, n + 1)
                act.wait_ge(cm_stored[0], i * 16 + 16)
                act.activation(sc[0][:], acc[0][:], ACT.Silu).then_inc(silu[0], 1)
                conv_head(act, 1, n, i, 2 * i + (PAIRS_LRU + XZ + 1))
                act.wait_ge(taps[1], i * 3 + 4)
                act.wait_ge(cm_stored[1], n * 16 + 16)
                act.activation(sc[1][:], acc[1][:], ACT.Silu).then_inc(silu[1], 1)
            act.wait_ge(g.psum_free[0], PAIRS_IN + 1)
            act.activation(dt_t[:], dt_t[:], ACT.Identity, bias=c["dt_bias"][:, 0:1])

        @block.vector
        def _(dve):
            for s in range(2):
                dve.sem_inc(taps[s], 1)
                dve.sem_inc(cm_stored[s], 16)
                dve.memset(up[s][:, 0:1], 0.0).then_inc(pads, 1)
                dve.memset(up[s][:, S + 1:S + 4], 0.0).then_inc(pads, 1)
            dve.sem_inc(tok_done, 1)
            dve.sem_inc(tok_stored, 16)
            dve.wait_ge(pads, 4)

            def by_tokens(n):
                dve.wait_ge(tr, n + 2)
                dve.wait_ge(tok_stored, n * 16 + 16)
                dve.tensor_copy(half(tok[:]), psum[2][:]).then_inc(tok_done, 1)

            with dve.Fori(0, XZ) as n:
                conv_taps(dve, 0, n, n, n + PAIRS_LRU)
                dve.wait_ge(cm_stored[1], n * 16 + 16)
                take(dve, sc[1][:], 1, n)
                by_tokens(n)
            with dve.Fori(0, BC) as i:
                conv_taps(dve, 0, i + XZ, i + XZ, 2 * i + (PAIRS_LRU + XZ))
                by_tokens(i + XZ)
                conv_taps(dve, 1, i + XZ, i, 2 * i + (PAIRS_LRU + XZ + 1))
            dve.wait_ge(g.tile_done[0], PAIRS_IN)
            dve.tensor_tensor(half(dt_t[:]), psum[0][0:2 * HEADS], half(rstd[0:2 * HEADS, :]), ALU.mult)\
               .then_inc(g.psum_free[0], 1)


HH = HEADS // 2
CW = HH * HD


def ssd_coef_phase(nc, c, dt_t, co, psum, preload):
    with phase(nc, "cf") as (ctx, sb, sem):
        W = CH * 2 * HEADS
        z, tmp, da = sb("z", [P, W]), [sb(f"tmp{j}", [P, W]) for j in range(3)], co["da"]
        tr, a_done, v_done, da_done, sums, exps = (sem(n) for n in ("tr", "act", "dve", "da_done", "sums", "exps"))
        flat = lambda t: t[:].rearrange("p c h -> p (c h)")
        softplus = Softplus(z[:], tmp, flat(co["dt"]), 1.0)
        block = ctx.enter_context(nc.Block())

        @block.sync
        def _(sp):
            preload(sp)

        @block.tensor
        def _(pe):
            for n in range(CH):
                mm = pe.transpose(psum[0][:, 0, n * 32:n * 32 + 32], dt_t[:, n * P:(n + 1) * P], c["ident"][0:32, 0:32])
            mm.then_inc(tr, 1)
            pe.wait_ge(da_done, 1)
            f, b = da[:, :, 0:HEADS], da[:, :, HEADS:2 * HEADS]
            w = psum[1][:, 0, 0:W].rearrange("p (c h) -> p c h", c=CH)
            e = psum[1][:, 1, 0:W].rearrange("p (c h) -> p c h", c=CH)
            for out, mask, rhs in ((w[:, :, 0:HEADS], "m_ls", f), (w[:, :, HEADS:], "m_us", b),
                                   (e[:, :, 0:HEADS], "m_ui", f), (e[:, :, HEADS:], "m_li", b),
                                   (psum[2][:, 0, 0:W].rearrange("p (c h) -> p c h", c=CH), "ones", da[:])):
                mm = pe.matmul(out, c[mask][:], rhs, start=True, stop=True)
            mm.then_inc(sums, 1)

        @block.scalar
        def _(act):
            act.wait_ge(tr, 1)
            act.activation(z[:], psum[0][:, 0, 0:W], ACT.Copy).then_inc(a_done, 1)
            act.wait_ge(a_done, 1)
            softplus.act(act, a_done, 1)
            act.wait_ge(sums, 1)
            for out, src in (("w", psum[1][:, 0, 0:W]), ("e", psum[1][:, 1, 0:W]), ("tot", psum[2][:, 0, 0:W])):
                act.activation(flat(co[out]), src, ACT.Exp).then_inc(exps, 1)

        @block.vector
        def _(dve):
            softplus.dve(dve, a_done, v_done, 3, 0)
            dve.scalar_tensor_tensor(out=da[:], in0=co["dt"][:], scalar=-1.0,
                                     in1=c["a_exp"][:].unsqueeze(1).to_broadcast([P, CH, 2 * HEADS]),
                                     op0=ALU.mult, op1=ALU.mult).then_inc(da_done, 1)
            dve.wait_ge(exps, 3)
            dve.tensor_tensor(co["cw"][:], co["dt"][:], co["w"][:], ALU.mult)


def ssd_back_states_phase(nc, io, c, dt_t, co, hb, psum):
    with phase(nc, "bs") as (ctx, sb, sem):
        bt, xs = ([sb(f"{n}{q}", [P, w]) for q in range(4)] for n, w in (("bt", G * N_ST), ("xs", D)))
        xw = [sb(f"xw{q}", [P, D]) for q in range(2)]
        full = [sem(f"full{q}") for q in range(4)]
        xw_done, s_done, decayed, h_done = sem("xw_done"), sem("s_done"), sem("decayed"), sem("h_done")
        LAST, SLOTS = CH - 1, 4

        def load(sp, j):
            sp.dma_start(bt[j % SLOTS][:], io["bt_d"][LAST - j]).then_inc(full[j % SLOTS], 16)
            sp.dma_start(xs[j % SLOTS][:], io["xs_d"][LAST - j]).then_inc(full[j % SLOTS], 16)

        ssd_coef_phase(nc, c, dt_t, co, psum, lambda sp: [load(sp, j) for j in range(SLOTS)])
        block = ctx.enter_context(nc.Block())

        def steps(eng, step):
            for j in range(LAST):
                step(j, j % 2, j // 2)

        @block.sync
        def _(sp):
            for j in range(SLOTS, LAST):
                sp.wait_ge(s_done, j - 3)
                load(sp, j)

        @block.gpsimd
        def _(pool):
            def step(j, q, i):
                pool.wait_ge(full[j % SLOTS], j // SLOTS * 32 + 32)
                if j >= 2:
                    pool.wait_ge(s_done, j - 1)
                pool.tensor_tensor(xw[q][:].rearrange("p (h d) -> p h d", h=HEADS),
                                   xs[j % SLOTS][:].rearrange("p (h d) -> p h d", h=HEADS),
                                   co["cw"][:, LAST - j, HEADS:].unsqueeze(2)
                                   .to_broadcast([P, HEADS, HD]), ALU.mult).then_inc(xw_done, 1)

            steps(pool, step)

        @block.tensor
        def _(pe):
            def step(j, q, i):
                pe.wait_ge(xw_done, j + 1)
                pe.wait_ge(h_done, j + 1)
                for gg in range(G):
                    mm = pe.matmul(psum[q][:, gg // 2, (gg % 2) * 256:(gg % 2) * 256 + 256],
                                   bt[j % SLOTS][:, gg * N_ST:(gg + 1) * N_ST], xw[q][:, gg * 256:(gg + 1) * 256],
                                   start=True, stop=True)
                mm.then_inc(s_done, 1)

            steps(pe, step)

        @block.vector
        def _(dve):
            dve.memset(hb[:, LAST, :], 0.0).then_inc(h_done, 2)

            def step(j, q, i):
                cc = LAST - j
                tot = co["tot"][:, cc, HEADS:].unsqueeze(2).to_broadcast([P, HEADS, HD])
                new = hb[:, cc - 1, :]
                dve.wait_ge(h_done, j + 2)
                dve.tensor_tensor(new.rearrange("p (h d) -> p h d", h=HEADS),
                                  hb[:, cc, :].rearrange("p (h d) -> p h d", h=HEADS), tot, ALU.mult)\
                   .then_inc(decayed, 1)
                dve.wait_ge(decayed, j + 1)
                dve.wait_ge(s_done, j + 1)
                dve.tensor_tensor(half(new), psum[q][:], half(new), ALU.add).then_inc(h_done, 1)

            steps(dve, step)


def ssd_phase(nc, io, c, co, hb, u, psum):
    with phase(nc, "sd") as (ctx, sb, sem):
        two = lambda n, shape: [sb(f"{n}{s}", shape) for s in range(2)]
        bc, cc_, z = ([sb(f"{n}{q}", shape) for q in range(4)] for n, shape in
                      (("b", [P, 2, P]), ("c", [P, 2, P]), ("z", [P, 4, P])))
        bt, xs = [sb(f"bt{q}", [P, 2 * N_ST]) for q in range(4)], [sb(f"xs{q}", [P, CW]) for q in range(4)]
        xf, xb, xw, dx, y, y2 = (two(n, [P, CW]) for n in ("xf", "xb", "xw", "dx", "y", "y2"))
        rf, rb, ex, gu, gl = (two(n, [P, HH, P]) for n in ("rf", "rb", "ex", "gu", "gl"))
        cu, cl = two("cu", [P, 2, P]), two("cl", [P, 2, P])
        hf = sb("hf", [P, 2, CW])
        full = [sem(f"full{q}") for q in range(4)]
        (rf_ok, rb_ok, xsc, dx_ok, seg, cbt, exp_ok, cul, gu_ok, gl_ok, back, hf_ok, y_ok, tr, u_ok) = (
            [sem(f"{n}{s}") for s in range(2)] for n in
            ("rf_ok", "rb_ok", "xsc", "dx_ok", "seg", "cbt", "exp_ok", "cul", "gu_ok", "gl_ok", "back", "hf_ok",
             "y_ok", "tr", "u_ok"))
        dstep = sem("dstep")
        block = ctx.enter_context(nc.Block())
        TURNS = CH // 2

        def unit(i, m, ahead):
            return (i + (m + ahead) // 4, (m + ahead) % 4) if (m + ahead) // 4 else (i, m + ahead)

        def pipeline(eng, early, front, third, back_):
            def step(i, m, left=None):
                if left is None or left >= 2:
                    early(*unit(i, m, 2))
                if left is None or left >= 1:
                    front(*unit(i, m, 1))
                if not (isinstance(i, int) and i == 0 and m == 0):
                    third(*unit(i, m, -1))
                back_(i, m)

            early(0, 0)
            early(0, 1)
            front(0, 0)
            for m in range(4):
                step(0, m)
            with eng.Fori(1, TURNS - 1) as i:
                for m in range(4):
                    step(i, m)
            for m in range(4):
                step(TURNS - 1, m, left=3 - m)
            third(TURNS - 1, 3)

        none = lambda i, m: None
        heads = lambda ap: ap.rearrange("p (h d) -> p h d", h=HH)

        def coef(name, d, i, m):
            at = d * HEADS + (m % 2) * HH
            return co[name][:, bass.ds(2 * i + m // 2, 1), at:at + HH].rearrange("p c h -> p (c h)").unsqueeze(2)

        @block.sync
        def _(sp):
            def load(i, m):
                h, c_ = m % 2, 2 * i + m // 2
                t = bass.ds(c_ * P, P)
                for dst, src in ((bc[m][:], io["b_d"][2 * h:2 * h + 2, :, t].rearrange("g p t -> p g t")),
                                 (cc_[m][:], io["c_d"][2 * h:2 * h + 2, :, t].rearrange("g p t -> p g t")),
                                 (xs[m][:], io["xs_d"][c_][:, h * CW:(h + 1) * CW]),
                                 (bt[m][:], io["bt_d"][c_][:, h * 256:(h + 1) * 256]),
                                 (z[m][:], io["z_d"][4 * h:4 * h + 4, :, t].rearrange("k p t -> p k t"))):
                    sp.dma_start(dst, src).then_inc(full[m], 16)

            for m in range(4):
                load(0, m)
            with sp.Fori(1, TURNS) as i:
                for m in range(4):
                    sp.wait_ge(u_ok[m % 2], 2 * i + m // 2)
                    load(i, m)

        @block.gpsimd
        def _(pool):
            def early(i, m):
                h, c_ = m % 2, 2 * i + m // 2
                pool.wait_ge(seg[h], c_ + 1)
                pool.tensor_tensor(rb[h][:], c["m_li"][:].unsqueeze(1).to_broadcast([P, HH, P]),
                                   coef("da", 1, i, m).to_broadcast([P, HH, P]), ALU.mult).then_inc(rb_ok[h], 1)

            def front(i, m):
                h, c_ = m % 2, 2 * i + m // 2
                pool.wait_ge(full[m], i * 80 + 80)
                pool.wait_ge(back[h], c_ + 1)
                for dst, name, d in ((xf, "dt", 0), (xb, "dt", 1), (xw, "cw", 0)):
                    pool.tensor_tensor(heads(dst[h][:]), heads(xs[m][:]), coef(name, d, i, m).to_broadcast([P, HH, HD]),
                                       ALU.mult).then_inc(xsc[h], 1)
                pool.wait_ge(y_ok[h], c_ + 1)
                pool.tensor_tensor(heads(dx[h][:]), heads(xs[m][:]), c["d_skip"][:, h * HH:(h + 1) * HH].unsqueeze(2)
                                   .to_broadcast([P, HH, HD]), ALU.mult).then_inc(dx_ok[h], 1)
                pool.wait_ge(exp_ok[h], c_ + 2)
                pool.wait_ge(cul[h], c_ * 2 + 4)
                pool.tensor_tensor(gl[h][:].rearrange("p (g h) t -> p g h t", g=2),
                                   ex[h][:].rearrange("p (g h) t -> p g h t", g=2),
                                   cl[h][:].unsqueeze(2).to_broadcast([P, 2, 4, P]), ALU.mult).then_inc(gl_ok[h], 1)

            pipeline(pool, early, front, none, none)

        @block.tensor
        def _(pe):
            for s in range(2):
                pe.sem_inc(back[s], 1)
                pe.sem_inc(tr[s], 1)
                pe.sem_inc(seg[s], 1)

            def front(i, m):
                h, c_ = m % 2, 2 * i + m // 2
                pe.wait_ge(rf_ok[h], c_ + 1)
                pe.wait_ge(rb_ok[h], c_ + 1)
                pe.wait_ge(exp_ok[1 - h], c_ + (1 + h))
                for gg in range(2):
                    for mask, r, start in (("m_ls", rf, True), ("m_us", rb, False)):
                        mm = pe.matmul(psum[0][:, gg, :], c[mask][:], r[h][:, 4 * gg:4 * gg + 4, :],
                                       start=start, stop=not start)
                mm.then_inc(seg[h], 1)
                pe.wait_ge(full[m], i * 80 + 80)
                pe.wait_ge(cul[1 - h], c_ * 2 + (2 + 2 * h))
                for gg in range(2):
                    mm = pe.matmul(psum[1][:, 0, gg * P:(gg + 1) * P], bc[m][:, gg, :], cc_[m][:, gg, :],
                                   start=True, stop=True)
                mm.then_inc(cbt[h], 1)

            def third(i, m):
                h, c_ = m % 2, 2 * i + m // 2
                pe.wait_ge(y_ok[h], c_ + 2)
                pe.wait_ge(u_ok[1 - h], c_ + (1 + h))
                for j in range(4):
                    mm = pe.transpose(psum[3][:, 1, j * P:(j + 1) * P], y[h][:, j * P:(j + 1) * P], c["ident"][:])
                mm.then_inc(tr[h], 1)

            def back_(i, m):
                h, c_ = m % 2, 2 * i + m // 2
                pe.wait_ge(gu_ok[h], c_ + 1)
                pe.wait_ge(gl_ok[h], c_ + 1)
                pe.wait_ge(xsc[h], c_ * 3 + 3)
                pe.wait_ge(y_ok[1 - h], c_ + (1 + h))
                pe.wait_ge(hf_ok[1 - h], c_ + (1 + h))
                pe.wait_ge(hf_ok[h], c_ + 1)
                for hd in range(HH):
                    o = psum[1][:, 1, hd * HD:(hd + 1) * HD]
                    pe.matmul(o, gu[h][:, hd, :], xf[h][:, hd * HD:(hd + 1) * HD], start=True, stop=False)
                    pe.matmul(o, gl[h][:, hd, :], xb[h][:, hd * HD:(hd + 1) * HD], start=False, stop=True)
                for gg in range(2):
                    q = slice(gg * 256, (gg + 1) * 256)
                    pe.matmul(psum[2][:, 0, q], cc_[m][:, gg, :], hf[:, h, q], start=True, stop=True)
                    pe.matmul(psum[2][:, 1, q], cc_[m][:, gg, :],
                              hb[:, bass.ds(c_, 1), h * CW + gg * 256:h * CW + gg * 256 + 256]
                              .rearrange("p c n -> p (c n)"), start=True, stop=True)
                    mm = pe.matmul(psum[3][:, 0, q], bt[m][:, gg * N_ST:(gg + 1) * N_ST], xw[h][:, q],
                                   start=True, stop=True)
                mm.then_inc(back[h], 1)

            pipeline(pe, none, front, third, back_)

        @block.scalar
        def _(act):
            for s in range(2):
                act.sem_inc(exp_ok[s], 1)

            def front(i, m):
                h, c_ = m % 2, 2 * i + m // 2
                act.wait_ge(seg[h], c_ + 2)
                act.wait_ge(back[h], c_ + 1)
                act.activation(ex[h][:].rearrange("p (g h) t -> p g (h t)", g=2), psum[0][:], ACT.Exp)\
                   .then_inc(exp_ok[h], 1)

            pipeline(act, none, front, none, none)

        @block.vector
        def _(dve):
            for s in range(2):
                dve.sem_inc(cul[s], 2)
                dve.sem_inc(y_ok[s], 1)
                dve.sem_inc(u_ok[s], 1)
                dve.memset(hf[:, s, :], 0.0).then_inc(hf_ok[s], 1)

            def early(i, m):
                h, c_ = m % 2, 2 * i + m // 2
                dve.wait_ge(seg[h], c_ + 1)
                dve.tensor_tensor(rf[h][:], c["m_ui"][:].unsqueeze(1).to_broadcast([P, HH, P]),
                                  coef("da", 0, i, m).to_broadcast([P, HH, P]), ALU.mult).then_inc(rf_ok[h], 1)

            def products(i, m):
                h, c_ = m % 2, 2 * i + m // 2
                dve.wait_ge(back[h], c_ + 1)
                dve.wait_ge(cbt[h], c_ + 1)
                for dst, mask in ((cu, "m_ui"), (cl, "m_li")):
                    dve.tensor_tensor(dst[h][:], psum[1][:, 0, 0:2 * P].rearrange("p (g t) -> p g t", g=2),
                                      c[mask][:].unsqueeze(1).to_broadcast([P, 2, P]), ALU.mult).then_inc(cul[h], 1)
                dve.wait_ge(exp_ok[h], c_ + 2)
                dve.wait_ge(cul[h], c_ * 2 + 4)
                dve.tensor_tensor(gu[h][:].rearrange("p (g h) t -> p g h t", g=2),
                                  ex[h][:].rearrange("p (g h) t -> p g h t", g=2),
                                  cu[h][:].unsqueeze(2).to_broadcast([P, 2, 4, P]), ALU.mult).then_inc(gu_ok[h], 1)

            def third(i, m):
                h, c_ = m % 2, 2 * i + m // 2
                dve.wait_ge(tr[h], c_ + 2)
                dve.tensor_tensor(u[:, 4 * h:4 * h + 4, bass.ds(c_ * P, P)],
                                  psum[3][:, 1, :].rearrange("p (k t) -> p k t", k=4), z[m][:], ALU.mult)\
                   .then_inc(u_ok[h], 1)

            def back_(i, m):
                h, c_, n = m % 2, 2 * i + m // 2, i * 20 + 5 * m
                dve.wait_ge(back[h], c_ + 2)
                dve.wait_ge(tr[h], c_ + 1)
                dve.tensor_tensor(heads(y[h][:]), heads(psum[2][:, 0, :]), coef("e", 0, i, m).to_broadcast([P, HH, HD]),
                                  ALU.mult).then_inc(dstep, 1)
                dve.tensor_tensor(heads(y2[h][:]), heads(psum[2][:, 1, :]), coef("e", 1, i, m)
                                  .to_broadcast([P, HH, HD]), ALU.mult).then_inc(dstep, 1)
                dve.tensor_tensor(heads(hf[:, h, :]), heads(hf[:, h, :]), coef("tot", 0, i, m)
                                  .to_broadcast([P, HH, HD]), ALU.mult).then_inc(dstep, 1)
                dve.wait_ge(dstep, n + 2)
                dve.tensor_tensor(y[h][:], y[h][:], y2[h][:], ALU.add).then_inc(dstep, 1)
                dve.wait_ge(dstep, n + 3)
                dve.tensor_tensor(hf[:, h, :], psum[3][:, 0, :], hf[:, h, :], ALU.add).then_inc(hf_ok[h], 1)
                dve.wait_ge(dstep, n + 4)
                dve.tensor_tensor(y[h][:], psum[1][:, 1, :], y[h][:], ALU.add).then_inc(dstep, 1)
                dve.wait_ge(dx_ok[h], c_ + 1)
                dve.wait_ge(dstep, n + 5)
                dve.tensor_tensor(y[h][:], y[h][:], dx[h][:], ALU.add).then_inc(y_ok[h], 1)

            def step(i, m, left=None):
                if not (isinstance(i, int) and i == 0 and m == 0):
                    third(*unit(i, m, -1))
                if left is None or left >= 1:
                    products(*unit(i, m, 1))
                if left is None or left >= 2:
                    early(*unit(i, m, 2))
                back_(i, m)

            early(0, 0)
            early(0, 1)
            products(0, 0)
            for m in range(4):
                step(0, m)
            with dve.Fori(1, TURNS - 1) as i:
                for m in range(4):
                    step(i, m)
            for m in range(4):
                step(TURNS - 1, m, left=3 - m)
            third(TURNS - 1, 3)


GH = 8
GC = 64
NCH = S // GC
SCALE = float(P) ** -0.5


def norm_phase(nc, c, src, groups, gain, hi, lo, psum, tag):
    per = KT // groups
    with phase(nc, tag) as (ctx, sb, sem):
        h = [sb(f"h{b}", [P, S]) for b in range(4)]
        diag = sb("diag", [P, CH, P])
        v, r, t = (sb(n, [P, groups, CH]) for n in ("v", "r", "t"))
        sq_done, added, sq_used, newton, diag_done, spread, h_done, hi_done = (
            sem(n) for n in ("sq_done", "added", "sq_used", "newton", "diag_done", "spread", "h_done", "hi_done"))
        lo_done = [sem(f"lo_done{b}") for b in range(2)]
        block = ctx.enter_context(nc.Block())
        flat = lambda ap: ap.rearrange("p g n -> p (g n)")
        is_last = lambda k: k % per == per - 1
        adds = lambda k: sum(j % per > 0 for j in range(k + 1))

        def split_lo(eng, k):
            eng.wait_ge(hi_done, k + 1)
            eng.tensor_tensor(lo[:, k, :], h[k % 4][:], hi[:, k, :].bitcast(F32), ALU.subtract)\
               .then_inc(lo_done[k % 2], 1)

        @block.scalar
        def _(act):
            for k in range(KT):
                if k >= 4:
                    if is_last(k - 4):
                        act.wait_ge(sq_used, (k - 4) // per + 1)
                    else:
                        act.wait_ge(added, adds(k - 3))
                act.activation(h[k % 4][:], src[:, k, :], ACT.Square).then_inc(sq_done, 1)
            for k in range(KT):
                act.wait_ge(h_done, k + 1)
                act.activation(hi[:, k, :], h[k % 4][:], ACT.Copy).then_inc(hi_done, 1)

        @block.gpsimd
        def _(pool):
            for k in range(1, KT, 2):
                split_lo(pool, k)

        @block.tensor
        def _(pe):
            for g in range(groups):
                k = (g + 1) * per - 1
                pe.wait_ge(added, adds(k))
                for n in range(CH):
                    pos = g * CH + n
                    mm = pe.matmul(psum[0][:, 0, pos:pos + 1], h[k % 4][:, n * P:(n + 1) * P], c["ones"][:, 0:1],
                                   start=(g == 0 and n == 0), stop=True, skip_group_check=True)
                mm.then_inc(sq_used, 1)
            for g in range(groups):
                pe.wait_ge(diag_done, g + 1)
                for hh in range(NH):
                    mm = pe.matmul(psum[2 + g % 2][:, hh, :], c["ones"][:],
                                   diag[:, 4 * hh:4 * hh + 4, :], start=True, stop=True)
                mm.then_inc(spread, 1)

        @block.vector
        def _(dve):
            def spread_group(g):
                dve.tensor_tensor(diag[:], c["ident"][:].unsqueeze(1).to_broadcast([P, CH, P]),
                                  r[:, g, :].unsqueeze(2).to_broadcast([P, CH, P]), ALU.mult).then_inc(diag_done, 1)

            for k in range(KT):
                if k % per > 0:
                    dve.wait_ge(sq_done, k + 1)
                    if k % per > 1:
                        dve.wait_ge(added, adds(k) - 1)
                    dve.tensor_tensor(h[k % 4][:], h[(k - 1) % 4][:], h[k % 4][:], ALU.add).then_inc(added, 1)
            dve.wait_ge(sq_used, groups)
            rsqrt_steps(dve, newton, 0, flat(v[:]), flat(r[:]), flat(t[:]), psum[0][:, 0, 0:groups * CH],
                        1.0 / (per * P))
            spread_group(0)
            for k in range(KT):
                g = k // per
                if k % per == 0:
                    dve.wait_ge(spread, g + 1)
                    if g + 1 < groups:
                        spread_group(g + 1)
                if k >= 4:
                    dve.wait_ge(lo_done[k % 2], (k - 4) // 2 + 1)
                dve.scalar_tensor_tensor(out=half(h[k % 4][:]), in0=half(src[:, k, :]), scalar=gain[:, k:k + 1],
                                         in1=psum[2 + g % 2][:], op0=ALU.mult, op1=ALU.mult).then_inc(h_done, 1)
                if k % 2 == 1:
                    split_lo(dve, k - 1)


def half2(x, k):
    return x[:, bass.ds(k, 1), :].rearrange("p k (h n) -> p (k h) n", h=NH)


def gla_phase(nc, io, c, g, first, hi, lo, acc, rstd, psum):
    with phase(nc, "gl") as (ctx, sb, sem):
        scan0, masks = sb("scan0", [P, S]), [sb(n, [P, P], U32) for n in ("m_f", "m_b")]
        const_full = sem("const_full")
        X, Y = psum[2], psum[3]
        two = lambda n, shape: [sb(f"{n}{d}", shape) for d in ("f", "b")]
        kk, gs, qh, kh = (two(n, [P, S]) for n in ("k", "gs", "qh", "kh"))
        q, v = sb("q", [P, S]), sb("v", [P, S])
        kt, vt = two("kt", [P, CH, P]), sb("vt", [P, CH, P])
        at = two("at", [P, CH, P])
        m = two("m", [P, P, NCH])
        wb = sb("wrep", [P, P, NCH])
        tot, ws, w = two("tot", [P, 2 * NCH]), two("ws", [P, NCH - 1]), two("w", [P, NCH])
        tick = sb("tick", [P, 2])
        y, sqd = sb("y", [P, S]), sb("sqd", [P, CH, P])
        gate, o = [sb(f"gate{b}", [P, S]) for b in range(2)], acc
        rms, rstd_done = RmsParts(c, sb, sem, sqd[:].rearrange("p c t -> p (c t)"), X, Y), sem("rstd_done")
        rv, rr, rt = (sb(n, [P, CH]) for n in ("rv", "rr", "rt"))
        (zeroed, th, lg, kdone, fsum, totd, xdone, wsum, wexp, en, kh_ok, ep, qh_ok, gth, gated) = (
            sem(n) for n in ("zeroed", "tanh", "log_f", "k_done", "f_sums", "totals", "x_done", "w_sums", "w_exp",
                             "exp_neg", "kh_ok", "exp_pos", "qh_ok", "gate_tanh", "gated"))
        (att, at_ok, kv, kv_ok, wbc, m_ok, ymm, ycopy, sqok) = (
            sem(n) for n in ("attention", "masked", "kv", "kv_ok", "w_repeated", "states", "outputs", "y_copied",
                             "y_squared"))
        (tr, trcopy, stat, newton, dg, bc, norm, o_ok, o_stored) = (
            sem(n) for n in ("transposed", "tr_copied", "y2_sums", "newton", "diagonals", "y_spread", "normed", "o_ok",
                             "o_stored"))
        block = ctx.enter_context(nc.Block())
        TURNS = GH // 2

        def turns(eng, turn):
            turn(0, 0, 0, True, False, False)
            turn(1, 0, 1, True, True, False)
            with eng.Fori(1, TURNS) as i:
                for b in range(2):
                    turn(2 * i + b, i, b, True, True, True)
            turn(GH, TURNS, 0, False, True, True)
            turn(GH + 1, TURNS, 1, False, False, True)

        def slot(i, b, j):
            return (5 * b + j) % 2, 5 * i + (first + (5 * b + j) // 2)

        blocks = lambda ap: ap.rearrange("p (c a t) -> p c a t", a=2, t=32)

        def kv_sets(d, hf_):
            for par in range(2):
                cs = [cc for cc in range(8 * hf_ + par, 8 * hf_ + 8, 2) if cc != (NCH - 1 if d == 0 else 0)]
                yield par, cs

        KV_READS = 8

        @block.sync
        def _(sp):
            for dst, n in ((scan0, "scan0"), (masks[0], "m_f"), (masks[1], "m_b")):
                sp.dma_start(dst[:], io[n]).then_inc(const_full, 16)

            def turn(n, i, b, cur, prev, prev2):
                if cur:
                    for p_ in ((1, 2, 3) if b == 0 else (4, 5)):
                        g.load_pair(sp, 5 * i + (first + p_))
                if prev2:
                    sp.wait_ge(o_ok, n - 1)
                    sp.dma_start(io["hg_d"][n - 2], o[:]).then_inc(o_stored, 16)

            turn(0, 0, 0, True, False, False)
            turn(1, 0, 1, True, True, False)
            with sp.Fori(1, TURNS - 1) as i:
                for b in range(2):
                    turn(2 * i + b, i, b, True, True, True)
            for b in range(2):
                turn(GH - 2 + b, TURNS - 1, b, True, True, True)
            turn(GH, TURNS, 0, False, True, True)
            turn(GH + 1, TURNS, 1, False, False, True)
            sp.wait_ge(o_stored, 16 * (GH + 1))

        @block.gpsimd
        def _(pool):
            g.split(pool, first, first + 5 * TURNS)

        @block.tensor
        def _(pe):
            def turn(n, i, b, cur, prev, prev2):
                def gemm(j):
                    if cur:
                        s, pair = slot(i, b, j)
                        g.tile(pe, pair, s, hi, lo)

                def kv_half(d, hf_, ps):
                    for par, cs in kv_sets(d, hf_):
                        rows = slice(64 * par, 64 * par + 64)
                        for cc in cs:
                            jj = (cc // 2) % 4
                            mm = pe.matmul(ps[:, par, jj * P:(jj + 1) * P], kt[d][rows, cc // 2, :],
                                           vt[rows, cc // 2, :], start=True, stop=True)
                    mm.then_inc(kv, 1)

                def transposes(src, ps):
                    for n_ in range(CH):
                        mm = pe.transpose(ps[:, n_ // 4, (n_ % 4) * P:(n_ % 4 + 1) * P], src[:, n_ * P:(n_ + 1) * P],
                                          c["ident"][:])
                    mm.then_inc(tr, 1)

                if not prev and not prev2:
                    rms.pe_sums(pe, acc)
                gemm(0)
                if not prev and not prev2:
                    rms.pe_spread(pe)
                if prev2:
                    pe.wait_ge(sqok, n - 1)
                    pe.wait_ge(trcopy, (n if prev else GH) * 3)
                    for n_ in range(CH):
                        mm = pe.matmul(X[:, 0, n_:n_ + 1], sqd[:, n_, :], c["ones"][:, 0:1], start=(n_ == 0), stop=True,
                                       skip_group_check=True)
                    mm.then_inc(stat, 1)
                if prev:
                    pe.wait_ge(qh_ok, n * 2)
                    pe.wait_ge(kh_ok, n * 2)
                    pe.wait_ge(trcopy, n * 3)
                    if prev2:
                        pe.wait_ge(newton, (n - 2) * RSQRT_STEPS + 1)
                    for d, ps in enumerate((X, Y)):
                        for n_ in range(CH):
                            t_ = slice(n_ * P, (n_ + 1) * P)
                            mm = pe.matmul(ps[:, n_ // 4, (n_ % 4) * P:(n_ % 4 + 1) * P], kh[d][:, t_], qh[d][:, t_],
                                           start=True, stop=True)
                        mm.then_inc(att, 1)
                gemm(1)
                if prev2:
                    pe.wait_ge(dg, n - 1)
                    if prev:
                        pe.wait_ge(at_ok, n * 2)
                    for hh in range(NH):
                        mm = pe.matmul(X[:, hh, :], c["ones"][:], sqd[:, 4 * hh:4 * hh + 4, :], start=True, stop=True)
                    mm.then_inc(bc, 1)
                if prev:
                    pe.wait_ge(at_ok, n * 2)
                    kv_half(0, 1, Y)
                    if prev2:
                        pe.wait_ge(norm, n - 1)
                    kv_half(0, 0, X)
                gemm(2)
                if prev:
                    pe.wait_ge(kv_ok, (n - 1) * KV_READS + 2)
                    kv_half(1, 1, Y)
                    pe.wait_ge(kv_ok, (n - 1) * KV_READS + 4)
                    kv_half(1, 0, X)
                gemm(3)
                if prev:
                    pe.wait_ge(m_ok, n * 2)
                    pe.wait_ge(at_ok, n * 2)
                    pe.wait_ge(kv_ok, n * KV_READS)
                    for n_ in range(CH):
                        o_ = lambda a_, w_: X[:, n_ // 4, (n_ % 4) * P + a_:(n_ % 4) * P + a_ + w_]
                        for d in range(2):
                            pe.matmul(o_(0, P), vt[:, n_, :], at[d][:, n_, :], start=(d == 0), stop=(d == 1),
                                      skip_group_check=True)
                        parts = [(d, 2 * n_ + a_) for a_ in range(2) for d in range(2)
                                 if (d, 2 * n_ + a_) not in ((0, 0), (1, NCH - 1))]
                        for d, cc in parts:
                            mm = pe.matmul(o_((cc % 2) * GC, GC), m[d][:, :, cc], qh[d][:, cc * GC:(cc + 1) * GC],
                                           start=False, stop=True, skip_group_check=True)
                    mm.then_inc(ymm, 1)
                if cur:
                    pe.wait_ge(kh_ok, 2 * n + 1)
                    if not prev:
                        pe.wait_ge(rstd_done, 1)
                    if prev:
                        pe.wait_ge(kv_ok, n * KV_READS)
                    transposes(kh[0], Y)
                gemm(4)
                if cur:
                    pe.wait_ge(kh_ok, 2 * n + 2)
                    if prev:
                        pe.wait_ge(ycopy, n)
                    transposes(kh[1], X)
                    s, pair = slot(i, b, 3)
                    pe.wait_ge(g.psum_free[s], pair + 2)
                    pe.wait_ge(trcopy, 3 * n + 1)
                    transposes(v, Y)

            turns(pe, turn)

        @block.scalar
        def _(act):
            act.wait_ge(zeroed, 6)
            act.wait_ge(rms.spread_done, 1)
            act.activation(half(rstd[:]), Y[:], ACT.Copy).then_inc(rstd_done, 1)

            def turn(n, i, b, cur, prev, prev2):
                if cur:
                    hd = bass.ds(n, 1)
                    for j in range(2):
                        s, pair = slot(i, b, j)
                        act.wait_ge(g.psum_free[s], pair + 2)
                        act.activation(kk[j][:], kk[j][:], ACT.Tanh, scale=0.5).then_inc(th, 1)
                    act.wait_ge(th, 2 * n + 2)
                    if prev:
                        act.wait_ge(ep, n * 2)
                    act.wait_ge(zeroed, 6)
                    for d in range(2):
                        act.activation(gs[d][:], kk[d][:], ACT.Ln, scale=c["oml"][:, hd], bias=c["lnb"][:, hd])\
                           .then_inc(lg, 1)
                if prev:
                    if prev2:
                        act.wait_ge(m_ok, (n - 1) * 2)
                    act.activation(wb[:], w[0][:].unsqueeze(1).to_broadcast([P, P, NCH]), ACT.Copy).then_inc(wbc, 1)
                if cur:
                    for d in range(2):
                        act.wait_ge(xdone, 2 * n + d + 1)
                        if prev:
                            act.wait_ge(att, n * 2)
                        act.activation(kh[d][:], gs[d][:], ACT.Exp, scale=-1.0).then_inc(en, 1)
                if prev:
                    act.wait_ge(m_ok, n * 2 - 1)
                    act.activation(wb[:], w[1][:].unsqueeze(1).to_broadcast([P, P, NCH]), ACT.Copy).then_inc(wbc, 1)
                if cur:
                    if prev:
                        act.wait_ge(wbc, n * 2)
                        act.wait_ge(kv_ok, n * KV_READS)
                    for d in range(2):
                        act.wait_ge(wsum, 2 * n + d + 1)
                        act.activation(w[d][:, 1 - d:NCH - d], ws[d][:], ACT.Exp).then_inc(wexp, 1)
                if prev:
                    act.wait_ge(ymm, n)
                    if prev2:
                        act.wait_ge(norm, n - 1)
                        act.wait_ge(o_ok, n - 1)
                    act.activation(half(y[:]), X[:], ACT.Copy).then_inc(ycopy, 1)
                    act.wait_ge(ycopy, n)
                    if prev2:
                        act.wait_ge(bc, n - 1)
                    act.activation(sqd[:].rearrange("p c t -> p (c t)"), y[:], ACT.Square).then_inc(sqok, 1)
                if cur:
                    act.wait_ge(tr, 3 * n + 1)
                    act.activation(kt[0][:].rearrange("p (h c) t -> p h (c t)", h=NH), Y[:], ACT.Copy)\
                       .then_inc(trcopy, 1)
                    for d in range(2):
                        act.activation(qh[d][:], gs[d][:], ACT.Exp).then_inc(ep, 1)
                    s, pair = slot(i, b, 4)
                    act.wait_ge(g.psum_free[s], pair + 2)
                    act.wait_ge(qh_ok, 2 * n + 2)
                    act.activation(q[:], gate[b][:], ACT.Tanh, scale=0.5).then_inc(gth, 1)
                    for dst, k_, ps in ((kt[1], 2, X), (vt, 3, Y)):
                        act.wait_ge(tr, 3 * n + k_)
                        act.activation(dst[:].rearrange("p (h c) t -> p h (c t)", h=NH), ps[:], ACT.Copy)\
                           .then_inc(trcopy, 1)

            turns(act, turn)

        @block.vector
        def _(dve):
            dve.sem_inc(o_stored, 16)
            rms.dve_roots(dve)
            for d in range(2):
                dve.memset(at[d][:], 0.0).then_inc(zeroed, 1)
                dve.memset(w[d][:, d * (NCH - 1):d * (NCH - 1) + 1], 0.0).then_inc(zeroed, 1)
                dve.memset(m[d][:, :, d * (NCH - 1):d * (NCH - 1) + 1], 0.0).then_inc(zeroed, 1)
            dve.wait_ge(zeroed, 6)
            dve.wait_ge(const_full, 48)
            dve.wait_ge(rstd_done, 1)

            def turn(n, i, b, cur, prev, prev2):
                def take(j, out, scale=1.0):
                    s, pair = slot(i, b, j)
                    dve.wait_ge(g.tile_done[s], pair + 1)
                    dve.scalar_tensor_tensor(out=half(out), in0=psum[s][:], scalar=scale, in1=half(rstd[:]),
                                             op0=ALU.mult, op1=ALU.mult).then_inc(g.psum_free[s], 1)

                if cur:
                    if prev:
                        dve.wait_ge(kh_ok, n * 2)
                    take(0, kk[0][:])
                if prev2:
                    dve.wait_ge(stat, n - 1)
                    rsqrt_steps(dve, newton, (n - 2) * RSQRT_STEPS, rv[:], rr[:], rt[:], X[:, 0, 0:CH], 1.0 / P)
                    dve.tensor_tensor(sqd[:], c["ident"][:].unsqueeze(1).to_broadcast([P, CH, P]),
                                      rr[:].unsqueeze(2).to_broadcast([P, CH, P]), ALU.mult).then_inc(dg, 1)
                if prev:
                    for d, (ps, mask) in enumerate(((X, masks[0]), (Y, masks[1]))):
                        dve.wait_ge(att, n * 2 - 1 + d)
                        if prev2:
                            dve.wait_ge(ymm, n - 1)
                        dve.memset(tick[:, d:d + 1], 0.0)
                        dve.copy_predicated(at[d][:], mask[:].unsqueeze(1).to_broadcast([P, CH, P]),
                                            ps[:].rearrange("p h (c t) -> p (h c) t", t=P)).then_inc(at_ok, 1)
                if cur:
                    take(1, kk[1][:])
                if prev2:
                    dve.wait_ge(bc, n - 1)
                    dve.scalar_tensor_tensor(out=half(y[:]), in0=half(y[:]), scalar=c["hg_gain"][:, bass.ds(n - 2, 1)],
                                             in1=X[:], op0=ALU.mult, op1=ALU.mult).then_inc(norm, 1)
                    dve.wait_ge(norm, n - 1)
                    dve.wait_ge(gated, n - 1)
                    dve.wait_ge(o_stored, (n - 1) * 16)
                    dve.tensor_tensor(o[:], y[:], gate[b][:], ALU.mult).then_inc(o_ok, 1)

                def kv_read(d, hf_, ps, k_):
                    dve.wait_ge(kv, (n - 1) * 4 + k_)
                    for par, cs in kv_sets(d, hf_):
                        a_, st = cs[0] + (1 if d == 0 else -1), len(cs)
                        sl = slice(a_, a_ + 2 * st - 1, 2)
                        j0 = (cs[0] // 2) % 4
                        dve.tensor_tensor(m[d][:, :, sl].rearrange("p v c -> p c v"),
                                          ps[:, par, j0 * P:(j0 + st) * P].rearrange("p (c v) -> p c v", v=P),
                                          w[d][:, sl].unsqueeze(2).to_broadcast([P, st, P]), ALU.mult)\
                           .then_inc(kv_ok, 1)

                if prev:
                    dve.wait_ge(wexp, n * 2)
                    if prev2:
                        dve.wait_ge(ymm, n - 1)
                    kv_read(0, 1, Y, 1)
                    kv_read(0, 0, X, 2)

                if cur:
                    hd = bass.ds(n, 1)
                    for d in range(2):
                        dve.wait_ge(lg, 2 * n + d + 1)
                        dve.tensor_scalar(kk[d][:], kk[d][:], c["noml"][:, hd], c["oml"][:, hd], ALU.mult, ALU.add)\
                           .then_inc(kdone, 1)
                        t_ = slice(None) if d == 0 else slice(None, None, -1)
                        dve.tensor_tensor_scan(gs[d][:, t_], scan0[:], gs[d][:, t_], 0.0, ALU.mult, ALU.add)\
                           .then_inc(fsum, 1)
                    for d in range(2):
                        dve.wait_ge(fsum, 2 * n + d + 1)
                        if prev:
                            dve.wait_ge(wsum, n * 2)
                        dve.tensor_copy(tot[d][:], gs[d][:, 31 if d == 0 else 0::32]).then_inc(totd, 1)
                    for d in range(2):
                        dve.wait_ge(totd, 2 * n + d + 1)
                        a_ = d
                        xv = blocks(gs[d][:])[:, :, a_, :]
                        dve.tensor_tensor(xv, xv, tot[d][:, a_::2].unsqueeze(2).to_broadcast([P, NCH, 32]),
                                          ALU.subtract).then_inc(xdone, 1)
                        if prev:
                            dve.wait_ge(wexp, n * 2)
                        dve.tensor_tensor(ws[d][:], tot[d][:, 1:2 * NCH - 2:2], tot[d][:, 2::2], ALU.add)\
                           .then_inc(wsum, 1)
                    if prev:
                        dve.wait_ge(gated, n)
                    take(2, q[:], SCALE)
                if prev:
                    dve.wait_ge(wbc, n * 2 - 1)
                    dve.wait_ge(kv_ok, (n - 1) * KV_READS + 4)
                    fl = lambda ap: ap.rearrange("p v c -> p (v c)")
                    dve.tensor_tensor_scan(fl(m[0][:]), fl(wb[:]), fl(m[0][:]), 0.0, ALU.mult, ALU.add)\
                       .then_inc(m_ok, 1)
                    kv_read(1, 1, Y, 3)
                    kv_read(1, 0, X, 4)
                    dve.wait_ge(wbc, n * 2)
                    dve.wait_ge(kv_ok, n * KV_READS)
                    dve.tensor_tensor_scan(fl(m[1][:])[:, ::-1], fl(wb[:])[:, ::-1], fl(m[1][:])[:, ::-1], 0.0,
                                           ALU.mult, ALU.add).then_inc(m_ok, 1)
                if cur:
                    if prev:
                        dve.wait_ge(tr, n * 3)
                    take(3, v[:])
                    for d in range(2):
                        dve.wait_ge(en, 2 * n + d + 1)
                        dve.wait_ge(kdone, 2 * n + d + 1)
                        dve.tensor_tensor(kh[d][:], kh[d][:], kk[d][:], ALU.mult).then_inc(kh_ok, 1)
                    s, pair = slot(i, b, 2)
                    dve.wait_ge(g.psum_free[s], pair + 2)
                    for d in range(2):
                        dve.wait_ge(ep, 2 * n + d + 1)
                        dve.tensor_tensor(qh[d][:], qh[d][:], q[:], ALU.mult).then_inc(qh_ok, 1)
                    if prev2:
                        dve.wait_ge(o_ok, n - 1)
                    take(4, gate[b][:])
                    dve.wait_ge(gth, n + 1)
                    dve.scalar_tensor_tensor(out=gate[b][:], in0=q[:], scalar=1.0, in1=gate[b][:],
                                             op0=ALU.add, op1=ALU.mult).then_inc(gated, 1)

            turns(dve, turn)


def tail_phase(nc, io, c, g, x, acc, rstd, x_src, y_src, last, other, halves, first, gain, next_gain, store, psum,
               tag):
    with phase(nc, tag) as (ctx, sb, sem):
        t = [sb(f"t{s}", [P, S]) for s in range(2)]
        sq = sb("sq", [P, S])
        rms, rms_next = (RmsParts(c, lambda n, shape: sb(n + e, shape), lambda n: sem(n + e), sq[:], psum[2], psum[3])
                         for e in ("", "2"))
        y_full = [sem(f"y_full{s}") for s in range(2)]
        x_full = [sem(f"x_full{b}") for b in range(2)]
        (y_hi, y_ready, x_hi, x_ready, sq_done, acc_done, rstd_done, squared, hid_hi, hid_ready, stored) = (
            sem(n) for n in ("y_hi", "y_ready", "x_hi", "x_ready", "sq_done", "acc_done", "rstd_done",
                             "squared", "hid_hi", "hid_ready", "stored"))
        BL = FF // D
        PR = KT // 2
        BASE = first + halves * PR
        PAIRS = BASE + BL * 2 * PR
        (n_hi, n_lo), (h_hi, h_lo) = other, last
        block = ctx.enter_context(nc.Block())

        def stage_pairs(eng, body, start=0):
            with eng.Fori(start, PR) as i:
                for s in range(2):
                    body(i, s)

        @block.sync
        def _(sp):
            for k in range(KT):
                if k >= 2:
                    sp.wait_ge(y_ready, k - 1)
                sp.dma_start(t[k % 2][:], y_src[k]).then_inc(y_full[k % 2], 16)
                if k == 1 or (halves == 2 and k % 2 == 1):
                    g.load_pair(sp, first + 1 + k // 2)
            g.load(sp, first + (PR if halves == 2 else 1), PAIRS)
            if next_gain is not None:
                for k in range(KT):
                    sp.wait_ge(g.psum_free[k % 2], PAIRS - PR + k // 2 + 2)
                    sp.dma_start(store[:, k, :], x[:, k, :]).then_inc(stored, 16)
                sp.wait_ge(stored, 16 * KT)

        @block.gpsimd
        def _(pool):
            g.split(pool, first, PAIRS)

        @block.tensor
        def _(pe):
            def out_pair(base, hi, lo, k_wait):
                g.tile(pe, base, 0, hi, lo, k_wait)
                g.tile(pe, base, 1, hi, lo)
                stage_pairs(pe, lambda i, s: g.tile(pe, i + base, s, hi, lo), 1)

            if halves == 2:
                out_pair(first, n_hi, n_lo, None)
            out_pair(BASE - PR, h_hi, h_lo, lambda k: pe.wait_ge(y_ready, k + 1))

            def spread(k):
                if k == PR:
                    rms.pe_spread(pe)

            def stage2(b, i, s):
                wait = (lambda k: pe.wait_ge(hid_ready, b * KT + (k + 1))) if s == 0 else None
                g.tile(pe, b * (2 * PR) + (i + (BASE + PR)), s, h_hi, h_lo, wait)

            g.tile(pe, BASE, 0, n_hi, n_lo, lambda k: pe.wait_ge(x_ready, k + 1))
            pe.wait_ge(acc_done, KT + 1)
            rms.pe_sums(pe, acc)
            g.tile(pe, BASE, 1, n_hi, n_lo, spread)
            stage_pairs(pe, lambda i, s: g.tile(pe, i + BASE, s, n_hi, n_lo), 1)
            stage_pairs(pe, lambda i, s: stage2(0, i, s))
            with pe.Fori(1, BL) as b:
                stage_pairs(pe, lambda i, s: g.tile(pe, b * (2 * PR) + (i + BASE), s, n_hi, n_lo))
                stage_pairs(pe, lambda i, s: stage2(b, i, s))
            pe.wait_ge(acc_done, 2 * KT + 2)
            if next_gain is None:
                rms_next.pe_sums(pe, acc)
                rms_next.pe_spread(pe)

        @block.scalar
        def _(act):
            def load_x(tiles):
                for q in tiles:
                    act.dma_start(x[:, q, :], x_src[:, q, :]).then_inc(x_full[q // 2 > 0], 16)

            if halves == 2:
                load_x(range(KT))
            for k in range(KT):
                act.wait_ge(y_full[k % 2], 16 * (k // 2 + 1))
                act.activation(h_hi[:, k, :], t[k % 2][:], ACT.Copy).then_inc(y_hi, 1)
                if halves == 1 and k >= KT // 2:
                    load_x(range(2 * k - KT, 2 * k - KT + 2))

            def norm_parts(i, s, pair, sums, gain):
                act.wait_ge(g.psum_free[s], i + (pair + 2))
                act.wait_ge(acc_done, 2 * i + (s + sums))
                if gain is not None:
                    act.activation(at(n_hi, 2 * i + s), at(x, 2 * i + s), ACT.Copy,
                                   scale=gain[:, bass.ds(2 * i + s, 1)]).then_inc(x_hi, 1)
                act.activation(sq[:], at(x, 2 * i + s), ACT.Square).then_inc(sq_done, 1)

            def hidden(b, i, s):
                n = b * KT + (2 * i + (s + 1))
                act.wait_ge(g.psum_free[s], b * (2 * PR) + (i + (BASE + 2)))
                act.activation(t[s][:], t[s][:], ACT.Square).then_inc(squared, 1)
                act.wait_ge(squared, n)
                act.activation(at(h_hi, 2 * i + s), t[s][:], ACT.Copy).then_inc(hid_hi, 1)

            stage_pairs(act, lambda i, s: norm_parts(i, s, BASE - PR, 1, gain))
            act.wait_ge(rms.spread_done, 1)
            act.activation(half(rstd[:]), psum[3][:], ACT.Copy).then_inc(rstd_done, 1)
            with act.Fori(0, BL) as b:
                stage_pairs(act, lambda i, s: hidden(b, i, s))

            stage_pairs(act, lambda i, s: norm_parts(i, s, PAIRS - PR, KT + 2, next_gain))
            if next_gain is None:
                act.wait_ge(rms_next.spread_done, 1)
                act.activation(half(rstd[:]), psum[3][:], ACT.Copy).then_inc(rstd_done, 1)

        @block.vector
        def _(dve):
            dve.memset(acc[:], 0.0).then_inc(acc_done, 1)

            def split_y(k):
                dve.wait_ge(y_hi, k + 1)
                dve.tensor_tensor(h_lo[:, k, :], t[k % 2][:], h_hi[:, k, :].bitcast(F32), ALU.subtract)\
                   .then_inc(y_ready, 1)

            def add(pair, i, s):
                dve.wait_ge(g.tile_done[s], pair + 1)
                dve.tensor_tensor(half2(x, 2 * i + s), psum[s][:], half2(x, 2 * i + s), ALU.add)\
                   .then_inc(g.psum_free[s], 1)

            def norm_parts(i, s, pair, parts, squares, sums, gain):
                add(i + pair, i, s)
                if gain is not None:
                    dve.wait_ge(x_hi, 2 * i + (s + 1 + parts))
                    dve.scalar_tensor_tensor(out=at(n_lo, 2 * i + s), in0=at(x, 2 * i + s),
                                             scalar=gain[:, bass.ds(2 * i + s, 1)],
                                             in1=at(n_hi, 2 * i + s).bitcast(F32),
                                             op0=ALU.mult, op1=ALU.subtract).then_inc(x_ready, 1)
                dve.wait_ge(sq_done, 2 * i + (s + 1 + squares))
                dve.wait_ge(acc_done, 2 * i + (s + sums))
                dve.tensor_tensor(acc[:], acc[:], sq[:], ALU.add).then_inc(acc_done, 1)

            def hidden(b, i, s):
                n = b * KT + (2 * i + (s + 1))
                dve.wait_ge(g.tile_done[s], b * (2 * PR) + (i + (BASE + 1)))
                dve.scalar_tensor_tensor(out=half(t[s][:]), in0=psum[s][:], scalar=0.0, in1=half(rstd[:]),
                                         op0=ALU.max, op1=ALU.mult).then_inc(g.psum_free[s], 1)
                dve.wait_ge(hid_hi, n)
                dve.tensor_tensor(at(h_lo, 2 * i + s), t[s][:], at(h_hi, 2 * i + s).bitcast(F32), ALU.subtract)\
                   .then_inc(hid_ready, 1)
                dve.wait_ge(hid_ready, n)

            def last_half(i, s):
                norm_parts(i, s, BASE - PR, 0, 0, 1, gain)

            if halves == 2:
                for k in range(KT):
                    split_y(k)
                    if k % 2 == 0 and k < 4:
                        dve.wait_ge(x_full[k // 2], (2, KT - 2)[k // 2] * 16)
                    add(first + k // 2, k // 2, k % 2)
                dve.wait_ge(y_ready, KT)
                stage_pairs(dve, last_half)
            else:
                for k in range(KT):
                    split_y(k)
                dve.wait_ge(y_ready, KT)
                dve.wait_ge(x_full[0], 2 * 16)
                for s in range(2):
                    last_half(0, s)
                dve.wait_ge(x_full[1], (KT - 2) * 16)
                stage_pairs(dve, last_half, 1)
            dve.wait_ge(acc_done, KT + 1)
            rms.dve_roots(dve)
            dve.memset(acc[:], 0.0).then_inc(acc_done, 1)
            dve.wait_ge(rstd_done, 1)

            def stage2(b, i, s):
                add(b * (2 * PR) + (i + (BASE + PR)), i, s)

            with dve.Fori(0, BL - 1) as b:
                stage_pairs(dve, lambda i, s: hidden(b, i, s))
                stage_pairs(dve, lambda i, s: stage2(b, i, s))
            stage_pairs(dve, lambda i, s: hidden(BL - 1, i, s))

            stage_pairs(dve, lambda i, s: norm_parts(i, s, PAIRS - PR, KT, KT, KT + 2, next_gain))
            dve.wait_ge(acc_done, 2 * KT + 2)
            if next_gain is None:
                rms_next.dve_roots(dve)


def final_phase(nc, x, rstd, gain, store, tag):
    with phase(nc, tag) as (ctx, sb, sem):
        done, stored = sem("done"), sem("stored")
        block = ctx.enter_context(nc.Block())

        @block.vector
        def _(dve):
            for k in range(KT):
                dve.scalar_tensor_tensor(out=x[:, k, :], in0=x[:, k, :], scalar=gain[:, k:k + 1], in1=rstd[:],
                                         op0=ALU.mult, op1=ALU.mult).then_inc(done, 1)

        @block.sync
        def _(sp):
            for k in range(KT):
                sp.wait_ge(done, k + 1)
                sp.dma_start(store[:, k, :], x[:, k, :]).then_inc(stored, 16)
            sp.wait_ge(stored, 16 * KT)


def at(t, k):
    return t[:, bass.ds(k, 1), :].rearrange("p k n -> p (k n)")

P_EVEN_OUT = PAIRS_IN
P_ODD_IN = P_EVEN_OUT + KT + FF // P
P_ODD_OUT = P_ODD_IN + 5 * GH // 2

CONST = dict(
    gains=[P, 5, KT], conv_w=[P, 24, 4], conv_b=[P, 24], gate_b=[P, KT, 4], dt_bias=[2 * HEADS, 1], ssd_norm=[P, KT],
    hgrn_norm=[P, KT], d_skip=[P, HEADS], ones=[P, P], ident=[P, P],
    a_exp=[P, 2 * HEADS], lb_e=[P, KT], lb_d=[P, KT], lru_rate=[P, 2, KT], lru_rate2=[P, 2, KT], lru_rate_n=[P, 2, KT],
    gate_bh=[P, KT, 4], oml=[P, KT], noml=[P, KT], lnb=[P, KT], hg_gain=[P, KT], zero=[P, 1])
TRIANGLES = ("m_ui", "m_us", "m_li", "m_ls")

SCRATCH = dict(yb_d=[KT, P, S], hg_d=[KT, P, S], z_d=[KT, P, S], xs_d=[CH, P, D], b_d=[G, P, S], c_d=[G, P, S],
               bt_d=[CH, P, G * N_ST], x_d=[P, KT, S])


def encoder(nc, io):
    with ExitStack() as ctx:
        psum = [ctx.enter_context(nc.psum_tensor(f"ps{b}", [P, NH, HALF], F32)) for b in range(4)]
        io = dict(io, **{n: nc.dram_tensor(n, shape, F32).ap() for n, shape in SCRATCH.items()})
        keep = lambda stack, n, shape, dt=F32, **side: stack.enter_context(nc.sbuf_tensor(n, shape, dt, **side))
        pair = lambda stack, n: tuple(keep(stack, f"{n}_{part}", [P, KT, S], F32R) for part in ("hi", "lo"))
        c = {n: keep(ctx, f"c_{n}", shape) for n, shape in CONST.items()}
        gain = lambda n: c["gains"][:, n, :]
        _, sb, sem = ctx.enter_context(phase(nc, "g"))
        g = Gemm(c, sb, sem, psum[0:2], io["w"], io["w"].shape[0] // 2)

        with ExitStack() as at_right:
            with ExitStack() as ssd:
                c.update({n: keep(ssd, f"c_{n}", [P, P]) for n in TRIANGLES})
                dt_t = keep(ssd, "dt_t", [2 * HEADS, S])
                co = {n: keep(ssd, f"co_{n}", [P, CH, 2 * HEADS]) for n in ("dt", "da", "w", "e", "tot", "cw")}
                with ExitStack() as proj:
                    h = pair(proj, "h0")
                    acc0, rstd0 = keep(proj, "acc0", [P, S]), keep(proj, "rstd0", [P, S])
                    with nc.sbuf_tensor("x0", [P, KT, S], F32) as x:
                        setup_phase(nc, io, c, g, x, *h, acc0)
                    lru_phase(nc, io, c, g, *h, acc0, rstd0, psum)
                    conv_phase(nc, io, c, g, *h, rstd0, psum, dt_t)
                with nc.sbuf_tensor("hb", [P, CH, D], F32) as hb:
                    u = keep(at_right, "u", [P, KT, S], side="right")
                    ssd_back_states_phase(nc, io, c, dt_t, co, hb, psum)
                    ssd_phase(nc, io, c, co, hb, u, psum)
            h = pair(ctx, "h")
            norm_phase(nc, c, u, G, c["ssd_norm"], *h, psum, "nu")
        rstd, acc = (keep(ctx, n, [P, S], side="right") for n in ("rstd", "acc"))
        with ExitStack() as even:
            y = pair(even, "y0")
            x = keep(even, "x1", [P, KT, S])
            tail_phase(nc, io, c, g, x, acc, rstd, io["xT"], io["yb_d"], y, h, 2, P_EVEN_OUT, gain(1), gain(2),
                       io["x_d"], psum, "te")

        gla_phase(nc, io, c, g, P_ODD_IN, *h, acc, rstd, psum)
        y = pair(ctx, "y1")
        x = keep(ctx, "x2", [P, KT, S])
        tail_phase(nc, io, c, g, x, acc, rstd, io["x_d"], io["hg_d"], y, h, 1, P_ODD_OUT, gain(3), None, None, psum,
                   "to")
        final_phase(nc, x, rstd, gain(4), io["out"], "fi")


def weight_tiles(w):
    K, N = w.shape
    return w.reshape(K // D, KT, P, N // P, P).transpose(0, 3, 2, 1, 4).reshape(K // D, N // P, P, D)


def by_channel(v):
    return np.moveaxis(v.reshape(*v.shape[:-1], v.shape[-1] // P, P), -1, 0)


def mlp_stream(w1, w2):
    w1 = weight_tiles(w1)[0].reshape(FF // D, KT, P, D)
    return np.concatenate([w1, weight_tiles(w2)], axis=1).reshape(-1, P, D)


def weight_stream(even_w_in, even_w_out, odd_w_in, odd_w_out, mlp_w1, mlp_w2):
    n_dt = 2 * HEADS
    wide = even_w_in.shape[1] - n_dt
    e = weight_tiles(even_w_in[:, :wide])[0]
    x, b, c, u, z, gate = np.split(e, np.cumsum([KT, G, G, KT, KT]))
    pairs = lambda first, second: np.stack([first, second], 1).reshape(-1, P, D)
    dt = weight_tiles(np.concatenate([even_w_in[:, wide:], np.zeros((D, P - n_dt), even_w_in.dtype)], 1))[0]
    lru = np.concatenate([u[:2], pairs(gate[:-2], u[2:]), gate[-2:]])
    odd = weight_tiles(odd_w_in)[0].reshape(5, GH, P, D)[[1, 2, 0, 3, 4]].transpose(1, 0, 2, 3).reshape(-1, P, D)
    return np.concatenate([lru, pairs(x, z), pairs(b, c), dt, np.zeros_like(dt),
                           weight_tiles(even_w_out).reshape(-1, P, D), mlp_stream(mlp_w1[0], mlp_w2[0]),
                           odd, weight_tiles(odd_w_out)[0], mlp_stream(mlp_w1[1], mlp_w2[1])])


def layout(x, even_w_in, even_conv_w, even_conv_b, ssd_a_log, ssd_dt_bias, ssd_d, ssd_norm_w, lru_w_a, lru_b_a,
           lru_w_x, lru_b_x, lru_lambda, even_w_out, odd_w_in, hgrn_lb_logits, hgrn_norm_w, odd_w_out, norm_mix,
           norm_mlp, mlp_w1, mlp_w2, norm_final):
    C = np.ascontiguousarray
    n_conv = even_conv_b.shape[1] // P
    tile = np.arange(n_conv)
    order = np.concatenate([tile[-KT:], tile[:KT], tile[KT:-KT].reshape(2, G).T.reshape(-1)])
    conv_w = even_conv_w[0].reshape(-1, n_conv, P)[:, order].transpose(2, 1, 0)
    conv_b = even_conv_b[0].reshape(n_conv, P)[order].T
    W = lru_w_a.shape[-1]
    gate_w = np.zeros((KT, P, 2, 2, P), lru_w_a.dtype)
    for r, blocks in enumerate((lru_w_a[0], lru_w_x[0])):
        for part in range(P // W):
            at = slice(W * part, W * part + W)
            gate_w[:, at, :, r, at] = blocks[:, part::P // W].transpose(1, 2, 0, 3)
    gate_b = np.stack([lru_b_a[0], lru_b_x[0]], 1).reshape(4, KT, P).transpose(2, 1, 0)
    gains = by_channel(np.stack([norm_mix[0], norm_mlp[0], norm_mix[1], norm_mlp[1], norm_final]))
    f = np.float32
    s, t = np.arange(P)[:, None], np.arange(P)[None, :]
    same_chunk = s // GC == t // GC
    return dict(
        xT=C(x[0].T.reshape(KT, P, S).transpose(1, 0, 2)),
        w=C(weight_stream(even_w_in[0], even_w_out[0], odd_w_in[0], odd_w_out[0], mlp_w1, mlp_w2)),
        gate_w=C(gate_w.reshape(KT, P, 4 * P)), conv_w=C(conv_w), conv_b=C(conv_b), gate_b=C(gate_b), gains=C(gains),
        dt_bias=C(ssd_dt_bias[0].reshape(-1, 1)), a_log=C(ssd_a_log[0].reshape(1, -1)),
        d_skip=C(ssd_d[0].reshape(1, -1)), ssd_norm=C(by_channel(ssd_norm_w[0])),
        hgrn_norm=C(by_channel(hgrn_norm_w[0])), lam=C(by_channel(lru_lambda[0])),
        lb_logits=C(by_channel(hgrn_lb_logits)),
        ones=np.ones((P, P), f), ident=np.eye(P, dtype=f),
        m_ui=(s <= t).astype(f), m_us=(s < t).astype(f), m_li=(s >= t).astype(f), m_ls=(s > t).astype(f),
        m_f=(same_chunk & (s <= t)).astype(np.uint32), m_b=(same_chunk & (s >= t)).astype(np.uint32),
        scan0=np.tile((np.arange(S) % 32 != 0).astype(f), (P, 1)),
    )


def kernel(**inputs):
    import concourse.bacc as bacc
    from concourse.bass_utils import run_bass_kernel_spmd

    arrays = layout(**{name: np.asarray(value) for name, value in inputs.items()})
    nc = bacc.Bacc("TRN2", target_bir_lowering=False, num_devices=1)
    io = {name: nc.dram_tensor(f"in_{name}", a.shape, mybir.dt.from_np(a.dtype), kind="ExternalInput").ap()
          for name, a in arrays.items()}
    io["out"] = nc.dram_tensor("out_y", [P, KT, S], F32, kind="ExternalOutput").ap()
    encoder(nc, io)
    r = run_bass_kernel_spmd(nc, [{f"in_{name}": a for name, a in arrays.items()}], core_ids=[0])
    return np.ascontiguousarray(r.results[0]["out_y"].transpose(2, 1, 0).reshape(1, S, D))
```
